# Optimizing a Trainium2 kernel written in Bass

```python
import jax, jax.numpy as jnp
from jax import lax
import numpy as np

D_MODEL = 1024
BATCH = 1
SEQ = 256
DEPTH = 2

N_MIXERS = 2
SB_HEADS = 16
SB_HEAD_DIM = D_MODEL // SB_HEADS
SB_BLOCK = 128
RET_HEADS = 4
RET_QK_DIM = D_MODEL // RET_HEADS
RET_V_DIM = 2 * D_MODEL // RET_HEADS
RET_CHUNK = 128
ROPE_BASE = 10000.0
MLP_HIDDEN = 4 * D_MODEL
RMS_EPS = 1e-6
GN_EPS = 1e-6
N_SB_LAYERS = (DEPTH + N_MIXERS - 1) // N_MIXERS
N_RET_LAYERS = DEPTH // N_MIXERS


F32 = jnp.float32

def rms_norm(x, g):
    xf = x.astype(F32)
    y = xf * lax.rsqrt(jnp.mean(xf * xf, axis=-1, keepdims=True) + RMS_EPS)
    return (y * g.astype(F32)).astype(x.dtype)

def stick_breaking_attention(h, w_in, w_out):
    b, s, _ = h.shape
    q, k, v = jnp.split(h @ w_in, 3, axis=-1)

    def heads(t):
        return t.reshape(b, s, SB_HEADS, SB_HEAD_DIM).transpose(0, 2, 1, 3).astype(F32)

    q, k, v = heads(q), heads(k), heads(v)
    scale = SB_HEAD_DIM ** -0.5
    outs = []
    for blk in range(s // SB_BLOCK):
        start = blk * SB_BLOCK
        end = start + SB_BLOCK
        qb = q[:, :, start:end]
        kp = k[:, :, :end]
        vp = v[:, :, :end]
        z = jnp.einsum('bhqd,bhkd->bhqk', qb, kp) * scale
        t_idx = start + jnp.arange(SB_BLOCK)[:, None]
        s_idx = jnp.arange(end)[None, :]
        mask = s_idx < t_idx
        log_keep = jnp.where(mask, jax.nn.log_sigmoid(-z), 0.0)
        later = lax.cumsum(log_keep, axis=3, reverse=True) - log_keep
        a = jnp.where(mask, jnp.exp(jax.nn.log_sigmoid(z) + later), 0.0)
        outs.append(jnp.einsum('bhqk,bhkd->bhqd', a, vp))
    o = jnp.concatenate(outs, axis=2)
    o = o.transpose(0, 2, 1, 3).reshape(b, s, D_MODEL).astype(h.dtype)
    return o @ w_out

def rotary(x, pos):
    half = x.shape[-1] // 2
    inv_freq = 1.0 / (ROPE_BASE ** jnp.linspace(0.0, 1.0, half, dtype=F32))
    ang = pos.astype(F32)[:, None] * inv_freq[None, :]
    cos, sin = jnp.cos(ang), jnp.sin(ang)
    x1, x2 = x[..., :half], x[..., half:]
    return jnp.concatenate([x1 * cos - x2 * sin, x1 * sin + x2 * cos], axis=-1)

def retention(h, w_in, w_out):
    b, s, _ = h.shape
    c = RET_CHUNK
    nc = s // c
    q, k, v, g = jnp.split(h @ w_in, [D_MODEL, 2 * D_MODEL, 4 * D_MODEL], axis=-1)
    q = q.reshape(b, s, RET_HEADS, RET_QK_DIM).transpose(0, 2, 1, 3).astype(F32)
    k = k.reshape(b, s, RET_HEADS, RET_QK_DIM).transpose(0, 2, 1, 3).astype(F32)
    v = v.reshape(b, s, RET_HEADS, RET_V_DIM).transpose(0, 2, 1, 3).astype(F32)
    pos = jnp.arange(s)
    q = rotary(q, pos)
    k = rotary(k, pos) * (RET_QK_DIM ** -0.5)

    log_gamma = jnp.log1p(-jnp.exp2(-5.0 - jnp.arange(RET_HEADS, dtype=F32)))
    idx = jnp.arange(c, dtype=F32)
    rel = idx[:, None] - idx[None, :]
    decay_in = jnp.where(rel >= 0, jnp.exp(log_gamma[:, None, None] * jnp.maximum(rel, 0.0)), 0.0)
    q_decay = jnp.exp(log_gamma[:, None] * (idx + 1.0))[None, :, :, None]
    k_decay = jnp.exp(log_gamma[:, None] * (c - 1.0 - idx))[None, :, :, None]
    chunk_decay = jnp.exp(log_gamma * c)[None, :, None, None]

    qc = q.reshape(b, RET_HEADS, nc, c, RET_QK_DIM)
    kc = k.reshape(b, RET_HEADS, nc, c, RET_QK_DIM)
    vc = v.reshape(b, RET_HEADS, nc, c, RET_V_DIM)

    scores = jnp.einsum('bhnid,bhnjd->bhnij', qc, kc) * decay_in[None, :, None]
    inner = jnp.einsum('bhnij,bhnje->bhnie', scores, vc)

    def step(state, xs):
        q_n, k_n, v_n = xs
        cross = jnp.einsum('bhid,bhde->bhie', q_n, state) * q_decay
        state = state * chunk_decay + jnp.einsum('bhjd,bhje->bhde', k_n * k_decay, v_n)
        return state, cross

    state0 = jnp.zeros((b, RET_HEADS, RET_QK_DIM, RET_V_DIM), F32)
    xs = (qc.transpose(2, 0, 1, 3, 4), kc.transpose(2, 0, 1, 3, 4), vc.transpose(2, 0, 1, 3, 4))
    _, cross = lax.scan(step, state0, xs)
    o = (inner + cross.transpose(1, 2, 0, 3, 4)).reshape(b, RET_HEADS, s, RET_V_DIM)

    mu = jnp.mean(o, axis=-1, keepdims=True)
    var = jnp.mean(jnp.square(o - mu), axis=-1, keepdims=True)
    o = (o - mu) * lax.rsqrt(var + GN_EPS)
    o = o.transpose(0, 2, 1, 3).reshape(b, s, RET_HEADS * RET_V_DIM)
    y = jax.nn.silu(g.astype(F32)) * o
    return y.astype(h.dtype) @ w_out

def squared_relu_mlp(h, w_up, w_down):
    u = jax.nn.relu(h @ w_up)
    return (u * u) @ w_down

def first_inputs(seed: int = 0) -> dict:
    key = jax.random.key(seed)
    ks = jax.random.split(key, 11)

    def w(k, shape, fan_in):
        return jax.random.normal(k, shape, F32) * (fan_in ** -0.5)

    def gain(k, shape):
        return 1.0 + 0.05 * jax.random.normal(k, shape, F32)

    return {
        "x": jax.random.normal(ks[0], (BATCH, SEQ, D_MODEL), F32),
        "w_sb_in": w(ks[1], (N_SB_LAYERS, D_MODEL, 3 * D_MODEL), D_MODEL),
        "w_sb_out": w(ks[2], (N_SB_LAYERS, D_MODEL, D_MODEL), D_MODEL),
        "w_ret_in": w(ks[3], (N_RET_LAYERS, D_MODEL, 6 * D_MODEL), D_MODEL),
        "w_ret_out": w(ks[4], (N_RET_LAYERS, 2 * D_MODEL, D_MODEL), 2 * D_MODEL),
        "g_mix": gain(ks[5], (DEPTH, D_MODEL)),
        "g_mlp": gain(ks[6], (DEPTH, D_MODEL)),
        "w_mlp_up": w(ks[7], (DEPTH, D_MODEL, MLP_HIDDEN), D_MODEL),
        "w_mlp_down": w(ks[8], (DEPTH, MLP_HIDDEN, D_MODEL), MLP_HIDDEN),
        "g_final": gain(ks[9], (D_MODEL,)),
    }

def first_block(x, w_sb_in, w_sb_out, w_ret_in, w_ret_out, g_mix, g_mlp, w_mlp_up, w_mlp_down, g_final):
    h = x
    for layer in range(DEPTH):
        hn = rms_norm(h, g_mix[layer])
        i = layer // N_MIXERS
        if layer % N_MIXERS == 0:
            h = h + stick_breaking_attention(hn, w_sb_in[i], w_sb_out[i])
        else:
            h = h + retention(hn, w_ret_in[i], w_ret_out[i])
        h = h + squared_relu_mlp(rms_norm(h, g_mlp[layer]), w_mlp_up[layer], w_mlp_down[layer])
    return rms_norm(h, g_final)


N_A_LAYERS = DEPTH // 2
N_B_LAYERS = DEPTH - N_A_LAYERS
EPS = 1e-6
NEG_INF = -1e30
ROPE_THETA = 10000.0

GLA_HEADS = 4
GLA_DK = D_MODEL // (2 * GLA_HEADS)
GLA_DV = D_MODEL // GLA_HEADS
GLA_GATE_RANK = 16
GLA_TAU = 16.0
GLA_CHUNK = 64
GLA_IN = 2 * GLA_HEADS * GLA_DK + 2 * GLA_HEADS * GLA_DV + GLA_GATE_RANK

NSA_HEADS = 16
NSA_KV_HEADS = 4
NSA_GROUP = NSA_HEADS // NSA_KV_HEADS
NSA_HEAD_DIM = D_MODEL // NSA_HEADS
CMP_BLOCK = 32
CMP_STRIDE = 16
CMP_HIDDEN = 4 * NSA_HEAD_DIM
SEL_BLOCK = 64
SEL_TOPK = 16
WINDOW = 512
NSA_QCHUNK = 32
NSA_IN = NSA_HEADS * NSA_HEAD_DIM + 3 * NSA_HEADS
NSA_KV_OUT = 6 * NSA_KV_HEADS * NSA_HEAD_DIM
FORCE_SCORE = 1e4

FFN_DIM = 2816
CONV_WIDTH = 3


def rmsnorm(x, g):
    x32 = x.astype(jnp.float32)
    y = x32 * lax.rsqrt(jnp.mean(x32 * x32, axis=-1, keepdims=True) + EPS)
    return (y * g).astype(x.dtype)

def rope(x, pos):
    half = x.shape[-1] // 2
    inv = ROPE_THETA ** (-jnp.arange(half, dtype=jnp.float32) / half)
    ang = pos.astype(jnp.float32)[:, None] * inv[None, :]
    cos, sin = jnp.cos(ang), jnp.sin(ang)
    x1 = x[..., :half].astype(jnp.float32)
    x2 = x[..., half:].astype(jnp.float32)
    return jnp.concatenate([x1 * cos - x2 * sin, x1 * sin + x2 * cos], axis=-1).astype(x.dtype)

def masked_softmax(s, mask):
    s = jnp.where(mask, s.astype(jnp.float32), NEG_INF)
    return jnp.where(mask, jax.nn.softmax(s, axis=-1), 0.0)

def conv_ffn(h, w_up, conv_w, conv_b, w_down):
    S = h.shape[1]
    u = h @ w_up
    up = jnp.pad(u, ((0, 0), (CONV_WIDTH - 1, 0), (0, 0)))
    u = conv_b + up[:, 0:S] * conv_w[0]
    for j in range(1, CONV_WIDTH):
        u = u + up[:, j:j + S] * conv_w[j]
    gate, val = jnp.split(u, 2, axis=-1)
    return (jax.nn.silu(gate) * val) @ w_down

def gla_mixer(h, w_in, w_alpha_up, b_alpha, g_out, w_o):
    Bsz, S, _ = h.shape
    H, DK, DV, C = GLA_HEADS, GLA_DK, GLA_DV, GLA_CHUNK
    NC = S // C
    proj = h @ w_in
    splits = [H * DK, 2 * H * DK, 2 * H * DK + H * DV, 2 * H * DK + 2 * H * DV]
    q, k, v, r, a_low = jnp.split(proj, splits, axis=-1)
    log_a = jax.nn.log_sigmoid((a_low @ w_alpha_up + b_alpha).astype(jnp.float32)) / GLA_TAU

    def to_chunks(t, d):
        return t.astype(jnp.float32).reshape(Bsz, NC, C, H, d).transpose(1, 0, 3, 2, 4)

    qc = to_chunks(q, DK) * DK ** -0.5
    kc = to_chunks(k, DK)
    vc = to_chunks(v, DV)
    gc = to_chunks(log_a, DK)
    causal = jnp.tril(jnp.ones((C, C), dtype=bool))[:, :, None]

    def step(state, inp):
        q_, k_, v_, g_ = inp
        b = jnp.cumsum(g_, axis=2)
        o_inter = jnp.einsum('bhtk,bhkv->bhtv', q_ * jnp.exp(b), state)
        diff = b[:, :, :, None, :] - b[:, :, None, :, :]
        decay = jnp.where(causal, jnp.exp(jnp.minimum(diff, 0.0)), 0.0)
        att = jnp.einsum('bhtk,bhsk,bhtsk->bhts', q_, k_, decay)
        o_intra = jnp.einsum('bhts,bhsv->bhtv', att, v_)
        b_last = b[:, :, -1:, :]
        new_state = state * jnp.exp(b_last[:, :, 0, :, None]) + jnp.einsum(
            'bhsk,bhsv->bhkv', k_ * jnp.exp(b_last - b), v_)
        return new_state, o_inter + o_intra

    state0 = jnp.zeros((Bsz, H, DK, DV), jnp.float32)
    _, o = lax.scan(step, state0, (qc, kc, vc, gc))
    o = o.transpose(1, 0, 3, 2, 4).reshape(Bsz, S, H, DV)
    o = o * lax.rsqrt(jnp.mean(o * o, axis=-1, keepdims=True) + EPS) * g_out
    o = o.reshape(Bsz, S, H * DV).astype(h.dtype) * jax.nn.silu(r)
    return o @ w_o

def compress_blocks(t_raw, pe, w1, w2):
    Bsz, Hk, S, Dh = t_raw.shape
    n_cmp = (S - CMP_BLOCK) // CMP_STRIDE + 1
    idx = np.arange(n_cmp)[:, None] * CMP_STRIDE + np.arange(CMP_BLOCK)[None, :]
    blocks = (t_raw[:, :, idx, :] + pe).reshape(Bsz, Hk, n_cmp, CMP_BLOCK * Dh)
    return jax.nn.gelu(blocks @ w1) @ w2

def cmp_to_sel_weights(S):
    n_cmp = (S - CMP_BLOCK) // CMP_STRIDE + 1
    n_sel = S // SEL_BLOCK
    c0 = np.arange(n_cmp)[:, None] * CMP_STRIDE
    s0 = np.arange(n_sel)[None, :] * SEL_BLOCK
    ov = np.clip(np.minimum(c0 + CMP_BLOCK, s0 + SEL_BLOCK) - np.maximum(c0, s0), 0, None)
    return (ov / CMP_BLOCK).astype(np.float32)

def nsa_shared_kv(x, g_kv, w_kv, pe_k, pe_v, wk1, wk2, wv1, wv2):
    Bsz, S, _ = x.shape
    hn = rmsnorm(x, g_kv)
    kv = (hn @ w_kv).reshape(Bsz, S, 6, NSA_KV_HEADS, NSA_HEAD_DIM).transpose(2, 0, 3, 1, 4)
    pos = jnp.arange(S)
    k_cmp = compress_blocks(kv[0], pe_k, wk1, wk2)
    v_cmp = compress_blocks(kv[1], pe_v, wv1, wv2)
    k_sel = rope(kv[2], pos)
    k_win = rope(kv[4], pos)
    return k_cmp, v_cmp, k_sel, kv[3], k_win, kv[5]

gather_blocks = jax.vmap(jax.vmap(lambda blocks, ix: blocks[ix]))

def nsa_mixer(h, w_in, w_o, k_cmp, v_cmp, k_sel, v_sel, k_win, v_win):
    Bsz, S, _ = h.shape
    Hk, G, Dh, SB, QC = NSA_KV_HEADS, NSA_GROUP, NSA_HEAD_DIM, SEL_BLOCK, NSA_QCHUNK
    n_cmp = k_cmp.shape[2]
    n_sel = S // SB
    top = min(SEL_TOPK, n_sel)
    scale = Dh ** -0.5
    pos = jnp.arange(S)
    proj = h @ w_in
    q = proj[..., :NSA_HEADS * Dh].reshape(Bsz, S, Hk, G, Dh).transpose(0, 2, 3, 1, 4)
    gates = jax.nn.sigmoid(proj[..., NSA_HEADS * Dh:].astype(jnp.float32))
    gates = gates.reshape(Bsz, S, 3, Hk, G).transpose(2, 0, 3, 4, 1)[..., None]

    cmp_end = jnp.arange(n_cmp) * CMP_STRIDE + CMP_BLOCK - 1
    p_cmp = masked_softmax(jnp.einsum('bkgsd,bknd->bkgsn', q, k_cmp) * scale,
                           cmp_end[None, :] <= pos[:, None])
    o_cmp = jnp.einsum('bkgsn,bknd->bkgsd', p_cmp, v_cmp)

    imp = jnp.einsum('bkgsn,nj->bksj', p_cmp, jnp.asarray(cmp_to_sel_weights(S)))
    blk = jnp.arange(n_sel)[None, :]
    cur = (pos // SB)[:, None]
    forced = (blk == 0) | (blk == cur) | (blk == cur - 1)
    imp = jnp.where(blk > cur, -1.0, jnp.where(forced, FORCE_SCORE, imp))
    _, sel_idx = lax.top_k(imp, top)

    q_rot = rope(q, pos)
    k_blocks = k_sel.reshape(Bsz, Hk, n_sel, SB, Dh)
    v_blocks = v_sel.reshape(Bsz, Hk, n_sel, SB, Dh)
    pad = ((0, 0), (0, 0), (WINDOW, 0), (0, 0))
    k_win_pad = jnp.pad(k_win, pad)
    v_win_pad = jnp.pad(v_win, pad)

    def chunk(c):
        t0 = c * QC
        qc = lax.dynamic_slice_in_dim(q_rot, t0, QC, axis=3)
        qpos = t0 + jnp.arange(QC)
        idx = lax.dynamic_slice_in_dim(sel_idx, t0, QC, axis=2)
        ks = gather_blocks(k_blocks, idx).reshape(Bsz, Hk, QC, top * SB, Dh)
        vs = gather_blocks(v_blocks, idx).reshape(Bsz, Hk, QC, top * SB, Dh)
        kpos = (idx[..., None] * SB + jnp.arange(SB)).reshape(Bsz, Hk, 1, QC, top * SB)
        p_sel = masked_softmax(jnp.einsum('bkgqd,bkqmd->bkgqm', qc, ks) * scale,
                               kpos <= qpos[:, None])
        o_sel = jnp.einsum('bkgqm,bkqmd->bkgqd', p_sel, vs)
        kw = lax.dynamic_slice_in_dim(k_win_pad, t0, WINDOW + QC, axis=2)
        vw = lax.dynamic_slice_in_dim(v_win_pad, t0, WINDOW + QC, axis=2)
        kwpos = t0 - WINDOW + jnp.arange(WINDOW + QC)
        dist = qpos[:, None] - kwpos[None, :]
        win_mask = (kwpos[None, :] >= 0) & (dist >= 0) & (dist < WINDOW)
        p_win = masked_softmax(jnp.einsum('bkgqd,bknd->bkgqn', qc, kw) * scale, win_mask)
        o_win = jnp.einsum('bkgqn,bknd->bkgqd', p_win, vw)
        return o_sel, o_win

    o_sel, o_win = lax.map(chunk, jnp.arange(S // QC))
    o_sel = jnp.moveaxis(o_sel, 0, 3).reshape(Bsz, Hk, G, S, Dh)
    o_win = jnp.moveaxis(o_win, 0, 3).reshape(Bsz, Hk, G, S, Dh)
    o = gates[0] * o_cmp + gates[1] * o_sel + gates[2] * o_win
    o = o.transpose(0, 3, 1, 2, 4).reshape(Bsz, S, NSA_HEADS * Dh).astype(h.dtype)
    return o @ w_o

def second_inputs(seed: int = 0) -> dict:
    key = jax.random.key(seed)
    ks = jax.random.split(key, 32)
    f32 = jnp.float32

    def nrm(k, shape, fan_in):
        return jax.random.normal(k, shape, f32) * fan_in ** -0.5

    def gain(k, shape):
        return 1.0 + 0.02 * jax.random.normal(k, shape, f32)

    two_f = 2 * FFN_DIM
    return {
        'x': jax.random.normal(ks[0], (BATCH, SEQ, D_MODEL), f32),
        'norm_mix': gain(ks[1], (DEPTH, D_MODEL)),
        'norm_ffn': gain(ks[2], (DEPTH, D_MODEL)),
        'gla_w_in': nrm(ks[3], (N_A_LAYERS, D_MODEL, GLA_IN), D_MODEL),
        'gla_w_alpha_up': nrm(ks[4], (N_A_LAYERS, GLA_GATE_RANK, GLA_HEADS * GLA_DK), GLA_GATE_RANK),
        'gla_b_alpha': 0.1 * jax.random.normal(ks[5], (N_A_LAYERS, GLA_HEADS * GLA_DK), f32),
        'gla_norm': gain(ks[6], (N_A_LAYERS, GLA_HEADS, GLA_DV)),
        'gla_w_o': nrm(ks[7], (N_A_LAYERS, GLA_HEADS * GLA_DV, D_MODEL), GLA_HEADS * GLA_DV),
        'kv_norm': gain(ks[8], (D_MODEL,)),
        'nsa_w_kv': nrm(ks[9], (D_MODEL, NSA_KV_OUT), D_MODEL),
        'cmp_pe_k': 0.02 * jax.random.normal(ks[10], (CMP_BLOCK, NSA_HEAD_DIM), f32),
        'cmp_pe_v': 0.02 * jax.random.normal(ks[11], (CMP_BLOCK, NSA_HEAD_DIM), f32),
        'cmp_k_w1': nrm(ks[12], (CMP_BLOCK * NSA_HEAD_DIM, CMP_HIDDEN), CMP_BLOCK * NSA_HEAD_DIM),
        'cmp_k_w2': nrm(ks[13], (CMP_HIDDEN, NSA_HEAD_DIM), CMP_HIDDEN),
        'cmp_v_w1': nrm(ks[14], (CMP_BLOCK * NSA_HEAD_DIM, CMP_HIDDEN), CMP_BLOCK * NSA_HEAD_DIM),
        'cmp_v_w2': nrm(ks[15], (CMP_HIDDEN, NSA_HEAD_DIM), CMP_HIDDEN),
        'nsa_w_in': nrm(ks[16], (N_B_LAYERS, D_MODEL, NSA_IN), D_MODEL),
        'nsa_w_o': nrm(ks[17], (N_B_LAYERS, NSA_HEADS * NSA_HEAD_DIM, D_MODEL), NSA_HEADS * NSA_HEAD_DIM),
        'ffn_w_up': nrm(ks[18], (DEPTH, D_MODEL, two_f), D_MODEL),
        'ffn_conv_w': nrm(ks[19], (DEPTH, CONV_WIDTH, two_f), CONV_WIDTH),
        'ffn_conv_b': 0.02 * jax.random.normal(ks[20], (DEPTH, two_f), f32),
        'ffn_w_down': nrm(ks[21], (DEPTH, FFN_DIM, D_MODEL), FFN_DIM),
        'norm_final': gain(ks[22], (D_MODEL,)),
    }

def second_block(x, norm_mix, norm_ffn, gla_w_in, gla_w_alpha_up, gla_b_alpha, gla_norm, gla_w_o,
              kv_norm, nsa_w_kv, cmp_pe_k, cmp_pe_v, cmp_k_w1, cmp_k_w2, cmp_v_w1, cmp_v_w2,
              nsa_w_in, nsa_w_o, ffn_w_up, ffn_conv_w, ffn_conv_b, ffn_w_down, norm_final):
    shared = None
    for layer in range(DEPTH):
        if layer < N_A_LAYERS:
            hn = rmsnorm(x, norm_mix[layer])
            x = x + gla_mixer(hn, gla_w_in[layer], gla_w_alpha_up[layer], gla_b_alpha[layer],
                              gla_norm[layer], gla_w_o[layer])
        else:
            if layer == N_A_LAYERS:
                shared = nsa_shared_kv(x, kv_norm, nsa_w_kv, cmp_pe_k, cmp_pe_v,
                                       cmp_k_w1, cmp_k_w2, cmp_v_w1, cmp_v_w2)
            b = layer - N_A_LAYERS
            hn = rmsnorm(x, norm_mix[layer])
            x = x + nsa_mixer(hn, nsa_w_in[b], nsa_w_o[b], *shared)
        hn = rmsnorm(x, norm_ffn[layer])
        x = x + conv_ffn(hn, ffn_w_up[layer], ffn_conv_w[layer], ffn_conv_b[layer], ffn_w_down[layer])
    return rmsnorm(x, norm_final)


def setup_inputs(seed=0):
    out = dict(first_inputs(seed))
    for name, value in second_inputs(seed + 1).items():
        if name != "x":
            out[name + "_2"] = value
    return out


def reference(
    x, w_sb_in, w_sb_out, w_ret_in, w_ret_out, g_mix, g_mlp, w_mlp_up, w_mlp_down, g_final,
    norm_mix_2, norm_ffn_2, gla_w_in_2, gla_w_alpha_up_2, gla_b_alpha_2, gla_norm_2, gla_w_o_2,
    kv_norm_2, nsa_w_kv_2, cmp_pe_k_2, cmp_pe_v_2, cmp_k_w1_2, cmp_k_w2_2, cmp_v_w1_2,
    cmp_v_w2_2, nsa_w_in_2, nsa_w_o_2, ffn_w_up_2, ffn_conv_w_2, ffn_conv_b_2, ffn_w_down_2,
    norm_final_2,
):
    x = first_block(
        x, w_sb_in, w_sb_out, w_ret_in, w_ret_out, g_mix, g_mlp, w_mlp_up, w_mlp_down, g_final,
    )
    return second_block(
        x, norm_mix_2, norm_ffn_2, gla_w_in_2, gla_w_alpha_up_2, gla_b_alpha_2, gla_norm_2,
        gla_w_o_2, kv_norm_2, nsa_w_kv_2, cmp_pe_k_2, cmp_pe_v_2, cmp_k_w1_2, cmp_k_w2_2,
        cmp_v_w1_2, cmp_v_w2_2, nsa_w_in_2, nsa_w_o_2, ffn_w_up_2, ffn_conv_w_2, ffn_conv_b_2,
        ffn_w_down_2, norm_final_2,
    )


_drawn_inputs = setup_inputs


def setup_inputs(seed=0):
    import zlib

    import numpy as np

    out = dict(_drawn_inputs(seed))
    spreads = {}
    factors = {'norm_ffn_2': 3.129,
     'gla_norm_2': 4.837,
     'kv_norm_2': 8.0,
     'cmp_pe_k_2': 64.0,
     'cmp_pe_v_2': 64.0,
     'ffn_conv_b_2': 3.095,
     'norm_final_2': 8.678}
    for name, (base, spread) in spreads.items():
        noise = np.random.default_rng([zlib.crc32(name.encode()), seed]).standard_normal(out[name].shape)
        drawn = base * np.exp(spread * noise) if base else spread * noise
        out[name] = __import__('jax').numpy.asarray(drawn.astype(out[name].dtype))
    for name, factor in factors.items():
        out[name] = (out[name] * factor).astype(out[name].dtype)
    return out
```

```python
import numpy as np
import concourse.bass as bass
from concourse import mybir

F32 = mybir.dt.float32
I32 = mybir.dt.int32
ALU = mybir.AluOpType
ACT = mybir.ActivationFunctionType
AX = mybir.AxisListType

T = 256
D = 1024
P = 128
TT = T // P
KT = D // P
CH = 4096
RING = 4
EPS = 1e-6
NEG = -1e30
SB_HEADS, RET_HEADS, GLA_HEADS, NSA_HEADS, NSA_KV = 16, 4, 4, 16, 4
MLP_C = 4 * D // 512
FFN_TILES = 2816 // P
FFN_C = FFN_TILES // 2
CMP = 16
SOFT_CAP = 30.0

GAINS = 9
S_GAIN = 0
S_CONV = S_GAIN + GAINS * KT
S_BALPHA = S_CONV + 2 * FFN_TILES * 8
S_WALOW = S_BALPHA + 4
S_WGATE = S_WALOW + KT * 16
S_W2K = S_WGATE + KT * 48
S_W2V = S_W2K + 2 * P
S_PE = S_W2V + 2 * 64
S_ALPHA = S_PE + 2 * 16
S_TOTAL = S_ALPHA + 512

C_ID = 0
C_NTRI = C_ID + P
C_NONE = C_NTRI + P
C_COS = C_NONE + P
C_SIN = C_COS + T
C_DECAY = C_SIN + T
C_RCOS = C_DECAY + RET_HEADS * 384
C_RSIN = C_RCOS + T
C_SWAP = C_RSIN + T
C_CAUSAL = C_SWAP + P
C_CADD = C_CAUSAL + 384
C_CMUL = C_CADD + TT * CMP
C_BD = C_CMUL + TT * CMP
C_LEVEL = C_BD + 8
C_TOTAL = C_LEVEL + 8 * P

Q_SB = 0
Q_MLP = (8, 40)
Q_RET = 24
Q_GLA = 56
Q_FFN = (64, 95)
Q_NSA = 86
Q_END = 117
ARENA = 18600


def build(nc, ws, wd, small, consts, rows, x_in, out):
    from contextlib import ExitStack
    ctx = ExitStack()
    with ctx:
        def sb(name, shape):
            return ctx.enter_context(nc.sbuf_tensor(name, shape, F32))

        def sem(name):
            return ctx.enter_context(nc.semaphore(name))

        ring = sb("ring", [P, RING, CH])
        h = sb("h", [P, TT, D])
        xs = sb("xs", [P, TT, D])
        xT = sb("xT", [P, KT, T])
        sm = sb("sm", [P, S_TOTAL])
        cs = sb("cs", [P, C_TOTAL])
        rowg = sb("rowg", [P, 3, D])
        stat = sb("stat", [P, 96])
        power = sb("power", [P, 16])
        arena = sb("arena", [P, ARENA])
        ps = ctx.enter_context(nc.psum_tensor("ps", [P, 8, 512], F32))

        ident = cs[:, C_ID:C_ID + P]
        ssq, msq, rstd = stat[:, 0:2], stat[:, 2:4], stat[:, 4:6]
        ss8, ms8, rs8 = stat[:, 8:16], stat[:, 16:24], stat[:, 24:32]
        mv = stat[:, 32:48].rearrange("p (i c) -> p i c", c=2)
        bn = stat[:, 48:96].rearrange("p (i c) -> p i c", c=6)

        def region(at, *dims):
            n = int(np.prod(dims))
            assert at + n <= ARENA, (at, n)
            v = arena[:, at:at + n]
            if len(dims) == 2:
                v = v.rearrange("p (a b) -> p a b", b=dims[1])
            if len(dims) == 3:
                v = v.rearrange("p (a b c) -> p a b c", b=dims[1], c=dims[2])
            return v

        hT = region(0, 2, 4, T)
        relu = region(2048, 2, 512)
        conv = region(3072, 2, 2, T)
        silu = region(4096, 2, T)
        sb_q, sb_k, sb_v, sb_o = region(0, KT, T), region(2048, KT, T), region(4096, TT, D), region(6144, KT, T)
        sb_e, sb_s, sb_a = region(8192, 2, 2, 384), region(9728, 2, 2, 384), region(11264, 2, 2, 384)
        rt_q, rt_k = region(0, KT, T), region(2048, KT, T)
        rt_v, rt_g = region(4096, TT, 2 * D), region(8192, TT, 2 * D)
        rt_s = region(12288, RET_HEADS, 384)
        rt_c, rt_n = region(13824, 2, 512), region(14848, 2, 512)
        rt_y = region(0, 2 * KT, T)
        gl_q, gl_k = region(0, 4, T), region(1024, 4, T)
        gl_v, gl_r = region(2048, TT, D), region(4096, TT, D)
        gl_c, gl_x, gl_l = region(6144, 4, T), region(7168, 4, T), region(8192, 4, T)
        gl_w = [region(9216 + 1024 * j, 4, T) for j in range(8)]
        gl_a = [region(17408 + 0, 4, P), region(17408 + 512, 4, P)]
        gl_across = gl_x[:, 0:2, :].rearrange("p a (b c) -> p (a b) c", c=P)
        gl_low = gl_l[0:16, 0, :]
        gl_y = region(9216, KT, T)
        xT2 = region(0, KT, T)
        ns_raw = region(2048, 2, NSA_KV, T)
        ns_x = region(4096, 2, 16, 60)
        ns_t2 = region(4096, 2, T)
        ns_s = region(4096, 2, 2, 384)
        ns_h = region(6016, 4, 2, 64)
        ns_hv = region(6528, 2, 2, P)
        ns_kc = region(7040, NSA_KV, CMP)
        ns_gate = region(7104, TT, 48)
        ns_m = region(7200, 2, 2, 2)
        ns_l = region(7208, 2, 2, 2)
        ns_f = region(7216, 2, 2, 2)
        ns_cm, ns_cl = region(7232, TT, 16), region(7264, TT, 16)
        ns_vbd = region(7296, 2, 8, 64)
        ns_kd = region(8320, 2, NSA_KV, T)
        ns_v = region(10368, TT, 512)
        ns_q, ns_qr = region(11392, KT, T), region(13440, KT, T)
        ns_k, ns_t1 = region(15488, 2, 2, T), region(16512, 2, T)
        ns_p = region(15488, 2, 2, 384)
        ns_cs, ns_cp = region(17024, TT, 16, CMP), region(17536, 4, P)
        ns_on, ns_oT = region(2048, TT, D), region(0, KT, T)

        loaded = sem("small_loaded")
        rows_in = sem("rows_loaded")
        weights_in = [sem(f"weights_in{s}") for s in range(RING)]
        half_done = sem("chunk_half_done")
        ss_ready, ms_ready, rstd_ready = sem("sumsq_ready"), sem("meansq_ready"), sem("rstd_ready")
        xs_ready, xt_done = sem("xs_ready"), sem("norm_transposed")
        xT_a, xT_d = sem("xT_by_act"), sem("xT_by_dve")
        h_ready = sem("h_ready")
        pow_ready = sem("power_ready")
        act_step, dve_step = sem("act_step"), sem("dve_step")
        stored = sem("stored")

        class Evac:
            def __init__(self, name):
                self.freed = sem(name + "_unit_freed")

        def bank(u):
            return 4 + u % 4

        def slot(q):
            return q % RING

        def chunk(q):
            return ring[:, slot(q), :]

        MID = [0, 0]

        def pos_u(c):
            return c if c < 2 else 3 + 4 * ((c - 2) // 2) + 2 * ((c - 2) % 2)

        H_AT = [0, 4, 8, 12, 16, 18, 22, 26, 30, 34]
        TRANSPOSED = [0, 1, 2, 3, 5, 6, 7, 8]
        GAIN_OF = {0: [0], 1: [1], 2: [2], 3: [3], 5: [4], 6: [5], 7: [6, 7], 8: [8]}

        sb_u, rt_u, gl_u, ns_u = Evac("sb"), Evac("ret"), Evac("gla"), Evac("nsa")
        sbz, sbc, sbe, sbl, sbm = sem("sb_z"), sem("sb_clipped"), sem("sb_exp"), sem("sb_log"), sem("sb_softplus")
        sbs, sbt, sbx, sba, sbo, sbv = (sem("sb_masked"), sem("sb_summed"), sem("sb_weights"), sem("sb_wmasked"),
                                        sem("sb_out"), sem("sb_out_copied"))
        mlp_s = [(sem(f"mlp{i}_freed"), sem(f"mlp{i}_hidden")) for i in range(2)]
        ffn_s = [(sem(f"ffn{i}_freed"), sem(f"ffn{i}_hidden"), sem(f"ffn{i}_base"), sem(f"ffn{i}_tap"),
                  sem(f"ffn{i}_silu")) for i in range(2)]
        rt_qk, rt_sc, rt_dec, rt_o, rt_of, rt_ms, rt_rs, rt_yr, rt_tr, rt_ya, rt_yd = (
            sem("ret_qk"), sem("ret_scores"), sem("ret_decayed"), sem("ret_o"), sem("ret_o_free"),
            sem("ret_var"), sem("ret_rstd"), sem("ret_y"), sem("ret_transposed"), sem("ret_yT_act"), sem("ret_yT_dve"))
        gl_pj, gl_x_r, gl_e, gl_lg, gl_df, gl_ex, gl_wr, gl_lv, gl_cp, gl_o, gl_s, gl_m, gl_p, gl_yr, gl_tr, gl_ya, gl_yd, gl_rg = (
            sem("gla_small_proj"), sem("gla_logit"), sem("gla_exp"), sem("gla_log"), sem("gla_diff"), sem("gla_decay"),
            sem("gla_w"), sem("gla_level"), sem("gla_level_copied"), sem("gla_o"), sem("gla_sumsq"), sem("gla_meansq"),
            sem("gla_rstd"), sem("gla_y"), sem("gla_transposed"), sem("gla_yT_act"), sem("gla_yT_dve"), sem("gla_gate"))
        ns_pj, ns_xr, ns_hd, ns_sq, ns_u1, ns_th, ns_hr, ns_kv, ns_kcr, ns_vr, ns_qrr = (
            sem("nsa_small_proj"), sem("nsa_blocks"), sem("nsa_hidden"), sem("nsa_square"), sem("nsa_inner"),
            sem("nsa_tanh"), sem("nsa_gelu"), sem("nsa_cmp_kv"), sem("nsa_kc"), sem("nsa_vbd"), sem("nsa_roped"))
        ns_kdr, ns_cq, ns_ci, ns_ce, ns_cpr, ns_ct, ns_cc = (
            sem("nsa_kd"), sem("nsa_cmp_scores"), sem("nsa_cmp_shifted"), sem("nsa_cmp_exp"), sem("nsa_cmp_p"),
            sem("nsa_cmp_pT"), sem("nsa_cmp_pT_copied"))
        ns_qk, ns_add, ns_mx, ns_ex, ns_co, ns_pr, ns_tp, ns_tc, ns_o, ns_oc, ns_ot, ns_oa, ns_od = (
            sem("nsa_scores"), sem("nsa_masked"), sem("nsa_max"), sem("nsa_exp"), sem("nsa_coef"), sem("nsa_p"),
            sem("nsa_pT"), sem("nsa_pT_copied"), sem("nsa_o"), sem("nsa_o_copied"), sem("nsa_oT"),
            sem("nsa_oT_act"), sem("nsa_oT_dve"))

        block = ctx.enter_context(nc.Block())

        @block.sync
        def _(sp):
            sp.dma_start(h[:, :, :], x_in.rearrange("(t p) d -> p t d", p=P)).then_inc(loaded, 16)

            def load(q, src, words, free):
                if free:
                    sp.wait_ge(half_done, 2 * (q - RING) + 2)
                sp.dma_start(ring[:, slot(q), 0:words] if isinstance(q, int) else None, src)

            def stream(q, words, src, base=0):
                if not (isinstance(base, int) and q + base < RING):
                    sp.wait_ge(half_done, 2 * (q - RING) + 2 + 2 * base)
                sp.dma_start(ring[:, slot(q), 0:words], src).then_inc(weights_in[slot(q)], 16)

            def full(i):
                return ws[i] if isinstance(i, int) else ws[bass.ds(i, 1), :, :].rearrange("a p n -> p (a n)")

            def half(i):
                return wd[i] if isinstance(i, int) else wd[bass.ds(i, 1), :, :].rearrange("a p n -> p (a n)")

            for q in range(RING):
                stream(q, CH, full(q))
            with sp.Fori(1, Q_FFN[0] // RING) as it:
                for j in range(RING):
                    stream(j, CH, full(it * RING + j), it * RING)
            w, d = Q_FFN[0], 0
            for n in range(2):
                q = Q_FFN[n]
                stream(q, CH, full(w))
                stream(q + 1, CH, full(w + 1))
                stream(q + 2, CH // 2, half(d))
                with sp.Fori(0, (FFN_C - 3) // 2) as it:
                    stream(q + 3, CH, full(it * 2 + (w + 2)), it * RING)
                    stream(q + 4, CH // 2, half(it * 2 + (d + 1)), it * RING)
                    stream(q + 5, CH, full(it * 2 + (w + 3)), it * RING)
                    stream(q + 6, CH // 2, half(it * 2 + (d + 2)), it * RING)
                stream(q + 19, CH, full(w + FFN_C - 1))
                stream(q + 20, CH // 2, half(d + FFN_C - 2))
                stream(q + 21, CH // 2, half(d + FFN_C - 1))
                w, d = w + FFN_C, d + FFN_C
                if n == 0:
                    for j in range(Q_FFN[1] - Q_NSA):
                        stream(Q_NSA + j, CH, full(w + j))
                    w += Q_FFN[1] - Q_NSA
            for t in range(TT):
                sp.wait_ge(xs_ready, 2 * len(TRANSPOSED) + t + 1)
                sp.dma_start(out[t * P:(t + 1) * P, :], xs[:, t, :]).then_inc(stored, 16)
            sp.wait_ge(stored, 16 * TT)

        @block.gpsimd
        def _(pool):
            gp = nc.gpsimd
            pool.dma_start(rowg[:, :, :], rows.partition_broadcast(P)).then_inc(rows_in, 16)
            gp.memset(power[:, :], -0.5).then_inc(pow_ready, 1)
            pool.wait_ge(pow_ready, 1)

            def norm_power(n):
                pool.wait_ge(ms_ready, n + 1)
                gp.tensor_tensor(rstd, msq, power[:, 0:2], ALU.pow).then_inc(rstd_ready, 1)

            norm_power(0)

            def below(v):
                for d in (v[:, :, 0:P], v[:, :, T:384]):
                    r = gp.affine_select(out=d, in_=d, compare_op=ALU.is_gt, fill=0.0, base=0,
                                         pattern=[[0, 2], [1, P]], channel_multiplier=-1)
                return r

            def sp_mask(p):
                pool.wait_ge(sbm, p + 1)
                below(sb_s[:, p % 2]).then_inc(sbs, 1)

            sp_mask(0)
            sp_mask(1)
            for p in range(8):
                pool.wait_ge(sbx, p + 1)
                below(sb_a[:, p % 2]).then_inc(sba, 1)
                if p + 2 < 8:
                    sp_mask(p + 2)
            norm_power(1)
            norm_power(2)
            for u in range(8):
                dst = rt_q if u < 4 else rt_k
                v = dst[:, 2 * (u % 4):2 * (u % 4) + 2, :]
                a, b = rt_c[:, u % 2, :], rt_n[:, u % 2, :]
                pool.wait_ge(rt_u.freed, u + 1)
                gp.tensor_tensor(v[:, 0, :], a[:, 0:T], b[:, T:2 * T], ALU.subtract)
                gp.tensor_tensor(v[:, 1, :], b[:, 0:T], a[:, T:2 * T], ALU.add).then_inc(rt_qk, 1)
            pool.wait_ge(rt_ms, 1)
            gp.tensor_tensor(rs8, ms8, power[:, 0:8], ALU.pow).then_inc(rt_rs, 1)
            norm_power(3)
            norm_power(4)
            norm_power(5)
            pool.wait_ge(rows_in, 16)
            for t in range(TT):
                pool.wait_ge(gl_u.freed, 14 + t)
                gp.tensor_tensor(gl_r[:, t, :], gl_r[:, t, :], rowg[:, 1, :], ALU.mult).then_inc(gl_rg, 1)
            pool.wait_ge(gl_m, 1)
            gp.tensor_tensor(rs8, ms8, power[:, 0:8], ALU.pow).then_inc(gl_p, 1)
            norm_power(6)
            norm_power(7)
            for it in range(16):
                pool.wait_ge(ns_co, it + 1)
                for t in range(2):
                    v = ns_s[:, it % 2, :, P * t:P * t + P * (t + 1)]
                    f = ns_f[:, it % 2, :, t:t + 1].broadcast_to([P, 2, P * (t + 1)])
                    r = gp.tensor_tensor(v, v, f, ALU.mult)
                r.then_inc(ns_pr, 1)
            norm_power(8)
            norm_power(9)

        @block.tensor
        def _(pe):
            mm = nc.tensor.matmul

            def arrived(q, base=0):
                pe.wait_ge(weights_in[slot(q)], 16 * (q // RING + 1) + (0 if isinstance(base, int) else base))

            def norm(n):
                i = TRANSPOSED.index(n)
                for t in range(TT):
                    pe.wait_ge(xs_ready, 2 * i + t + 1)
                    for k in range(KT):
                        r = nc.tensor.transpose(ps[:, 4 + k // 2, (k % 2) * T + t * P:(k % 2) * T + (t + 1) * P],
                                                xs[:, t, k * P:(k + 1) * P], ident)
                        if t == 1 and k % 2 == 1:
                            r.then_inc(xt_done, 1)
                pe.wait_ge(xT_a, 2 * (i + 1))
                pe.wait_ge(xT_d, 2 * (i + 1))

            def transposed(q, u, src, freed, first=False, wait=None, turn=0):
                arrived(q, turn * 16 if not isinstance(turn, int) else 0)
                for i in range(2):
                    if wait is not None:
                        pe.wait_ge(freed, wait + i)
                    elif u + i >= 4:
                        pe.wait_ge(freed, u + i - 3)
                    for j in range(2):
                        for k in range(KT):
                            c = k * 512 + (2 * i + j) * P
                            r = mm(ps[:, bank(u + i), j * T:(j + 1) * T], chunk(q)[:, c:c + P], src[:, k, :],
                                   start=k == 0, stop=k == KT - 1)
                    r.then_inc(half_done, 1)

            def natural(q, u, src, freed, wait=None, turn=0):
                arrived(q, turn * 16 if not isinstance(turn, int) else 0)
                for t in range(TT):
                    if wait is not None:
                        pe.wait_ge(freed, wait + t)
                    elif u + t >= 4:
                        pe.wait_ge(freed, u + t - 3)
                    for k in range(KT):
                        r = mm(ps[:, bank(u + t), :], src[:, k, t * P:(t + 1) * P], chunk(q)[:, k * 512:(k + 1) * 512],
                               start=k == 0, stop=k == KT - 1)
                    r.then_inc(half_done, 1)

            def accumulate(q, tiles, first, last, turn=0):
                arrived(q, turn * 16 if not isinstance(turn, int) else 0)
                n = len(tiles)
                for k, tile in enumerate(tiles):
                    for j in range(4):
                        t, s = j // 2, j % 2
                        r = mm(ps[:, j, :], tile[:, t * P:(t + 1) * P],
                               chunk(q)[:, k * D + s * 512:k * D + (s + 1) * 512],
                               start=first and k == 0, stop=last and k == n - 1, skip_group_check=True)
                    if k == n // 2 - 1 or k == n - 1:
                        r.then_inc(half_done, 1)

            def hidden(q0, cs_, tiles, freed, ready):
                rounds = (cs_ - 2) // 2 if tiles == 4 else (cs_ - 3) // 2

                def up(c, q, turn=0):
                    w = None if isinstance(turn, int) else turn * 4 + (2 * c - 3)
                    if w is None:
                        transposed(q, 2 * c, xT, freed)
                    else:
                        transposed(q, 2 * c, xT, freed, wait=w, turn=turn)

                def down(c, q, first=False, last=False, turn=0):
                    if isinstance(turn, int):
                        pe.wait_ge(ready, 2 * c + 2)
                    else:
                        pe.wait_ge(ready, turn * 4 + (2 * c + 2))
                    accumulate(q, [hT[:, c % 2, k, :] for k in range(tiles)], first, last, turn=turn)

                up(0, q0)
                up(1, q0 + 1)
                down(0, q0 + 2, first=True)
                with pe.Fori(0, rounds) as it:
                    up(2, q0 + 3, it)
                    down(1, q0 + 4, turn=it)
                    up(3, q0 + 5, it)
                    down(2, q0 + 6, turn=it)
                q = q0 + 3 + 4 * rounds
                if tiles == 4:
                    down(cs_ - 1, q, last=True)
                else:
                    up(cs_ - 1, q)
                    down(cs_ - 2, q + 1)
                    down(cs_ - 1, q + 2, last=True)

            pe.wait_ge(loaded, 48)
            norm(0)
            for c in range(4):
                transposed(Q_SB + c, 2 * c, xT, sb_u.freed)
            for c in range(4, 6):
                natural(Q_SB + c, 2 * c, xT, sb_u.freed)
            ntri, none = cs[:, C_NTRI:C_NTRI + P], cs[:, C_NONE:C_NONE + P]

            def sb_z_(p):
                if p == 0:
                    pe.wait_ge(sb_u.freed, 12)
                if p >= 2:
                    pe.wait_ge(sbx, p - 1)
                for i in range(2):
                    b, o = 4 + 2 * (p % 2) + i, 64 * i
                    mm(ps[:, b, 0:T], sb_k[o:o + 64, p, 0:P], sb_q[o:o + 64, p, :], start=True, stop=True,
                       skip_group_check=True)
                    r = mm(ps[:, b, T:384], sb_k[o:o + 64, p, P:T], sb_q[o:o + 64, p, P:T], start=False, stop=True,
                           skip_group_check=True)
                r.then_inc(sbz, 1)

            def sb_sum(p):
                pe.wait_ge(sbs, p + 1)
                for i in range(2):
                    b, s = 4 + 2 * (p % 2) + i, sb_s[:, p % 2, i, :]
                    mm(ps[:, b, 0:T], ntri, s[:, 0:T], start=False, stop=True, skip_group_check=True)
                    mm(ps[:, b, P:T], none, s[:, T:384], start=False, stop=True, skip_group_check=True)
                    r = mm(ps[:, b, T:384], ntri, s[:, T:384], start=False, stop=True, skip_group_check=True)
                r.then_inc(sbt, 1)

            def sb_av(p):
                pe.wait_ge(sba, p + 1)
                if p >= 2:
                    pe.wait_ge(sbv, p - 1)
                for i in range(2):
                    c, a = (2 * p + i) * 64, sb_a[:, p % 2, i, :]
                    o = ps[64 * i:64 * i + 64, p % 2, :]
                    mm(o[:, 0:T], sb_v[:, 0, c:c + 64], a[:, 0:T], start=True, stop=False, skip_group_check=True)
                    r = mm(o[:, P:T], sb_v[:, 1, c:c + 64], a[:, T:384], start=False, stop=True, skip_group_check=True)
                r.then_inc(sbo, 1)

            sb_z_(0)
            sb_z_(1)
            for p in range(8):
                sb_sum(p)
                if p:
                    sb_av(p - 1)
                if p + 2 < 8:
                    sb_z_(p + 2)
            sb_av(7)
            pe.wait_ge(sbv, 8)
            for c in range(2):
                accumulate(Q_SB + 6 + c, [sb_o[:, 4 * c + k, :] for k in range(4)], c == 0, c == 1)
            norm(1)
            hidden(Q_MLP[0], MLP_C, 4, *mlp_s[0])

            norm(2)
            for c in range(4):
                transposed(Q_RET + c, 2 * c, xT, rt_u.freed)
            with pe.Fori(0, 2) as it:
                for c in range(4):
                    natural(Q_RET + 4 + c, 8 + 2 * c, xT, rt_u.freed, wait=it * 8 + (8 + 2 * c - 3), turn=it)
            pe.wait_ge(rt_u.freed, 24)
            pe.wait_ge(rt_qk, 8)
            for hd in range(RET_HEADS):
                for k in range(2):
                    mm(ps[:, 4 + hd, 0:T], rt_k[:, 2 * hd + k, 0:P], rt_q[:, 2 * hd + k, :], start=k == 0, stop=k == 1)
                for k in range(2):
                    r = mm(ps[:, 4 + hd, T:384], rt_k[:, 2 * hd + k, P:T], rt_q[:, 2 * hd + k, P:T],
                           start=k == 0, stop=k == 1)
                r.then_inc(rt_sc, 1)
            for hd in range(RET_HEADS):
                pe.wait_ge(rt_dec, hd + 1)
                for t in range(TT):
                    i = 2 * hd + t
                    if i >= 4:
                        pe.wait_ge(rt_of, i - 3)
                    r = mm(ps[:, i % 4, :], rt_s[:, hd, t * P:(t + 1) * P], rt_v[:, 0, hd * 512:(hd + 1) * 512],
                           start=True, stop=t == 0)
                    if t == 1:
                        r = mm(ps[:, i % 4, :], rt_s[:, hd, T:384], rt_v[:, 1, hd * 512:(hd + 1) * 512],
                               start=False, stop=True)
                    r.then_inc(rt_o, 1)
            for g in range(8):
                pe.wait_ge(rt_yr, 2 * (g // 2) + 2)
                if g >= 4:
                    pe.wait_ge(rt_ya if g % 2 == 0 else rt_yd, (g - 4) // 2 + 1)
                for k in range(2):
                    for t in range(TT):
                        r = nc.tensor.transpose(ps[:, bank(g), k * T + t * P:k * T + (t + 1) * P],
                                                rt_g[:, t, (2 * g + k) * P:(2 * g + k + 1) * P], ident)
                r.then_inc(rt_tr, 1)
            for c in range(4):
                pe.wait_ge(rt_ya, c + 1)
                pe.wait_ge(rt_yd, c + 1)
                accumulate(Q_RET + 12 + c, [rt_y[:, 4 * c + k, :] for k in range(4)], c == 0, c == 3)
            norm(3)
            hidden(Q_MLP[1], MLP_C, 4, *mlp_s[1])

            norm(5)
            for k in range(KT):
                r = mm(ps[0:16, 4, 0:T], sm[:, S_WALOW + 16 * k:S_WALOW + 16 * k + 16], xT[:, k, :],
                       start=k == 0, stop=k == KT - 1)
            r.then_inc(gl_pj, 1)
            transposed(Q_GLA, 1, xT, gl_u.freed)
            transposed(Q_GLA + 1, 3, xT, gl_u.freed)
            for i in range(2):
                pe.wait_ge(gl_u.freed, 5 + i - 3)
                for j in range(2):
                    c = S_ALPHA + (2 * i + j) * P
                    r = mm(ps[:, bank(5 + i), j * T:(j + 1) * T], sm[0:16, c:c + P], gl_low, start=True, stop=True)
                r.then_inc(gl_pj, 1)
            for c in range(2):
                natural(Q_GLA + 2 + c, 7 + 2 * c, xT, gl_u.freed)
            for c in range(2):
                natural(Q_GLA + 4 + c, 11 + 2 * c, xT, gl_u.freed)
            for i in range(16):
                l, t = i // 2, i % 2
                if l >= 1:
                    pe.wait_ge(gl_wr, l)
                if i >= 4:
                    pe.wait_ge(gl_cp, i - 3)
                for hd in range(GLA_HEADS):
                    kk = gl_k if l == 0 else gl_w[l - 1]
                    qq = gl_q if l == 0 else gl_w[l - 1]
                    r = mm(ps[:, i % 4, hd * P:(hd + 1) * P], kk[:, hd, t * P:(t + 1) * P], qq[:, hd, t * P:(t + 1) * P],
                           start=True, stop=True)
                r.then_inc(gl_lv, 1)
            pe.wait_ge(gl_wr, 8)
            pe.wait_ge(gl_cp, 13)
            for hd in range(GLA_HEADS):
                r = mm(ps[:, 0, hd * P:(hd + 1) * P], gl_w[7][:, hd, 0:P], gl_w[7][:, hd, P:T], start=True, stop=True)
            r.then_inc(gl_lv, 1)
            pe.wait_ge(gl_u.freed, 15)
            pe.wait_ge(gl_cp, 17)
            for t in range(TT):
                for hd in range(GLA_HEADS):
                    o = ps[:, 4 + 2 * t + hd // 2, (hd % 2) * T:(hd % 2 + 1) * T]
                    v = gl_v[:, :, hd * 256:(hd + 1) * 256]
                    if t == 1:
                        mm(o, gl_across[:, hd, :], v[:, 0, :], start=True, stop=False)
                    r = mm(o, gl_a[t][:, hd, :], v[:, t, :], start=t == 0, stop=True)
                r.then_inc(gl_o, 1)
            for t in range(TT):
                pe.wait_ge(gl_yr, t + 1)
                for k in range(KT):
                    r = nc.tensor.transpose(ps[:, k // 2, (k % 2) * T + t * P:(k % 2) * T + (t + 1) * P],
                                            gl_r[:, t, k * P:(k + 1) * P], ident)
                    if t == 1 and k % 2 == 1:
                        r.then_inc(gl_tr, 1)
            pe.wait_ge(gl_ya, 2)
            pe.wait_ge(gl_yd, 2)
            for c in range(2):
                accumulate(Q_GLA + 6 + c, [gl_y[:, 4 * c + k, :] for k in range(4)], c == 0, c == 1)
            norm(6)
            hidden(Q_FFN[0], FFN_C, 2, ffn_s[0][0], ffn_s[0][1])

            norm(7)
            transposed(Q_NSA, 0, xT, ns_u.freed)
            transposed(Q_NSA + 1, 2, xT, ns_u.freed)
            for i in range(2):
                q = Q_NSA + 2 + i
                pe.wait_ge(ns_xr, i + 1)
                arrived(q)
                for c in range(2):
                    for l in range(16):
                        r = mm(ps[:, i, c * 64:c * 64 + 60], chunk(q)[:, l * 256 + c * P:l * 256 + (c + 1) * P],
                               ns_x[:, i, l, :], start=l == 0, stop=l == 15)
                    r.then_inc(half_done, 1)
            natural(Q_NSA + 4, 4, xT, ns_u.freed)
            for c in range(2):
                transposed(Q_NSA + 5 + c, 6 + 2 * c, xT2, ns_u.freed)
            swap = cs[:, C_SWAP:C_SWAP + P]
            for i in range(6):
                pe.wait_ge(ns_u.freed, 10 + i - 3 if i < 3 else 10 + i - 3)
                if i >= 2:
                    pe.wait_ge(ns_u.freed, 10)
                src = ns_k[:, i, :, :] if i < 2 else ns_q[:, 2 * (i - 2):2 * (i - 2) + 2, :]
                mm(ps[:, bank(10 + i), :], swap, src, start=True, stop=True).then_inc(ns_pj, 1)
            pe.wait_ge(ns_u.freed, 13)
            for t in range(TT):
                for k in range(KT):
                    r = mm(ps[:, bank(16), t * 64:t * 64 + 48], xT2[:, k, t * P:(t + 1) * P],
                           sm[:, S_WGATE + 48 * k:S_WGATE + 48 * (k + 1)], start=k == 0, stop=k == KT - 1)
            r.then_inc(ns_pj, 1)
            pe.wait_ge(ns_hr, 2)
            for c in range(2):
                r = mm(ps[:, 2, 0:64], sm[:, S_W2K + c * P:S_W2K + (c + 1) * P], ns_h[:, 2, c, :],
                       start=c == 0, stop=c == 1)
            r.then_inc(ns_kv, 1)
            pe.wait_ge(ns_hr, 3)
            for g in range(2):
                for c in range(2):
                    r = mm(ps[:, 3, g * 64:(g + 1) * 64], ns_hv[:, g, c, :],
                           sm[:, S_W2V + c * 64:S_W2V + (c + 1) * 64], start=c == 0, stop=c == 1)
            r.then_inc(ns_kv, 1)
            pe.wait_ge(ns_kcr, 1)
            pe.wait_ge(ns_u.freed, 17)
            for t in range(TT):
                for hd in range(NSA_HEADS):
                    o = 64 * (hd % 2)
                    c = t * P + hd // 2 * CMP
                    r = mm(ps[:, 6 - hd % 2, c:c + CMP], ns_q[o:o + 64, hd // 2, t * P:(t + 1) * P],
                           ns_kc[o:o + 64, hd // 4, :], start=True, stop=True)
            r.then_inc(ns_cq, 1)
            pe.wait_ge(ns_cpr, 1)
            for i in range(4):
                r = nc.tensor.transpose(ps[:, 7, i * P:(i + 1) * P],
                                        ns_cs[:, i // 2, 8 * (i % 2):8 * (i % 2) + 8, :], ident)
            r.then_inc(ns_ct, 1)
            pe.wait_ge(ns_cc, 1)
            pe.wait_ge(ns_vr, 2)
            for i in range(4):
                mm(ps[:, i, :], ns_cp[:, i, :], ns_vbd[:, i % 2, :, :], start=True, stop=False, skip_group_check=True)

            def ns_qk_(it):
                br, pr = it // 8, it % 8
                if it == 0:
                    pe.wait_ge(ns_kdr, 2)
                    pe.wait_ge(ns_qrr, 4)
                else:
                    pe.wait_ge(ns_add, it)
                for i in range(2):
                    o = 64 * i
                    kd = ns_kd[o:o + 64, br, pr // 2, :]
                    q = ns_qr[o:o + 64, pr, :]
                    mm(ps[:, 4 + i, 0:P], q[:, 0:P], kd[:, 0:P], start=True, stop=True)
                    r = mm(ps[:, 4 + i, P:384], q[:, P:T], kd, start=True, stop=True)
                r.then_inc(ns_qk, 1)

            def ns_t_(it):
                pe.wait_ge(ns_pr, it + 1)
                for i in range(2):
                    for j in range(3):
                        r = nc.tensor.transpose(ps[:, 6 + i, j * P:(j + 1) * P],
                                                ns_s[:, it % 2, i, j * P:(j + 1) * P], ident)
                r.then_inc(ns_tp, 1)

            def ns_pv_(it):
                br, pr = it // 8, it % 8
                pe.wait_ge(ns_tc, it + 1)
                for i in range(2):
                    hd = 2 * pr + i
                    v = ns_v[:, :, br * 256 + (hd // 4) * 64:br * 256 + (hd // 4) * 64 + 64]
                    c = (hd % 8) * 64
                    p_ = ns_p[:, it % 2, i, :]
                    mm(ps[:, hd // 8, c:c + 64], p_[:, 0:P], v[:, 0, :], start=False, stop=br == 1,
                       skip_group_check=True)
                    mm(ps[:, 2 + hd // 8, c:c + 64], p_[:, P:T], v[:, 0, :], start=False, stop=False,
                       skip_group_check=True)
                    r = mm(ps[:, 2 + hd // 8, c:c + 64], p_[:, T:384], v[:, 1, :], start=False, stop=br == 1,
                           skip_group_check=True)
                return r

            ns_qk_(0)
            for it in range(16):
                if it + 1 < 16:
                    ns_qk_(it + 1)
                if it:
                    ns_pv_(it - 1)
                ns_t_(it)
            ns_pv_(15).then_inc(ns_o, 1)
            for t in range(TT):
                pe.wait_ge(ns_oc, 2 * t + 2)
                for k in range(KT):
                    r = nc.tensor.transpose(ps[:, 4 + k // 2, (k % 2) * T + t * P:(k % 2) * T + (t + 1) * P],
                                            ns_on[:, t, k * P:(k + 1) * P], ident)
                    if t == 1 and k % 2 == 1:
                        r.then_inc(ns_ot, 1)
            pe.wait_ge(ns_oa, 2)
            pe.wait_ge(ns_od, 2)
            for c in range(2):
                accumulate(Q_NSA + 7 + c, [ns_oT[:, 4 * c + k, :] for k in range(4)], c == 0, c == 1)
            norm(8)
            hidden(Q_FFN[1], FFN_C, 2, ffn_s[1][0], ffn_s[1][1])

        @block.scalar
        def _(act):
            A = nc.scalar.activation
            steps = [0]
            act.dma_start(sm[:, :], small).then_inc(loaded, 16)
            act.dma_start(cs[:, :], consts).then_inc(loaded, 16)
            act.wait_ge(loaded, 48)

            def link(ins):
                steps[0] += 1
                ins.then_inc(act_step, 1)
                act.wait_ge(act_step, steps[0])

            def sumsq(n):
                for t in range(TT):
                    if H_AT[n]:
                        act.wait_ge(h_ready, H_AT[n] - (2 if n != 5 else 1) * (1 - t))
                    A(xs[:, t, :], h[:, t, :], ACT.Square, accum_out=ssq[:, t:t + 1]).then_inc(ss_ready, 1)

            def norm(n):
                sumsq(n)
                i = TRANSPOSED.index(n)
                for b in (0, 2):
                    act.wait_ge(xt_done, 4 * i + b + 1)
                    for k in (2 * b, 2 * b + 1):
                        for dst, g in zip((xT, xT2), GAIN_OF[n]):
                            c = S_GAIN + g * KT + k
                            r = A(dst[:, k, :], ps[:, 4 + b, (k % 2) * T:(k % 2 + 1) * T], ACT.Copy,
                                  scale=sm[:, c:c + 1])
                    r.then_inc(xT_a, 1)

            def evac(u, q, dst, freed, func=ACT.Copy, scale=1.0, after=None, turn=None):
                if after is not None:
                    act.wait_ge(freed, after)
                act.wait_ge(half_done, (2 * q[0] + q[1] + 1) + (0 if turn is None else turn))
                A(dst, ps[:, bank(u), :], func, scale=scale).then_inc(freed, 1)

            def mlp(n):
                freed, ready = mlp_s[n]
                q0 = Q_MLP[n]

                def unit(u, turn=None):
                    q = q0 + pos_u(u // 2)
                    act.wait_ge(half_done, (2 * q + u % 2 + 1) + (0 if turn is None else turn * 8))
                    if u >= 2:
                        act.wait_ge(ready, (u - 1) + (0 if turn is None else turn * 4))
                    A(relu[:, u % 2, :], ps[:, bank(u), :], ACT.Relu).then_inc(freed, 1)

                for u in range(4):
                    unit(u)
                with act.Fori(0, (MLP_C - 2) // 2) as it:
                    for u in range(4, 8):
                        unit(u, it)

            def ffn(n):
                freed, ready, base, tap, sl = ffn_s[n]
                q0 = Q_FFN[n]
                col = S_CONV + n * FFN_TILES * 8

                def par(u, j, turn):
                    c = col + 8 * u + j
                    return sm[:, c:c + 1] if turn is None else sm[:, bass.ds(turn * 32 + c, 1)]

                def unit(u, turn=None):
                    q = q0 + pos_u(u // 2)
                    act.wait_ge(half_done, (2 * q + u % 2 + 1) + (0 if turn is None else turn * 8))
                    if u >= 2:
                        act.wait_ge(ready, (u - 1) + (0 if turn is None else turn * 4))
                    for g in range(2):
                        r = A(conv[:, u % 2, g, :], ps[:, bank(u), g * T:(g + 1) * T], ACT.Identity,
                              scale=par(u, 4 + g, turn), bias=par(u, 6 + g, turn))
                    r.then_inc(base, 1)
                    act.wait_ge(freed, (u + 1) + (0 if turn is None else turn * 4))
                    A(silu[:, u % 2, :], conv[:, u % 2, 0, :], ACT.Silu).then_inc(sl, 1)

                for u in range(4):
                    unit(u)
                with act.Fori(0, (FFN_C - 3) // 2) as it:
                    for u in range(4, 8):
                        unit(u, it)
                for u in range(FFN_TILES - 2, FFN_TILES):
                    unit(u)

            norm(0)
            for u in range(12):
                q = (Q_SB + u // 2, u % 2)
                if u < 4:
                    evac(u, q, sb_q[:, 2 * u:2 * u + 2, :], sb_u.freed, scale=0.125)
                elif u < 8:
                    evac(u, q, sb_k[:, 2 * u - 8:2 * u - 6, :], sb_u.freed)
                else:
                    c = (u - 8) // 2 * 512
                    evac(u, q, sb_v[:, u % 2, c:c + 512], sb_u.freed)

            def sb_soft(p):
                e = sb_e[:, p % 2, :, :]
                act.wait_ge(sbc, p + 1)
                A(e, e, ACT.Exp).then_inc(sbe, 1)
                act.wait_ge(sbe, p + 1)
                A(e, e, ACT.Ln, bias=1.0).then_inc(sbl, 1)

            sb_soft(0)
            sb_soft(1)
            for p in range(8):
                act.wait_ge(sbt, p + 1)
                b = 4 + 2 * (p % 2)
                A(sb_a[:, p % 2, :, :], ps[:, b:b + 2, 0:384], ACT.Exp).then_inc(sbx, 1)
                if p + 2 < 8:
                    sb_soft(p + 2)
            norm(1)
            mlp(0)
            norm(2)
            for u in range(8, 24):
                q = (Q_RET + u // 2, u % 2)
                c = (u // 2 % 4) * 512
                dst = (rt_v if u < 16 else rt_g)[:, u % 2, c:c + 512]
                evac(u, q, dst, rt_u.freed, func=ACT.Copy if u < 16 else ACT.Silu, after=8 if u == 8 else None)
            act.wait_ge(rt_rs, 1)
            for i in range(8):
                v = rt_g[:, i % 2, (i // 2) * 512:(i // 2 + 1) * 512]
                act.wait_ge(rt_of, i + 1)
                A(v, v, ACT.Copy, scale=rs8[:, i:i + 1]).then_inc(rt_yr, 1)
            for g in range(0, 8, 2):
                act.wait_ge(rt_tr, g + 1)
                A(rt_y[:, 2 * g:2 * g + 2, :], ps[:, bank(g), :], ACT.Copy).then_inc(rt_ya, 1)
            norm(3)
            mlp(1)
            sumsq(4)
            norm(5)
            for u in range(1, 5):
                dst = (gl_q if u < 3 else gl_k)[:, 2 * ((u - 1) % 2):2 * ((u - 1) % 2) + 2, :]
                evac(u, (Q_GLA + (u - 1) // 2, (u - 1) % 2), dst, gl_u.freed, scale=P ** -0.5 if u < 3 else 1.0,
                     after=1 if u == 1 else None)
            act.wait_ge(gl_x_r, 1)
            A(gl_l[:, :, :], gl_l[:, :, :], ACT.Exp).then_inc(gl_e, 1)
            act.wait_ge(gl_e, 1)
            A(gl_l[:, :, :], gl_l[:, :, :], ACT.Ln, bias=1.0).then_inc(gl_lg, 1)
            for j in range(8):
                w = gl_w[j][:, :, :]
                act.wait_ge(gl_df, j + 1)
                link(A(w, w, ACT.Abs))
                A(w, w, ACT.Exp, scale=-1.0 / 16.0).then_inc(gl_ex, 1)
                if j % 2 == 1:
                    u = 7 + j // 2
                    evac(u, (Q_GLA + 2 + (u - 7) // 2, (u - 7) % 2),
                         gl_v[:, (u - 7) % 2, (u - 7) // 2 * 512:(u - 7) // 2 * 512 + 512], gl_u.freed,
                         after=7 if u == 7 else None)
            for u in range(11, 15):
                c = (u - 11) // 2 * 512
                evac(u, (Q_GLA + 4 + (u - 11) // 2, (u - 11) % 2), gl_r[:, (u - 11) % 2, c:c + 512], gl_u.freed,
                     func=ACT.Silu)
            for t in range(TT):
                act.wait_ge(gl_o, t + 1)
                junk = (gl_c, gl_l)[t]
                for hd in range(GLA_HEADS):
                    r = A(junk[:, hd, :], ps[:, 4 + 2 * t + hd // 2, (hd % 2) * T:(hd % 2 + 1) * T], ACT.Square,
                          accum_out=ss8[:, 4 * t + hd:4 * t + hd + 1])
                r.then_inc(gl_s, 1)
            for b in (0, 2):
                act.wait_ge(gl_tr, b + 1)
                A(gl_y[:, 2 * b:2 * b + 2, :], ps[:, b, :], ACT.Copy).then_inc(gl_ya, 1)
            norm(6)
            ffn(0)
            norm(7)
            for u in range(2):
                act.wait_ge(half_done, 2 * Q_NSA + u + 1)
                for o in range(2):
                    src = ps[64 * o:64 * o + 64, bank(u), :].rearrange("p (a t) -> p a t", t=T)
                    A(ns_raw[0:64, u, o:o + 3:2, :], src, ACT.Copy)
                    r = A(ns_raw[64:128, u, o:o + 3:2, 0:T - 1], src[:, :, 1:T], ACT.Copy)
                r.then_inc(ns_u.freed, 1)
            for u in range(2, 4):
                evac(u, (Q_NSA + 1, u - 2), ns_k[:, u - 2, :, :], ns_u.freed)
            for i in range(2):
                act.wait_ge(half_done, 2 * (Q_NSA + 2 + i) + 2)
                x = ps[:, i, 0:128].rearrange("p (c n) -> p c n", n=64)[:, :, 0:60]
                A(ns_h[:, i, :, 0:60], x, ACT.Square).then_inc(ns_sq, 1)
                act.wait_ge(ns_u1, i + 1)
                A(ns_h[:, i, :, 0:60], ns_h[:, i, :, 0:60], ACT.Tanh, scale=0.7978845608028654).then_inc(ns_th, 1)
            for u in range(4, 6):
                evac(u, (Q_NSA + 4, u - 4), ns_v[:, u - 4, :], ns_u.freed)
            for u in range(6, 10):
                evac(u, (Q_NSA + 5 + (u - 6) // 2, (u - 6) % 2), ns_q[:, 2 * (u - 6):2 * (u - 6) + 2, :], ns_u.freed,
                     scale=0.125)
            act.wait_ge(ns_u.freed, 16)
            act.wait_ge(ns_pj, 7)
            A(ns_gate[:, :, :], ps[:, bank(16), 0:128].rearrange("p (t n) -> p t n", n=64)[:, :, 0:48],
              ACT.Sigmoid).then_inc(ns_u.freed, 1)
            act.wait_ge(ns_kv, 1)
            A(ns_kc[:, :, :], ps[:, 2, 0:64], ACT.Copy, scale=0.5).then_inc(ns_kcr, 1)
            act.wait_ge(ns_ci, 1)
            A(ns_cs[:, :, :, :], ns_cs[:, :, :, :], ACT.Exp).then_inc(ns_ce, 1)
            act.wait_ge(ns_ct, 1)
            A(ns_cp[:, :, :], ps[:, 7, :], ACT.Copy).then_inc(ns_cc, 1)

            def ns_exp(it):
                act.wait_ge(ns_mx, it + 1)
                for i in range(2):
                    for t in range(2):
                        v = ns_s[:, it % 2, i, P * t:P * t + P * (t + 1)]
                        r = A(v, v, ACT.Exp, bias=ns_m[:, it % 2, i, t:t + 1], accum_out=ns_l[:, it % 2, i, t:t + 1])
                r.then_inc(ns_ex, 1)

            ns_exp(0)
            for it in range(16):
                if it + 1 < 16:
                    ns_exp(it + 1)
                act.wait_ge(ns_tp, it + 1)
                A(ns_p[:, it % 2, :, :], ps[:, 6:8, 0:384], ACT.Copy).then_inc(ns_tc, 1)
            for b in (0, 2):
                act.wait_ge(ns_ot, b + 1)
                A(ns_oT[:, 2 * b:2 * b + 2, :], ps[:, 4 + b, :], ACT.Copy).then_inc(ns_oa, 1)
            norm(8)
            ffn(1)
            sumsq(9)

        @block.vector
        def _(dve):
            V = nc.vector
            steps = [0]

            def link(ins):
                steps[0] += 1
                ins.then_inc(dve_step, 1)
                dve.wait_ge(dve_step, steps[0])

            dve.wait_ge(loaded, 48)

            def mean_square(n):
                dve.wait_ge(ss_ready, 2 * n + 2)
                V.tensor_scalar(msq, ssq, 1.0 / D, EPS, ALU.mult, ALU.add).then_inc(ms_ready, 1)
                dve.wait_ge(rstd_ready, n + 1)

            def norm(n):
                i = TRANSPOSED.index(n)
                mean_square(n)
                for t in range(TT):
                    V.tensor_scalar(xs[:, t, :], h[:, t, :], rstd[:, t:t + 1], None, ALU.mult).then_inc(xs_ready, 1)
                for b in (1, 3):
                    dve.wait_ge(xt_done, 4 * i + b + 1)
                    for k in (2 * b, 2 * b + 1):
                        for dst, g in zip((xT, xT2), GAIN_OF[n]):
                            c = S_GAIN + g * KT + k
                            r = V.tensor_scalar(dst[:, k, :], ps[:, 4 + b, (k % 2) * T:(k % 2 + 1) * T],
                                                sm[:, c:c + 1], None, ALU.mult)
                    r.then_inc(xT_d, 1)

            def natural_norm(n, row, dst, ready):
                dve.wait_ge(rows_in, 16)
                mean_square(n)
                for t in range(TT):
                    V.scalar_tensor_tensor(dst[:, t, :], h[:, t, :], rstd[:, t:t + 1], rowg[:, row, :],
                                           ALU.mult, ALU.mult).then_inc(ready, 1)

            def residual(q):
                dve.wait_ge(half_done, 2 * q + 2)
                for j in range(4):
                    v = h[:, j // 2, (j % 2) * 512:(j % 2 + 1) * 512]
                    V.tensor_tensor(v, ps[:, j, :], v, ALU.add).then_inc(h_ready, 1)

            def mlp(n):
                freed, ready = mlp_s[n]

                def unit(u, turn=None):
                    dve.wait_ge(freed, (u + 1) + (0 if turn is None else turn * 4))
                    v = relu[:, u % 2, :]
                    d = hT[:, (u // 2) % 2, 2 * (u % 2):2 * (u % 2) + 2, :]
                    V.tensor_tensor(d, v.rearrange("p (a t) -> p a t", t=T), v.rearrange("p (a t) -> p a t", t=T),
                                    ALU.mult).then_inc(ready, 1)

                for u in range(4):
                    unit(u)
                with dve.Fori(0, (MLP_C - 2) // 2) as it:
                    for u in range(4, 8):
                        unit(u, it)

            def ffn(n):
                freed, ready, base, tap, sl = ffn_s[n]
                col = S_CONV + n * FFN_TILES * 8

                def par(u, j, turn):
                    c = col + 8 * u + j
                    return sm[:, c:c + 1] if turn is None else sm[:, bass.ds(turn * 32 + c, 1)]

                def unit(u, turn=None):
                    add = 0 if turn is None else turn * 4
                    dve.wait_ge(base, (u + 1) + add)
                    for g in range(2):
                        c = conv[:, u % 2, g, 1:T]
                        V.scalar_tensor_tensor(c, ps[:, bank(u), g * T:(g + 1) * T - 1], par(u, 2 + g, turn), c,
                                               ALU.mult, ALU.add).then_inc(tap, 1)
                    dve.wait_ge(tap, (2 * u + 2) + (0 if turn is None else turn * 8))
                    for g in range(2):
                        c = conv[:, u % 2, g, 2:T]
                        r = V.scalar_tensor_tensor(c, ps[:, bank(u), g * T:(g + 1) * T - 2], par(u, g, turn), c,
                                                   ALU.mult, ALU.add)
                    r.then_inc(freed, 1)
                    dve.wait_ge(sl, (u + 1) + add)
                    V.tensor_tensor(hT[:, (u // 2) % 2, u % 2, :], silu[:, u % 2, :], conv[:, u % 2, 1, :],
                                    ALU.mult).then_inc(ready, 1)

                for u in range(4):
                    unit(u)
                with dve.Fori(0, (FFN_C - 3) // 2) as it:
                    for u in range(4, 8):
                        unit(u, it)
                for u in range(FFN_TILES - 2, FFN_TILES):
                    unit(u)

            norm(0)

            def banks(p):
                b = 4 + 2 * (p % 2)
                return ps[:, b:b + 2, 0:384]

            def clip(p):
                dve.wait_ge(sbz, p + 1)
                V.tensor_scalar(sb_e[:, p % 2, :, :], banks(p), SOFT_CAP, None, ALU.min).then_inc(sbc, 1)

            def softplus(p):
                dve.wait_ge(sbl, p + 1)
                V.tensor_tensor(sb_s[:, p % 2, :, :], banks(p), sb_e[:, p % 2, :, :], ALU.max).then_inc(sbm, 1)

            def out_copy(p):
                dve.wait_ge(sbo, p + 1)
                V.tensor_copy(sb_o[:, p, :], ps[:, p % 2, 0:T]).then_inc(sbv, 1)

            clip(0)
            clip(1)
            softplus(0)
            for p in range(8):
                if p + 1 < 8:
                    softplus(p + 1)
                if p:
                    out_copy(p - 1)
                if p + 2 < 8:
                    clip(p + 2)
            out_copy(7)
            residual(Q_SB + 7)
            norm(1)
            mlp(0)
            residual(Q_MLP[0] + 15)
            norm(2)
            cos = cs[:, C_COS:C_COS + T].unsqueeze(1).broadcast_to([P, 2, T])
            sin = cs[:, C_SIN:C_SIN + T].unsqueeze(1).broadcast_to([P, 2, T])
            for u in range(8):
                dve.wait_ge(half_done, 2 * (Q_RET + u // 2) + u % 2 + 1)
                if u >= 2:
                    dve.wait_ge(rt_qk, u - 1)
                src = ps[:, bank(u), :].rearrange("p (a t) -> p a t", t=T)
                V.tensor_tensor(rt_c[:, u % 2, :].rearrange("p (a t) -> p a t", t=T), src, cos, ALU.mult)
                V.tensor_tensor(rt_n[:, u % 2, :].rearrange("p (a t) -> p a t", t=T), src, sin, ALU.mult)\
                 .then_inc(rt_u.freed, 1)
            for hd in range(RET_HEADS):
                dve.wait_ge(rt_sc, hd + 1)
                c = C_DECAY + 384 * hd
                V.tensor_tensor(rt_s[:, hd, :], ps[:, 4 + hd, 0:384], cs[:, c:c + 384], ALU.mult).then_inc(rt_dec, 1)
            for i in range(8):
                dve.wait_ge(rt_o, i + 1)
                link(V.bn_stats(bn[:, i, :], ps[:, i % 4, :]))
                link(V.bn_aggr(mv[:, i, :], bn[:, i, :]))
                v = rt_g[:, i % 2, (i // 2) * 512:(i // 2 + 1) * 512]
                V.scalar_tensor_tensor(v, ps[:, i % 4, :], mv[:, i, 0:1], v, ALU.subtract, ALU.mult).then_inc(rt_of, 1)
            V.tensor_scalar(ms8, mv[:, :, 1], EPS, None, ALU.add).then_inc(rt_ms, 1)
            for g in range(1, 8, 2):
                dve.wait_ge(rt_tr, g + 1)
                V.tensor_copy(rt_y[:, 2 * g:2 * g + 2, :], ps[:, bank(g), :].rearrange("p (a t) -> p a t", t=T))\
                 .then_inc(rt_yd, 1)
            residual(Q_RET + 15)
            norm(3)
            mlp(1)
            residual(Q_MLP[1] + 15)
            natural_norm(4, 0, h, h_ready)
            norm(5)
            dve.wait_ge(gl_pj, 1)
            V.tensor_copy(gl_low, ps[0:16, 4, 0:T]).then_inc(gl_u.freed, 1)
            for t in range(TT):
                V.memset(gl_a[t][:, :, :], 0.0)
            for i in range(2):
                dve.wait_ge(gl_pj, 2 + i)
                if i == 0:
                    dve.wait_ge(gl_u.freed, 5)
                for j in range(2):
                    c = 2 * i + j
                    r = V.tensor_scalar(gl_x[:, c, :], ps[:, bank(5 + i), j * T:(j + 1) * T],
                                        sm[:, S_BALPHA + c:S_BALPHA + c + 1], -1.0, ALU.add, ALU.mult)
                r.then_inc(gl_u.freed, 1)
            dve.wait_ge(gl_u.freed, 7)
            V.tensor_scalar(gl_l[:, :, :], gl_x[:, :, :], SOFT_CAP, None, ALU.min).then_inc(gl_x_r, 1)
            dve.wait_ge(gl_lg, 1)
            link(V.tensor_tensor(gl_x[:, :, :], gl_x[:, :, :], gl_l[:, :, :], ALU.max))
            link(V.memset(gl_l[:, :, :], 0.0))
            for hd in range(GLA_HEADS):
                r = V.tensor_tensor_scan(gl_c[:, hd, :], gl_x[:, hd, :], gl_l[:, hd, :], 0.0, ALU.add, ALU.add)
            link(r)
            flat = gl_c[:, :, :].rearrange("p a t -> p (a t)")

            def level(v, j):
                n = 2 << j
                return v.rearrange("p a t -> p (a t)").rearrange("p (b n) -> p b n", n=n)

            for j in range(8):
                n = 2 << j
                c = flat.rearrange("p (b n) -> p b n", n=n)
                V.tensor_tensor(level(gl_w[j], j), c, c[:, :, n // 2 - 1:n // 2].broadcast_to([P, 4 * T // n, n]),
                                ALU.subtract).then_inc(gl_df, 1)
            for j in range(8):
                n = 2 << j
                dve.wait_ge(gl_ex, j + 1)
                w = level(gl_w[j], j)
                V.tensor_tensor(w[:, :, 0:n // 2], w[:, :, 0:n // 2], level(gl_k, j)[:, :, 0:n // 2], ALU.mult)
                V.tensor_tensor(w[:, :, n // 2:n], w[:, :, n // 2:n], level(gl_q, j)[:, :, n // 2:n],
                                ALU.mult).then_inc(gl_wr, 1)
            for i in range(16):
                l, t = i // 2, i % 2
                dve.wait_ge(gl_lv, i + 1)
                if i >= 2:
                    dve.wait_ge(gl_cp, i - 1)
                m = cs[:, C_LEVEL + l * P:C_LEVEL + (l + 1) * P].bitcast(I32).unsqueeze(1).broadcast_to([P, 4, P])
                V.copy_predicated(gl_a[t][:, :, :], m, ps[:, i % 4, :].rearrange("p (a t) -> p a t", t=P))\
                 .then_inc(gl_cp, 1)
            dve.wait_ge(gl_lv, 17)
            V.tensor_copy(gl_across, ps[:, 0, :].rearrange("p (a t) -> p a t", t=P)).then_inc(gl_cp, 1)
            dve.wait_ge(gl_s, 2)
            V.tensor_scalar(ms8, ss8, 1.0 / 256, EPS, ALU.mult, ALU.add).then_inc(gl_m, 1)
            dve.wait_ge(gl_p, 1)
            for t in range(TT):
                dve.wait_ge(gl_rg, t + 1)
                for hd in range(GLA_HEADS):
                    v = gl_r[:, t, hd * 256:(hd + 1) * 256]
                    r = V.scalar_tensor_tensor(v, ps[:, 4 + 2 * t + hd // 2, (hd % 2) * T:(hd % 2 + 1) * T],
                                               rs8[:, 4 * t + hd:4 * t + hd + 1], v, ALU.mult, ALU.mult)
                r.then_inc(gl_yr, 1)
            for b in (1, 3):
                dve.wait_ge(gl_tr, b + 1)
                V.tensor_copy(gl_y[:, 2 * b:2 * b + 2, :], ps[:, b, :].rearrange("p (a t) -> p a t", t=T))\
                 .then_inc(gl_yd, 1)
            residual(Q_GLA + 7)
            norm(6)
            ffn(0)
            residual(Q_FFN[0] + 21)
            norm(7)
            link(V.memset(ns_h[:, 2:4, :, :], 0.0))
            for i in range(2):
                dve.wait_ge(ns_u.freed, i + 1)
                for l in range(16):
                    o = ns_x[:, i, l, :].rearrange("p (a n) -> p a n", n=15)
                    pe_ = sm[:, S_PE + 16 * i + l:S_PE + 16 * i + l + 1]
                    r = V.tensor_scalar(o, ns_raw[:, i, :, 2 * l:2 * l + 16 * 14 + 1:16], pe_, None, ALU.add)
                r.then_inc(ns_xr, 1)
            for i in range(2):
                x = ps[:, i, 0:128].rearrange("p (c n) -> p c n", n=64)[:, :, 0:60]
                a = ns_h[:, i, :, 0:60]
                dve.wait_ge(ns_sq, i + 1)
                link(V.tensor_scalar(a, a, 0.044715, 1.0, ALU.mult, ALU.add))
                V.tensor_tensor(a, x, a, ALU.mult).then_inc(ns_u1, 1)
                dve.wait_ge(ns_th, i + 1)
                o = ns_h[:, 2 + i, :, :].rearrange("p c (a n) -> p c a n", n=CMP)
                for c in range(2):
                    r = V.scalar_tensor_tensor(o[:, c, :, 0:15], ns_h[:, i, c, 0:60].rearrange("p (a n) -> p a n", n=15),
                                               1.0, ps[:, i, c * 64:c * 64 + 60].rearrange("p (a n) -> p a n", n=15),
                                               ALU.add, ALU.mult)
                r.then_inc(ns_hr, 1)
            dve.wait_ge(ns_hr, 2)
            for g in range(2):
                for c in range(2):
                    src = ns_h[:, 3, c, :].rearrange("p (a n) -> p a n", n=CMP)[:, 2 * g:2 * g + 2, :]
                    dst = ns_hv[:, g, c, :].rearrange("p (a b n) -> p a b n", b=4, n=CMP)
                    r = V.tensor_copy(dst, src.unsqueeze(2).broadcast_to([P, 2, 4, CMP]))
            r.then_inc(ns_hr, 1)
            rcos = cs[:, C_RCOS:C_RCOS + T].unsqueeze(1).broadcast_to([P, 2, T])
            rsin = cs[:, C_RSIN:C_RSIN + T].unsqueeze(1).broadcast_to([P, 2, T])
            dve.wait_ge(ns_u.freed, 10)
            for i in range(6):
                raw = ns_k[:, i, :, :] if i < 2 else ns_q[:, 2 * (i - 2):2 * (i - 2) + 2, :]
                link(V.tensor_tensor(ns_t1[:, :, :], raw, rcos, ALU.mult))
                dve.wait_ge(ns_pj, i + 1)
                V.tensor_tensor(ns_t2[:, :, :], ps[:, bank(10 + i), :].rearrange("p (a t) -> p a t", t=T), rsin,
                                ALU.mult).then_inc(ns_u.freed, 1)
                dve.wait_ge(ns_u.freed, 11 + i)
                if i < 2:
                    for o in range(2):
                        for d in range(2):
                            r = V.tensor_tensor(ns_kd[64 * d:64 * d + 64, i, o:o + 3:2, :],
                                                ns_t1[64 * o:64 * o + 64, :, :], ns_t2[64 * o:64 * o + 64, :, :], ALU.add)
                    r.then_inc(ns_kdr, 1)
                    dve.wait_ge(ns_kdr, i + 1)
                else:
                    V.tensor_tensor(ns_qr[:, 2 * (i - 2):2 * (i - 2) + 2, :], ns_t1[:, :, :], ns_t2[:, :, :],
                                    ALU.add).then_inc(ns_qrr, 1)
                    dve.wait_ge(ns_qrr, i - 1)
            dve.wait_ge(ns_kv, 2)
            for g in range(2):
                V.tensor_tensor(ns_vbd[:, g, :, :], ps[:, 3, g * 64:(g + 1) * 64].unsqueeze(1).broadcast_to([P, 8, 64]),
                                cs[:, C_BD:C_BD + 8].unsqueeze(2).broadcast_to([P, 8, 64]), ALU.mult).then_inc(ns_vr, 1)
            dve.wait_ge(ns_cq, 1)
            c3 = ns_cs[:, :, :, :].rearrange("p t h n -> p (t h) n")

            def cmask(c, t):
                return cs[:, c + t * CMP:c + (t + 1) * CMP].unsqueeze(1)

            for t in range(TT):
                for o in range(2):
                    r = V.tensor_tensor(ns_cs[:, t, o:16:2, :],
                                        ps[:, 6 - o, t * P:(t + 1) * P].rearrange("p (h n) -> p h n", n=CMP),
                                        cmask(C_CADD, t).broadcast_to([P, 8, CMP]), ALU.add)
            link(r)
            cm = ns_cm[:, :, :].rearrange("p t h -> p (t h)")
            cl = ns_cl[:, :, :].rearrange("p t h -> p (t h)")
            link(V.tensor_reduce(cm, c3, AX.X, ALU.max))
            V.tensor_tensor(c3, c3, cm.unsqueeze(2).broadcast_to([P, 32, CMP]), ALU.subtract).then_inc(ns_ci, 1)
            dve.wait_ge(ns_ce, 1)
            link(V.tensor_reduce(cl, c3, AX.X, ALU.add))
            link(V.reciprocal(cl, cl))
            link(V.tensor_tensor(ns_cl[:, :, :], ns_cl[:, :, :], ns_gate[:, :, 0:16], ALU.mult))
            for t in range(TT):
                r = V.tensor_tensor(ns_cs[:, t, :, :], ns_cs[:, t, :, :], cmask(C_CMUL, t).broadcast_to([P, 16, CMP]),
                                    ALU.mult)
            link(r)
            V.tensor_tensor(c3, c3, cl.unsqueeze(2).broadcast_to([P, 32, CMP]), ALU.mult).then_inc(ns_cpr, 1)

            def ns_scores(it):
                dve.wait_ge(ns_qk, it + 1)
                if it >= 2:
                    dve.wait_ge(ns_tp, it - 1)
                s = ns_s[:, it % 2, :, :]
                V.tensor_tensor(s, ps[:, 4:6, 0:384],
                                cs[:, C_CAUSAL:C_CAUSAL + 384].unsqueeze(1).broadcast_to([P, 2, 384]), ALU.add)\
                 .then_inc(ns_add, 1)
                dve.wait_ge(ns_add, it + 1)
                for t in range(2):
                    r = V.tensor_reduce(ns_m[:, it % 2, :, t], s[:, :, P * t:P * t + P * (t + 1)], AX.X, ALU.max,
                                        negate=True)
                r.then_inc(ns_mx, 1)

            ns_scores(0)
            for it in range(16):
                if it + 1 < 16:
                    ns_scores(it + 1)
                dve.wait_ge(ns_ex, it + 1)
                l, f = ns_l[:, it % 2, :, :], ns_f[:, it % 2, :, :]
                link(V.reciprocal(f, l))
                br, pr = it // 8, it % 8
                g = ns_gate[:, :, 16 * (br + 1) + 2 * pr:16 * (br + 1) + 2 * pr + 2].rearrange("p t h -> p h t")
                V.tensor_tensor(f, f, g, ALU.mult).then_inc(ns_co, 1)
            dve.wait_ge(ns_o, 1)
            for j in range(4):
                V.tensor_copy(ns_on[:, j // 2, (j % 2) * 512:(j % 2 + 1) * 512], ps[:, j, :]).then_inc(ns_oc, 1)
            for b in (1, 3):
                dve.wait_ge(ns_ot, b + 1)
                V.tensor_copy(ns_oT[:, 2 * b:2 * b + 2, :], ps[:, 4 + b, :].rearrange("p (a t) -> p a t", t=T))\
                 .then_inc(ns_od, 1)
            residual(Q_NSA + 8)
            norm(8)
            ffn(1)
            residual(Q_FFN[1] + 21)
            natural_norm(9, 2, xs, xs_ready)


def constants():
    f = np.float32
    c = np.zeros((P, C_TOTAL), f)
    i = np.arange(P)
    c[:, C_ID:C_ID + P] = np.eye(P)
    c[:, C_NTRI:C_NTRI + P] = np.where(i[:, None] >= i[None, :], -1.0, 0.0)
    c[:, C_NONE:C_NONE + P] = -1.0
    pos = np.arange(T, dtype=f)
    inv = (f(1.0) / (f(10000.0) ** np.linspace(0.0, 1.0, P, dtype=f))).astype(f)
    ang = (inv[:, None] * pos[None, :]).astype(f)
    c[:, C_COS:C_COS + T], c[:, C_SIN:C_SIN + T] = np.cos(ang), np.sin(ang)
    lg = np.log1p(-np.exp2(-5.0 - np.arange(RET_HEADS)))
    for hd in range(RET_HEADS):
        for n, (s0, t0, w) in enumerate(((0, 0, T), (P, P, P))):
            rel = (t0 + np.arange(w))[None, :] - (s0 + i)[:, None]
            dec = np.where(rel >= 0, np.exp(lg[hd] * np.maximum(rel, 0)), 0.0) * 256 ** -0.5
            o = C_DECAY + 384 * hd + n * T
            c[:, o:o + w] = dec
    inv = (f(10000.0) ** (-np.arange(32, dtype=f) / f(32))).astype(f)
    ang = (inv[i % 32][:, None] * pos[None, :]).astype(f)
    c[:, C_RCOS:C_RCOS + T] = np.cos(ang)
    c[:, C_RSIN:C_RSIN + T] = np.sin(ang) * np.where(i % 64 < 32, -1.0, 1.0)[:, None]
    partner = np.where(i % 64 < 32, i + 32, i - 32)
    c[partner, C_SWAP + i] = 1.0
    causal = np.where(i[None, :] <= i[:, None], 0.0, NEG)
    c[:, C_CAUSAL:C_CAUSAL + P] = causal
    c[:, C_CAUSAL + T:C_CAUSAL + 384] = causal
    n = np.arange(CMP)
    for t in range(TT):
        ok = (n[None, :] * 16 + 31 <= (t * P + i)[:, None]) & (n[None, :] < CMP - 1)
        c[:, C_CADD + t * CMP:C_CADD + (t + 1) * CMP] = np.where(ok, 0.0, NEG)
        c[:, C_CMUL + t * CMP:C_CMUL + (t + 1) * CMP] = ok
    c[:, C_BD:C_BD + 8] = 0.5 * (i[:, None] // CMP == np.arange(8)[None, :])
    c[:, C_LEVEL:C_LEVEL + P] = np.eye(P)
    for l in range(1, 8):
        m = 1 << l
        same = i[:, None] // m == i[None, :] // m
        c[:, C_LEVEL + l * P:C_LEVEL + (l + 1) * P] = same & (i[:, None] % m < m // 2) & (i[None, :] % m >= m // 2)
    return c


def kernel(**inputs):
    import concourse.bacc as bacc
    from concourse.bass_utils import run_bass_kernel_spmd

    a = {k: np.asarray(v) for k, v in inputs.items()}

    def cols(w, c):
        return w[:, c].reshape(KT, P, 512).transpose(1, 0, 2).reshape(P, CH)

    def rows_(w, r, n=4):
        return w[r:r + n * P].reshape(n, P, D).transpose(1, 0, 2).reshape(P, n * D)

    ws, wd = [], []

    def all_cols(w, c0, n):
        ws.extend(cols(w, slice(c0 + 512 * j, c0 + 512 * (j + 1))) for j in range(n))

    def all_rows(w):
        ws.extend(rows_(w, r) for r in range(0, w.shape[0], 512))

    def mlp(n):
        up = [cols(a["w_mlp_up"][n], slice(512 * j, 512 * (j + 1))) for j in range(MLP_C)]
        down = [rows_(a["w_mlp_down"][n], 512 * j) for j in range(MLP_C)]
        ws.append(up[0])
        for j in range(1, MLP_C):
            ws.extend((up[j], down[j - 1]))
        ws.append(down[-1])

    def ffn(n):
        w, f = a["ffn_w_up_2"][n], FFN_TILES * P
        for j in range(FFN_C):
            ix = np.concatenate([s * f + (2 * j + e) * P + np.arange(P) for e in range(2) for s in range(2)])
            ws.append(cols(w, ix))
            wd.append(rows_(a["ffn_w_down_2"][n], 2 * P * j, 2))

    all_cols(a["w_sb_in"][0], 0, 6)
    all_rows(a["w_sb_out"][0])
    mlp(0)
    all_cols(a["w_ret_in"][0], 0, 12)
    all_rows(a["w_ret_out"][0])
    mlp(1)
    all_cols(a["gla_w_in_2"][0], 0, 6)
    all_rows(a["gla_w_o_2"][0])
    ffn(0)
    kv, win = a["nsa_w_kv_2"], a["nsa_w_in_2"][0]
    t256 = lambda j: kv[:, 256 * j:256 * (j + 1)]
    for x, y in ((0, 1), (2, 4)):
        ws.append(cols(np.concatenate([t256(x), t256(y)], 1), slice(0, 512)))
    for w in (a["cmp_k_w1_2"], a["cmp_v_w1_2"]):
        ws.append(w.reshape(16, P, 256).transpose(1, 0, 2).reshape(P, CH))
    ws.append(cols(np.concatenate([t256(3), t256(5)], 1), slice(0, 512)))
    all_cols(win, 0, 2)
    all_rows(a["nsa_w_o_2"][0])
    ffn(1)
    ws, wd = np.stack(ws), np.stack(wd)

    small = np.zeros((P, S_TOTAL), np.float32)
    for g, v in enumerate((a["g_mix"][0], a["g_mlp"][0], a["g_mix"][1], a["g_mlp"][1], a["norm_mix_2"][0],
                           a["norm_ffn_2"][0], a["kv_norm_2"], a["norm_mix_2"][1], a["norm_ffn_2"][1])):
        small[:, S_GAIN + g * KT:S_GAIN + (g + 1) * KT] = v.reshape(KT, P).T
    for n in range(2):
        taps = np.concatenate([a["ffn_conv_w_2"][n], a["ffn_conv_b_2"][n][None]], 0)
        v = taps.reshape(4, 2, FFN_TILES, P).transpose(3, 2, 0, 1).reshape(P, FFN_TILES * 8)
        small[:, S_CONV + n * FFN_TILES * 8:S_CONV + (n + 1) * FFN_TILES * 8] = v
    small[:, S_BALPHA:S_BALPHA + 4] = a["gla_b_alpha_2"][0].reshape(4, P).T
    small[:, S_WALOW:S_WGATE] = a["gla_w_in_2"][0][:, 3072:3088].reshape(KT, P, 16).transpose(1, 0, 2).reshape(P, -1)
    small[:, S_WGATE:S_W2K] = win[:, D:D + 48].reshape(KT, P, 48).transpose(1, 0, 2).reshape(P, -1)
    w2 = a["cmp_k_w2_2"].reshape(2, P, 64).transpose(1, 0, 2)
    small[:, S_W2K:S_W2V] = np.concatenate([w2, w2], 2).reshape(P, -1)
    small[:, S_W2V:S_PE] = a["cmp_v_w2_2"].reshape(2, P, 64).transpose(1, 0, 2).reshape(P, -1)
    small[:, S_PE:S_PE + 16] = a["cmp_pe_k_2"].reshape(16, P).T
    small[:, S_PE + 16:S_PE + 32] = a["cmp_pe_v_2"].reshape(16, P).T
    small[0:16, S_ALPHA:] = a["gla_w_alpha_up_2"][0]
    rows = np.stack([a["g_final"], a["gla_norm_2"][0].reshape(D), a["norm_final_2"]])

    arrays = {"ws": ws, "wd": wd, "small": small, "consts": constants(), "rows": rows,
              "x": np.ascontiguousarray(a["x"][0])}
    nc = bacc.Bacc("TRN2", target_bir_lowering=False, num_devices=1)
    aps = {k: nc.dram_tensor(k, v.shape, mybir.dt.from_np(v.dtype), kind="ExternalInput").ap()
           for k, v in arrays.items()}
    out = nc.dram_tensor("out", (T, D), F32, kind="ExternalOutput").ap()
    build(nc, aps["ws"], aps["wd"], aps["small"], aps["consts"], aps["rows"], aps["x"], out)
    r = run_bass_kernel_spmd(nc, [arrays], core_ids=[0])
    return r.results[0]["out"].reshape(1, T, D)
```

```python
import numpy as np
import concourse.bass as bass
from concourse import mybir

F32 = mybir.dt.float32
F32R = mybir.dt.float32r
I32 = mybir.dt.int32
ALU = mybir.AluOpType
ACT = mybir.ActivationFunctionType
AX = mybir.AxisListType

T = 256
D = 1024
P = 128
TT = T // P
KT = D // P
PIECE = 2048
RING = 3
EPS = 1e-6
NEG = -1e30
SB_HEADS, RET_HEADS, GLA_HEADS, NSA_HEADS, NSA_KV = 16, 4, 4, 16, 4
MLP_C = 4 * D // 512
FFN_TILES = 2816 // P
FFN_C = FFN_TILES // 2
CMP = 16
SOFT_CAP = 30.0

GAINS = 9
S_GAIN = 0
S_CONV = S_GAIN + GAINS * KT
S_BALPHA = S_CONV + 2 * FFN_TILES * 8
S_W2K = S_BALPHA + 4
S_W2V = S_W2K + 2 * P
S_PE = S_W2V + 2 * 64
S_ALPHA = S_PE + 2 * 16
S_ID = S_ALPHA + 512
S_TOTAL = S_ID + P
N_LOW = KT * 16
N_GATE = KT * 48

TAB = 1100
C_NTRI, C_NONE = 0, P
C_COS, C_SIN = 0, T
C_LEVEL = 0
C_RCOS, C_RSIN, C_SWAP, C_CAUSAL = 0, T, 2 * T, 2 * T + P
C_CADD = C_CAUSAL + 384
C_CMUL = C_CADD + TT * CMP
C_BD = C_CMUL + TT * CMP
DECAY = RET_HEADS * 384

G_SB = 0
G_MLP = (16, 80)
G_RET = 48
G_GLA = 112
G_FFN = (128, 179)
G_NSA = 161
G_END = 212
ARENA = 17408


def build(nc, ws, small, narrow, tables, decay, rows, x_in, out):
    from contextlib import ExitStack
    ctx = ExitStack()
    with ctx:
        def sb(name, shape, dt=F32):
            return ctx.enter_context(nc.sbuf_tensor(name, shape, dt))

        def sem(name):
            return ctx.enter_context(nc.semaphore(name))

        ring = sb("ring", [P, RING, PIECE])
        w_hi, w_lo = sb("w_hi", [P, RING, PIECE], F32R), sb("w_lo", [P, RING, PIECE], F32R)
        h = sb("h", [P, TT, D])
        x_hi, x_lo = sb("x_hi", [P, KT, T], F32R), sb("x_lo", [P, KT, T], F32R)
        y_hi, y_lo = sb("y_hi", [P, 12, T], F32R), sb("y_lo", [P, 12, T], F32R)
        n_hi, n_lo = sb("n_hi", [P, N_LOW + N_GATE], F32R), sb("n_lo", [P, N_LOW + N_GATE], F32R)
        sm = sb("sm", [P, S_TOTAL])
        tab = sb("tab", [P, TAB])
        rowg = sb("rowg", [P, D])
        stat = sb("stat", [P, 96])
        power = sb("power", [P, 16])
        arena = sb("arena", [P, ARENA])
        ps = ctx.enter_context(nc.psum_tensor("ps", [P, 8, 512], F32))

        ident = sm[:, S_ID:S_ID + P]
        ssq, msq, rstd = stat[:, 0:2], stat[:, 2:4], stat[:, 4:6]
        ss8, ms8, rs8 = stat[:, 8:16], stat[:, 16:24], stat[:, 24:32]
        mv = stat[:, 32:48].rearrange("p (i c) -> p i c", c=2)
        bn = stat[:, 48:96].rearrange("p (i c) -> p i c", c=6)

        def region(at, *dims):
            n = int(np.prod(dims))
            assert at + n <= ARENA, (at, n)
            v = arena[:, at:at + n]
            if len(dims) == 2:
                v = v.rearrange("p (a b) -> p a b", b=dims[1])
            if len(dims) == 3:
                v = v.rearrange("p (a b c) -> p a b c", b=dims[1], c=dims[2])
            return v

        xs = region(0, TT, D)
        narrow_raw = region(2048, N_LOW + N_GATE)
        relu, square = region(2048, 2, 512), region(5120, 2, 512)
        conv = region(3072, 2, 2, T)
        silu, prod = region(4096, 2, T), region(4608, 2, T)
        sb_q, sb_k, sb_v = region(0, KT, T), region(2048, KT, T), region(4096, TT, D)
        sb_e, sb_s, sb_a = region(8192, 2, 2, 384), region(9728, 2, 2, 384), region(11264, 2, 2, 384)
        rt_q, rt_k = region(0, KT, T), region(2048, KT, T)
        rt_v, rt_g = region(4096, TT, 2 * D), region(8192, TT, 2 * D)
        rt_s = region(12288, RET_HEADS, 384)
        rt_c, rt_n = region(13824, 2, 512), region(14848, 2, 512)
        rt_decay = region(15872, DECAY)
        gl_q, gl_k = region(0, 4, T), region(1024, 4, T)
        gl_v, gl_r = region(2048, TT, D), region(4096, TT, D)
        gl_c, gl_x, gl_l = region(6144, 4, T), region(7168, 4, T), region(8192, 4, T)
        gl_w = [region(9216 + 1024 * j, 4, T) for j in range(8)]
        gl_a = [region(8192, 4, P), region(8192 + 512, 4, P)]
        gl_nat = region(9216, TT, 16)
        gl_across = gl_x[:, 0:2, :].rearrange("p a (b c) -> p (a b) c", c=P)
        gl_low = gl_l[0:16, 0, :]
        ns_raw = region(2048, 2, NSA_KV, T)
        ns_x = region(4096, 2, 16, 60)
        ns_t2 = region(4096, 2, T)
        ns_s = region(4096, 2, 2, 384)
        ns_h = region(6016, 4, 2, 64)
        ns_hv = region(6528, 2, 2, P)
        ns_kc = region(7040, NSA_KV, CMP)
        ns_gate = region(7104, TT, 48)
        ns_m = region(7200, 2, 2, 2)
        ns_l = region(7208, 2, 2, 2)
        ns_f = region(7216, 2, 2, 2)
        ns_cm, ns_cl = region(7232, TT, 16), region(7264, TT, 16)
        ns_vbd = region(7296, 2, 8, 64)
        ns_kd = region(8320, 2, NSA_KV, T)
        ns_v = region(10368, TT, 512)
        ns_q, ns_qr = region(11392, KT, T), region(13440, KT, T)
        ns_k, ns_t1 = region(15488, 2, 2, T), region(16512, 2, T)
        ns_p = region(15488, 2, 2, 384)
        ns_cs, ns_cp = region(15488, TT, 16, CMP), region(16000, 4, P)
        ns_on = region(2048, TT, D)
        ns_xh = y_hi[:, 0:8, :].rearrange("p a t -> p (a t)")[:, 0:1920].rearrange("p (i l n) -> p i l n", i=2, n=60)
        ns_xl = y_lo[:, 0:8, :].rearrange("p a t -> p (a t)")[:, 0:1920].rearrange("p (i l n) -> p i l n", i=2, n=60)

        loaded = sem("small_loaded")
        tab_in, row_in = sem("tables_loaded"), sem("row_loaded")
        weights_in = [sem(f"weights_in{s}") for s in range(RING)]
        hi_ready, lo_ready = sem("piece_hi"), sem("piece_lo")
        done = sem("piece_done")
        n_ready = sem("narrow_split")
        ss_ready, ms_ready, rstd_ready = sem("sumsq_ready"), sem("meansq_ready"), sem("rstd_ready")
        xs_ready, xt_done = sem("xs_ready"), sem("norm_transposed")
        xT_hi, xT_lo = sem("xT_hi"), sem("xT_lo")
        h_ready = sem("h_ready")
        pow_ready = sem("power_ready")
        act_step, dve_step = sem("act_step"), sem("dve_step")
        stored = sem("stored")

        class Evac:
            def __init__(self, name):
                self.freed = sem(name + "_unit_freed")

        def bank(u):
            return 4 + u % 3

        def plus(n, turn, each):
            return n if turn is None else turn * each + n

        class Hidden:
            def __init__(self, g0, chunks, dn, rounds):
                self.g0, self.chunks, self.dn, self.rounds = g0, chunks, dn, rounds

            def up(self, c):
                return self.g0 + (2 * c if c < 2 else 4 + self.dn + (c - 2) * (2 + self.dn))

            def down(self, c):
                return self.g0 + 4 if c == 0 else self.g0 + 4 + self.dn + (c - 1) * (2 + self.dn) + \
                    (2 if c < self.chunks - 1 else 0)

            def run(self, eng, up, down):
                up(0, None)
                up(1, None)
                down(0, None)
                with eng.Fori(0, self.rounds) as turn:
                    for c in range(2, 5):
                        up(c, turn)
                        down(c - 1, turn)
                for c in range(2 + 3 * self.rounds, self.chunks):
                    up(c, None)
                    down(c - 1, None)
                down(self.chunks - 1, None)

            @property
            def each(self):
                return 3 * (2 + self.dn)

        mlp_h = [Hidden(g, MLP_C, 2, 2) for g in G_MLP]
        ffn_h = [Hidden(g, FFN_C, 1, 3 - n) for n, g in enumerate(G_FFN)]

        H_AT = [0, 4, 8, 12, 16, 18, 22, 26, 30, 34]
        XS_OF = {0: 0, 1: 1, 2: 2, 3: 3, 5: 4, 6: 5, 7: 6, 8: 7}
        XT_OF = {0: 0, 1: 1, 2: 2, 3: 3, 5: 4, 6: 5, 7: 6, "7b": 7, 8: 8}
        GAIN_OF = {0: 0, 1: 1, 2: 2, 3: 3, 5: 4, 6: 5, 7: 6, "7b": 7, 8: 8}

        sb_u, rt_u, gl_u, ns_u = Evac("sb"), Evac("ret"), Evac("gla"), Evac("nsa")
        sbz, sbc, sbe, sbl, sbm = sem("sb_z"), sem("sb_clipped"), sem("sb_exp"), sem("sb_log"), sem("sb_softplus")
        sbs, sbt, sbx, sba, sbo, sbv = (sem("sb_masked"), sem("sb_summed"), sem("sb_weights"), sem("sb_wmasked"),
                                        sem("sb_out"), sem("sb_out_copied"))
        mlp_s = [(sem(f"mlp{i}_freed"), sem(f"mlp{i}_hidden"), sem(f"mlp{i}_hi"), sem(f"mlp{i}_square")) for i in range(2)]
        y_h = sem("sb_out_hi")
        ffn_s = [(sem(f"ffn{i}_freed"), sem(f"ffn{i}_hidden"), sem(f"ffn{i}_base"), sem(f"ffn{i}_tap"),
                  sem(f"ffn{i}_silu"), sem(f"ffn{i}_product"), sem(f"ffn{i}_hi")) for i in range(2)]
        rt_qk, rt_sc, rt_dec, rt_o, rt_of, rt_ms, rt_rs, rt_yr, rt_tr, rt_ya, rt_yd = (
            sem("ret_qk"), sem("ret_scores"), sem("ret_decayed"), sem("ret_o"), sem("ret_o_free"),
            sem("ret_var"), sem("ret_rstd"), sem("ret_y"), sem("ret_transposed"), sem("ret_yT_hi"), sem("ret_yT_lo"))
        gl_pj, gl_x_r, gl_e, gl_lg, gl_df, gl_ex, gl_wr, gl_lv, gl_cp, gl_o, gl_s, gl_m, gl_p, gl_yr, gl_tr, gl_ya, gl_yd, gl_rg = (
            sem("gla_small_proj"), sem("gla_logit"), sem("gla_exp"), sem("gla_log"), sem("gla_diff"), sem("gla_decay"),
            sem("gla_w"), sem("gla_level"), sem("gla_level_copied"), sem("gla_o"), sem("gla_sumsq"), sem("gla_meansq"),
            sem("gla_rstd"), sem("gla_y"), sem("gla_transposed"), sem("gla_yT_hi"), sem("gla_yT_lo"), sem("gla_gate"))
        gl_sl, gl_nt, ns_xf, ns_xhr = sem("gla_silu"), sem("gla_natural"), sem("nsa_blocks_f32"), sem("nsa_blocks_hi")
        ns_pj, ns_xr, ns_hd, ns_sq, ns_u1, ns_th, ns_hr, ns_kv, ns_kcr, ns_vr, ns_qrr = (
            sem("nsa_small_proj"), sem("nsa_blocks"), sem("nsa_hidden"), sem("nsa_square"), sem("nsa_inner"),
            sem("nsa_tanh"), sem("nsa_gelu"), sem("nsa_cmp_kv"), sem("nsa_kc"), sem("nsa_vbd"), sem("nsa_roped"))
        ns_kdr, ns_cq, ns_ci, ns_ce, ns_cpr, ns_ct, ns_cc = (
            sem("nsa_kd"), sem("nsa_cmp_scores"), sem("nsa_cmp_shifted"), sem("nsa_cmp_exp"), sem("nsa_cmp_p"),
            sem("nsa_cmp_pT"), sem("nsa_cmp_pT_copied"))
        ns_qk, ns_add, ns_mx, ns_ex, ns_co, ns_pr, ns_tp, ns_tc, ns_o, ns_oc, ns_ot, ns_oa, ns_od = (
            sem("nsa_scores"), sem("nsa_masked"), sem("nsa_max"), sem("nsa_exp"), sem("nsa_coef"), sem("nsa_p"),
            sem("nsa_pT"), sem("nsa_pT_copied"), sem("nsa_o"), sem("nsa_o_copied"), sem("nsa_oT"),
            sem("nsa_oT_hi"), sem("nsa_oT_lo"))

        block = ctx.enter_context(nc.Block())

        @block.sync
        def _(sp):
            sp.dma_start(h[:, :, :], x_in.rearrange("(t p) d -> p t d", p=P)).then_inc(loaded, 16)

            def stream(g, turn=None):
                if turn is not None or g >= RING:
                    sp.wait_ge(lo_ready, plus(g - RING + 1, turn, RING))
                src = ws[g] if turn is None else ws[bass.ds(turn * RING + g, 1), :, :].rearrange("a p n -> p (a n)")
                sp.dma_start(ring[:, g % RING, :], src).then_inc(weights_in[g % RING], 16)

            for g in range(RING):
                stream(g)
            turns = (G_END - RING) // RING
            with sp.Fori(0, turns) as turn:
                for g in range(RING, 2 * RING):
                    stream(g, turn)
            for g in range(RING + turns * RING, G_END):
                stream(g)
            for t in range(TT):
                sp.wait_ge(xs_ready, 2 * len(XS_OF) + t + 1)
                sp.dma_start(out[t * P:(t + 1) * P, :], xs[:, t, :]).then_inc(stored, 16)
            sp.wait_ge(stored, 16 * TT)

        @block.gpsimd
        def _(pool):
            gp = nc.gpsimd
            gp.memset(power[:, :], -0.5).then_inc(pow_ready, 1)
            pool.wait_ge(pow_ready, 1)

            def norm_power(n):
                pool.wait_ge(ms_ready, n + 1)
                gp.tensor_tensor(rstd, msq, power[:, 0:2], ALU.pow).then_inc(rstd_ready, 1)

            norm_power(0)

            def below(v):
                for d in (v[:, :, 0:P], v[:, :, T:384]):
                    r = gp.affine_select(out=d, in_=d, compare_op=ALU.is_gt, fill=0.0, base=0,
                                         pattern=[[0, 2], [1, P]], channel_multiplier=-1)
                return r

            def sp_mask(p):
                pool.wait_ge(sbm, p + 1)
                below(sb_s[:, p % 2]).then_inc(sbs, 1)

            sp_mask(0)
            sp_mask(1)
            for p in range(8):
                pool.wait_ge(sbx, p + 1)
                below(sb_a[:, p % 2]).then_inc(sba, 1)
                if p + 2 < 8:
                    sp_mask(p + 2)
            norm_power(1)
            norm_power(2)
            for u in range(8):
                dst = rt_q if u < 4 else rt_k
                v = dst[:, 2 * (u % 4):2 * (u % 4) + 2, :]
                a, b = rt_c[:, u % 2, :], rt_n[:, u % 2, :]
                pool.wait_ge(rt_u.freed, u + 1)
                gp.tensor_tensor(v[:, 0, :], a[:, 0:T], b[:, T:2 * T], ALU.subtract)
                gp.tensor_tensor(v[:, 1, :], b[:, 0:T], a[:, T:2 * T], ALU.add).then_inc(rt_qk, 1)
            pool.wait_ge(rt_ms, 1)
            gp.tensor_tensor(rs8, ms8, power[:, 0:8], ALU.pow).then_inc(rt_rs, 1)
            norm_power(3)
            norm_power(4)
            norm_power(5)
            pool.wait_ge(row_in, 32)
            for t in range(TT):
                pool.wait_ge(gl_sl, t + 1)
                gp.tensor_tensor(gl_r[:, t, :], gl_r[:, t, :], rowg[:, :], ALU.mult).then_inc(gl_rg, 1)
            pool.wait_ge(gl_m, 1)
            gp.tensor_tensor(rs8, ms8, power[:, 0:8], ALU.pow).then_inc(gl_p, 1)
            norm_power(6)

            def ffn(n):
                freed, ready, base, tap, sl, pr, hh = ffn_s[n]
                st = ffn_h[n]

                def up(c, turn):
                    for u in (2 * c, 2 * c + 1):
                        pool.wait_ge(sl, plus(u + 1, turn, 6))
                        gp.tensor_tensor(prod[:, u % 2, :], silu[:, u % 2, :], conv[:, u % 2, 1, :], ALU.mult)\
                          .then_inc(pr, 1)
                        pool.wait_ge(hh, plus(u + 1, turn, 6))
                        i = 4 * (c % 3) + u % 2
                        gp.tensor_tensor(y_lo[:, i, :], prod[:, u % 2, :], y_hi[:, i, :].bitcast(F32), ALU.subtract)\
                          .then_inc(ready, 1)

                st.run(pool, up, lambda c, turn: None)

            ffn(0)
            norm_power(7)
            for it in range(16):
                pool.wait_ge(ns_co, it + 1)
                for t in range(2):
                    v = ns_s[:, it % 2, :, P * t:P * t + P * (t + 1)]
                    f = ns_f[:, it % 2, :, t:t + 1].broadcast_to([P, 2, P * (t + 1)])
                    r = gp.tensor_tensor(v, v, f, ALU.mult)
                r.then_inc(ns_pr, 1)
            norm_power(8)
            ffn(1)
            norm_power(9)

        @block.tensor
        def _(pe):
            mm = nc.tensor.matmul

            def norm(n):
                for t in range(TT):
                    if n in XS_OF:
                        pe.wait_ge(xs_ready, 2 * XS_OF[n] + t + 1)
                    for k in range(KT):
                        r = nc.tensor.transpose(ps[:, 4 + k // 2, (k % 2) * T + t * P:(k % 2) * T + (t + 1) * P],
                                                xs[:, t, k * P:(k + 1) * P], ident)
                        if t == 1 and k % 2 == 1:
                            r.then_inc(xt_done, 1)

            def x_tiles(n, k):
                if k % 2 == 0:
                    pe.wait_ge(xT_lo, 4 * XT_OF[n] + k // 2 + 1)

            def split(g, turn=None, each=0):
                pe.wait_ge(lo_ready, plus(g + 1, turn, each))

            def mm3(o, lh, ll, rh, rl, start, stop):
                mm(o, lh, rh, start=start, stop=False, skip_group_check=True)
                mm(o, lh, rl, start=False, stop=False, skip_group_check=True)
                return mm(o, ll, rh, start=False, stop=stop, skip_group_check=True)

            def transposed(g, u, freed, first=None, turn=None, each=0, units=0):
                split(g, turn, each)
                if u >= 3:
                    pe.wait_ge(freed, plus(u - 2, turn, units))
                s = g % RING
                for j in range(2):
                    for k in range(KT):
                        if first is not None and j == 0:
                            x_tiles(first, k)
                        c = k * 256 + j * P
                        r = mm3(ps[:, bank(u), j * T:(j + 1) * T], w_hi[:, s, c:c + P], w_lo[:, s, c:c + P],
                                x_hi[:, k, :], x_lo[:, k, :], k == 0, k == KT - 1)
                r.then_inc(done, 1)

            def natural(g, u, freed):
                for e in range(2):
                    split(g + e)
                    s = (g + e) % RING
                    for t in range(TT):
                        if e == 0 and u + t >= 3:
                            pe.wait_ge(freed, u + t - 2)
                        for k in range(4):
                            x = 4 * e + k
                            r = mm3(ps[:, bank(u + t), :], x_hi[:, x, t * P:(t + 1) * P], x_lo[:, x, t * P:(t + 1) * P],
                                    w_hi[:, s, k * 512:(k + 1) * 512], w_lo[:, s, k * 512:(k + 1) * 512],
                                    x == 0, x == KT - 1)
                    r.then_inc(done, 1)

            def accumulate(g, tiles, first, last, turn=None, each=0):
                split(g, turn, each)
                s = g % RING
                for k, tile in enumerate(tiles):
                    for j in range(4):
                        t, c = j // 2, k * D + (j % 2) * 512
                        r = mm3(ps[:, j, :], y_hi[:, tile, t * P:(t + 1) * P], y_lo[:, tile, t * P:(t + 1) * P],
                                w_hi[:, s, c:c + 512], w_lo[:, s, c:c + 512], first and k == 0, last and k == 1)
                r.then_inc(done, 1)

            def hidden(n, st, freed, ready):
                def up(c, turn):
                    for i in range(2):
                        transposed(st.up(c) + i, 2 * c + i, freed, first=n if c + i == 0 else None,
                                   turn=turn, each=st.each, units=6)

                def down(c, turn):
                    pe.wait_ge(ready, plus(2 * c + 2, turn, 6))
                    for i in range(st.dn):
                        accumulate(st.down(c) + i, (4 * (c % 3) + 2 * i, 4 * (c % 3) + 2 * i + 1), c == 0 and i == 0,
                                   c == st.chunks - 1 and i == st.dn - 1, turn, st.each)

                st.run(pe, up, down)

            def transpose_pair(b, src, g):
                for k in range(2):
                    for t in range(TT):
                        r = nc.tensor.transpose(ps[:, b, k * T + t * P:k * T + (t + 1) * P],
                                                src[:, t, (2 * g + k) * P:(2 * g + k + 1) * P], ident)
                return r

            pe.wait_ge(loaded, 48)
            norm(0)
            for u in range(8):
                transposed(G_SB + u, u, sb_u.freed, first=0 if u == 0 else None)
            for c in range(2):
                natural(G_SB + 8 + 2 * c, 8 + 2 * c, sb_u.freed)
            ntri, none = tab[:, C_NTRI:C_NTRI + P], tab[:, C_NONE:C_NONE + P]

            def sb_z_(p):
                if p == 0:
                    pe.wait_ge(tab_in, 16)
                    pe.wait_ge(sb_u.freed, 12)
                if p >= 2:
                    pe.wait_ge(sbx, p - 1)
                for i in range(2):
                    b, o = 4 + 2 * (p % 2) + i, 64 * i
                    mm(ps[:, b, 0:T], sb_k[o:o + 64, p, 0:P], sb_q[o:o + 64, p, :], start=True, stop=True,
                       skip_group_check=True)
                    r = mm(ps[:, b, T:384], sb_k[o:o + 64, p, P:T], sb_q[o:o + 64, p, P:T], start=False, stop=True,
                           skip_group_check=True)
                r.then_inc(sbz, 1)

            def sb_sum(p):
                pe.wait_ge(sbs, p + 1)
                for i in range(2):
                    b, s = 4 + 2 * (p % 2) + i, sb_s[:, p % 2, i, :]
                    mm(ps[:, b, 0:T], ntri, s[:, 0:T], start=False, stop=True, skip_group_check=True)
                    mm(ps[:, b, P:T], none, s[:, T:384], start=False, stop=True, skip_group_check=True)
                    r = mm(ps[:, b, T:384], ntri, s[:, T:384], start=False, stop=True, skip_group_check=True)
                r.then_inc(sbt, 1)

            def sb_av(p):
                pe.wait_ge(sba, p + 1)
                if p >= 2:
                    pe.wait_ge(sbv, p - 1)
                for i in range(2):
                    c, a = (2 * p + i) * 64, sb_a[:, p % 2, i, :]
                    o = ps[64 * i:64 * i + 64, p % 2, :]
                    mm(o[:, 0:T], sb_v[:, 0, c:c + 64], a[:, 0:T], start=True, stop=False, skip_group_check=True)
                    r = mm(o[:, P:T], sb_v[:, 1, c:c + 64], a[:, T:384], start=False, stop=True, skip_group_check=True)
                r.then_inc(sbo, 1)

            sb_z_(0)
            sb_z_(1)
            for p in range(8):
                sb_sum(p)
                if p:
                    sb_av(p - 1)
                if p + 2 < 8:
                    sb_z_(p + 2)
            sb_av(7)
            for i in range(4):
                pe.wait_ge(sbv, 2 * i + 2 if i else 8)
                accumulate(G_SB + 12 + i, (2 * i, 2 * i + 1), i == 0, i == 3)
            norm(1)
            hidden(1, mlp_h[0], mlp_s[0][0], mlp_s[0][1])

            norm(2)
            for u in range(8):
                transposed(G_RET + u, u, rt_u.freed, first=2 if u == 0 else None)
            for c in range(8):
                natural(G_RET + 8 + 2 * c, 8 + 2 * c, rt_u.freed)
            pe.wait_ge(rt_u.freed, 24)
            pe.wait_ge(rt_qk, 8)
            for hd in range(RET_HEADS):
                for k in range(2):
                    mm(ps[:, 4 + hd, 0:T], rt_k[:, 2 * hd + k, 0:P], rt_q[:, 2 * hd + k, :], start=k == 0, stop=k == 1)
                for k in range(2):
                    r = mm(ps[:, 4 + hd, T:384], rt_k[:, 2 * hd + k, P:T], rt_q[:, 2 * hd + k, P:T],
                           start=k == 0, stop=k == 1)
                r.then_inc(rt_sc, 1)
            for hd in range(RET_HEADS):
                pe.wait_ge(rt_dec, hd + 1)
                for t in range(TT):
                    i = 2 * hd + t
                    if i >= 4:
                        pe.wait_ge(rt_of, i - 3)
                    r = mm(ps[:, i % 4, :], rt_s[:, hd, t * P:(t + 1) * P], rt_v[:, 0, hd * 512:(hd + 1) * 512],
                           start=True, stop=t == 0)
                    if t == 1:
                        r = mm(ps[:, i % 4, :], rt_s[:, hd, T:384], rt_v[:, 1, hd * 512:(hd + 1) * 512],
                               start=False, stop=True)
                    r.then_inc(rt_o, 1)
            for g in range(10):
                if g < 8:
                    pe.wait_ge(rt_yr, 2 * (g // 2) + 2)
                    if g >= 4:
                        pe.wait_ge(rt_yd, g - 3)
                    transpose_pair(4 + g % 4, rt_g, g).then_inc(rt_tr, 1)
                if g >= 2:
                    i = g - 2
                    pe.wait_ge(rt_yd, i + 1)
                    accumulate(G_RET + 24 + i, (2 * i % 12, 2 * i % 12 + 1), i == 0, i == 7)
            norm(3)
            hidden(3, mlp_h[1], mlp_s[1][0], mlp_s[1][1])

            norm(5)
            pe.wait_ge(n_ready, 2)
            for t in range(TT):
                for k in range(KT):
                    if t == 0:
                        x_tiles(5, k)
                    x = slice(t * P, (t + 1) * P)
                    r = mm3(ps[:, 4, t * 16:t * 16 + 16], x_hi[:, k, x], x_lo[:, k, x],
                            n_hi[:, 16 * k:16 * k + 16], n_lo[:, 16 * k:16 * k + 16], k == 0, k == KT - 1)
            r.then_inc(gl_pj, 1)
            transposed(G_GLA, 1, gl_u.freed)
            pe.wait_ge(gl_nt, 1)
            for t in range(TT):
                r = mm(ps[0:16, 7, t * P:(t + 1) * P], gl_nat[:, t, :], ident, start=True, stop=True)
            r.then_inc(gl_pj, 1)
            for u in range(2, 5):
                transposed(G_GLA + u - 1, u, gl_u.freed)
            for i in range(2):
                pe.wait_ge(gl_nt, 2)
                pe.wait_ge(gl_u.freed, 5 + i - 2)
                for j in range(2):
                    c = S_ALPHA + (2 * i + j) * P
                    r = mm(ps[:, bank(5 + i), j * T:(j + 1) * T], sm[0:16, c:c + P], gl_low, start=True, stop=True)
                r.then_inc(gl_pj, 1)
            for c in range(4):
                natural(G_GLA + 4 + 2 * c, 7 + 2 * c, gl_u.freed)
            for i in range(16):
                l, t = i // 2, i % 2
                if l >= 1:
                    pe.wait_ge(gl_wr, l)
                if i >= 4:
                    pe.wait_ge(gl_cp, i - 3)
                for hd in range(GLA_HEADS):
                    kk = gl_k if l == 0 else gl_w[l - 1]
                    qq = gl_q if l == 0 else gl_w[l - 1]
                    r = mm(ps[:, i % 4, hd * P:(hd + 1) * P], kk[:, hd, t * P:(t + 1) * P], qq[:, hd, t * P:(t + 1) * P],
                           start=True, stop=True)
                r.then_inc(gl_lv, 1)
            pe.wait_ge(gl_wr, 8)
            pe.wait_ge(gl_cp, 13)
            for hd in range(GLA_HEADS):
                r = mm(ps[:, 0, hd * P:(hd + 1) * P], gl_w[7][:, hd, 0:P], gl_w[7][:, hd, P:T], start=True, stop=True)
            r.then_inc(gl_lv, 1)
            pe.wait_ge(gl_u.freed, 15)
            pe.wait_ge(gl_cp, 17)
            for t in range(TT):
                for hd in range(GLA_HEADS):
                    o = ps[:, 4 + 2 * t + hd // 2, (hd % 2) * T:(hd % 2 + 1) * T]
                    v = gl_v[:, :, hd * 256:(hd + 1) * 256]
                    if t == 1:
                        mm(o, gl_across[:, hd, :], v[:, 0, :], start=True, stop=False)
                    r = mm(o, gl_a[t][:, hd, :], v[:, t, :], start=t == 0, stop=True)
                r.then_inc(gl_o, 1)
            pe.wait_ge(gl_yr, 2)
            for g in range(4):
                transpose_pair(g, gl_r, g).then_inc(gl_tr, 1)
            pe.wait_ge(gl_yd, 4)
            for i in range(4):
                accumulate(G_GLA + 12 + i, (2 * i, 2 * i + 1), i == 0, i == 3)
            norm(6)
            hidden(6, ffn_h[0], ffn_s[0][0], ffn_s[0][1])

            norm(7)
            for u in range(4):
                transposed(G_NSA + u, u, ns_u.freed, first=7 if u == 0 else None)
            natural(G_NSA + 4, 4, ns_u.freed)
            pe.wait_ge(ns_u.freed, 6)
            norm("7b")
            for i in range(2):
                pe.wait_ge(ns_xr, i + 1)
                for e in range(2):
                    g = G_NSA + 6 + 2 * i + e
                    split(g)
                    s = g % RING
                    for l in range(8):
                        for c in range(2):
                            w = l * 256 + c * P
                            r = mm3(ps[:, i, c * 64:c * 64 + 60], w_hi[:, s, w:w + P], w_lo[:, s, w:w + P],
                                    ns_xh[:, i, 8 * e + l, :], ns_xl[:, i, 8 * e + l, :], e + l + c == 0, e * l == 7)
                    r.then_inc(done, 1)
            for u in range(6, 10):
                transposed(G_NSA + 4 + u, u, ns_u.freed, first="7b" if u == 6 else None)
            pe.wait_ge(tab_in, 80)
            swap = tab[:, C_SWAP:C_SWAP + P]
            for i in range(6):
                pe.wait_ge(ns_u.freed, 10 if i < 3 else 10 + i - 2)
                src = ns_k[:, i, :, :] if i < 2 else ns_q[:, 2 * (i - 2):2 * (i - 2) + 2, :]
                mm(ps[:, bank(10 + i), :], swap, src, start=True, stop=True).then_inc(ns_pj, 1)
            pe.wait_ge(ns_u.freed, 14)
            for t in range(TT):
                for k in range(KT):
                    c = N_LOW + 48 * k
                    x = slice(t * P, (t + 1) * P)
                    r = mm3(ps[:, bank(16), t * 64:t * 64 + 48], x_hi[:, k, x], x_lo[:, k, x], n_hi[:, c:c + 48],
                            n_lo[:, c:c + 48], k == 0, k == KT - 1)
            r.then_inc(ns_pj, 1)
            pe.wait_ge(ns_hr, 2)
            for c in range(2):
                r = mm(ps[:, 2, 0:64], sm[:, S_W2K + c * P:S_W2K + (c + 1) * P], ns_h[:, 2, c, :],
                       start=c == 0, stop=c == 1)
            r.then_inc(ns_kv, 1)
            pe.wait_ge(ns_hr, 3)
            for g in range(2):
                for c in range(2):
                    r = mm(ps[:, 3, g * 64:(g + 1) * 64], ns_hv[:, g, c, :],
                           sm[:, S_W2V + c * 64:S_W2V + (c + 1) * 64], start=c == 0, stop=c == 1)
            r.then_inc(ns_kv, 1)
            pe.wait_ge(ns_kcr, 1)
            pe.wait_ge(ns_u.freed, 17)
            for t in range(TT):
                for hd in range(NSA_HEADS):
                    o = 64 * (hd % 2)
                    c = t * P + hd // 2 * CMP
                    r = mm(ps[:, 6 - hd % 2, c:c + CMP], ns_q[o:o + 64, hd // 2, t * P:(t + 1) * P],
                           ns_kc[o:o + 64, hd // 4, :], start=True, stop=True)
            r.then_inc(ns_cq, 1)
            pe.wait_ge(ns_cpr, 1)
            for i in range(4):
                r = nc.tensor.transpose(ps[:, 7, i * P:(i + 1) * P],
                                        ns_cs[:, i // 2, 8 * (i % 2):8 * (i % 2) + 8, :], ident)
            r.then_inc(ns_ct, 1)
            pe.wait_ge(ns_cc, 1)
            pe.wait_ge(ns_vr, 2)
            for i in range(4):
                mm(ps[:, i, :], ns_cp[:, i, :], ns_vbd[:, i % 2, :, :], start=True, stop=False, skip_group_check=True)

            def ns_qk_(it):
                br, pr = it // 8, it % 8
                if it == 0:
                    pe.wait_ge(ns_kdr, 2)
                    pe.wait_ge(ns_qrr, 4)
                else:
                    pe.wait_ge(ns_add, it)
                for i in range(2):
                    o = 64 * i
                    kd = ns_kd[o:o + 64, br, pr // 2, :]
                    q = ns_qr[o:o + 64, pr, :]
                    mm(ps[:, 4 + i, 0:P], q[:, 0:P], kd[:, 0:P], start=True, stop=True)
                    r = mm(ps[:, 4 + i, P:384], q[:, P:T], kd, start=True, stop=True)
                r.then_inc(ns_qk, 1)

            def ns_t_(it):
                pe.wait_ge(ns_pr, it + 1)
                for i in range(2):
                    for j in range(3):
                        r = nc.tensor.transpose(ps[:, 6 + i, j * P:(j + 1) * P],
                                                ns_s[:, it % 2, i, j * P:(j + 1) * P], ident)
                r.then_inc(ns_tp, 1)

            def ns_pv_(it):
                br, pr = it // 8, it % 8
                pe.wait_ge(ns_tc, it + 1)
                for i in range(2):
                    hd = 2 * pr + i
                    v = ns_v[:, :, br * 256 + (hd // 4) * 64:br * 256 + (hd // 4) * 64 + 64]
                    c = (hd % 8) * 64
                    p_ = ns_p[:, it % 2, i, :]
                    mm(ps[:, hd // 8, c:c + 64], p_[:, 0:P], v[:, 0, :], start=False, stop=br == 1,
                       skip_group_check=True)
                    mm(ps[:, 2 + hd // 8, c:c + 64], p_[:, P:T], v[:, 0, :], start=False, stop=False,
                       skip_group_check=True)
                    r = mm(ps[:, 2 + hd // 8, c:c + 64], p_[:, T:384], v[:, 1, :], start=False, stop=br == 1,
                           skip_group_check=True)
                return r

            ns_qk_(0)
            for it in range(16):
                if it + 1 < 16:
                    ns_qk_(it + 1)
                if it:
                    ns_pv_(it - 1)
                ns_t_(it)
            ns_pv_(15).then_inc(ns_o, 1)
            pe.wait_ge(ns_oc, 4)
            for g in range(4):
                transpose_pair(4 + g, ns_on, g).then_inc(ns_ot, 1)
            for i in range(4):
                pe.wait_ge(ns_od, i + 1)
                accumulate(G_NSA + 14 + i, (2 * i, 2 * i + 1), i == 0, i == 3)
            norm(8)
            hidden(8, ffn_h[1], ffn_s[1][0], ffn_s[1][1])

        @block.scalar
        def _(act):
            A = nc.scalar.activation
            steps = [0]
            act.dma_start(sm[:, :], small).then_inc(loaded, 16)
            act.dma_start(narrow_raw, narrow).then_inc(loaded, 16)
            act.dma_start(tab[:, :], tables[0]).then_inc(tab_in, 16)
            act.dma_start(rowg[:, :], rows[0:1, :].partition_broadcast(P)).then_inc(row_in, 16)
            act.wait_ge(loaded, 48)

            def link(ins):
                steps[0] += 1
                ins.then_inc(act_step, 1)
                act.wait_ge(act_step, steps[0])

            def sumsq(n):
                for t in range(TT):
                    if H_AT[n]:
                        act.wait_ge(h_ready, H_AT[n] - (2 if n != 5 else 1) * (1 - t))
                    A(xs[:, t, :], h[:, t, :], ACT.Square, accum_out=ssq[:, t:t + 1]).then_inc(ss_ready, 1)

            def hi(g, turn=None, each=0):
                s = g % RING
                act.wait_ge(weights_in[s], 16 * (g // RING + 1) + (0 if turn is None else turn * (16 * each // RING)))
                A(w_hi[:, s, :], ring[:, s, :], ACT.Copy).then_inc(hi_ready, 1)

            def refill(g, turn=None, each=0):
                if g + RING < G_END:
                    act.wait_ge(done, plus(g + 1, turn, each))
                    hi(g + RING, turn, each)

            def norm_tiles(n):
                i = XT_OF[n]
                for b in range(4):
                    act.wait_ge(xt_done, 4 * i + b + 1)
                    for k in (2 * b, 2 * b + 1):
                        c = S_GAIN + GAIN_OF[n] * KT + k
                        r = A(x_hi[:, k, :], ps[:, 4 + b, (k % 2) * T:(k % 2 + 1) * T], ACT.Copy, scale=sm[:, c:c + 1])
                    r.then_inc(xT_hi, 1)

            def norm(n):
                sumsq(n)
                norm_tiles(n)

            def evac(u, g, dst, freed, func=ACT.Copy, scale=1.0, after=None):
                if after is not None:
                    act.wait_ge(freed, after)
                act.wait_ge(done, g + 1)
                A(dst, ps[:, bank(u), :], func, scale=scale).then_inc(freed, 1)

            def mlp(n):
                freed, ready, hh, sq = mlp_s[n]
                st = mlp_h[n]

                def up(c, turn):
                    for u in (2 * c, 2 * c + 1):
                        g = st.up(c) + u % 2
                        act.wait_ge(done, plus(g + 1, turn, st.each))
                        if u >= 2:
                            act.wait_ge(ready, plus(u - 1, turn, 6))
                        A(relu[:, u % 2, :], ps[:, bank(u), :], ACT.Relu).then_inc(freed, 1)
                        act.wait_ge(freed, plus(u + 1, turn, 6))
                        i = 4 * (c % 3) + 2 * (u % 2)
                        A(y_hi[:, i:i + 2, :], relu[:, u % 2, :].rearrange("p (a t) -> p a t", t=T), ACT.Square)\
                            .then_inc(hh, 1)
                        refill(g, turn, st.each)

                def down(c, turn):
                    for i in range(st.dn):
                        refill(st.down(c) + i, turn, st.each)

                st.run(act, up, down)

            def ffn(n):
                freed, ready, base, tap, sl, pr, hh = ffn_s[n]
                st = ffn_h[n]
                col = S_CONV + n * FFN_TILES * 8

                def par(u, j, turn):
                    c = col + 8 * u + j
                    return sm[:, c:c + 1] if turn is None else sm[:, bass.ds(turn * 48 + c, 1)]

                def up(c, turn):
                    for u in (2 * c, 2 * c + 1):
                        g = st.up(c) + u % 2
                        act.wait_ge(done, plus(g + 1, turn, st.each))
                        if u >= 2:
                            act.wait_ge(ready, plus(u - 1, turn, 6))
                        for e in range(2):
                            r = A(conv[:, u % 2, e, :], ps[:, bank(u), e * T:(e + 1) * T], ACT.Identity,
                                  scale=par(u, 4 + e, turn), bias=par(u, 6 + e, turn))
                        r.then_inc(base, 1)
                        refill(g, turn, st.each)
                        act.wait_ge(freed, plus(u + 1, turn, 6))
                        A(silu[:, u % 2, :], conv[:, u % 2, 0, :], ACT.Silu).then_inc(sl, 1)
                        act.wait_ge(pr, plus(u + 1, turn, 6))
                        A(y_hi[:, 4 * (c % 3) + u % 2, :], prod[:, u % 2, :], ACT.Copy).then_inc(hh, 1)

                def down(c, turn):
                    for i in range(st.dn):
                        refill(st.down(c) + i, turn, st.each)

                st.run(act, up, down)

            for g in range(RING):
                hi(g)
            A(n_hi[:, :], narrow_raw, ACT.Copy).then_inc(n_ready, 1)
            norm(0)
            for u in range(8):
                evac(u, G_SB + u, (sb_q if u < 4 else sb_k)[:, 2 * (u % 4):2 * (u % 4) + 2, :], sb_u.freed,
                     scale=0.125 if u < 4 else 1.0)
                refill(G_SB + u)
            for c in range(2):
                refill(G_SB + 8 + 2 * c)
                for t in range(TT):
                    evac(8 + 2 * c + t, G_SB + 9 + 2 * c, sb_v[:, t, c * 512:(c + 1) * 512], sb_u.freed)
                refill(G_SB + 9 + 2 * c)

            def sb_soft(p):
                e = sb_e[:, p % 2, :, :]
                act.wait_ge(sbc, p + 1)
                A(e, e, ACT.Exp).then_inc(sbe, 1)
                act.wait_ge(sbe, p + 1)
                A(e, e, ACT.Ln, bias=1.0).then_inc(sbl, 1)

            def sb_hi(p):
                act.wait_ge(sbo, p + 1)
                A(y_hi[:, p, :], ps[:, p % 2, 0:T], ACT.Copy).then_inc(y_h, 1)

            sb_soft(0)
            sb_soft(1)
            for p in range(8):
                act.wait_ge(sbt, p + 1)
                b = 4 + 2 * (p % 2)
                A(sb_a[:, p % 2, :, :], ps[:, b:b + 2, 0:384], ACT.Exp).then_inc(sbx, 1)
                if p:
                    sb_hi(p - 1)
                if p + 2 < 8:
                    sb_soft(p + 2)
            sb_hi(7)
            for i in range(4):
                refill(G_SB + 12 + i)
            sumsq(1)
            act.dma_start(tab[:, :], tables[1]).then_inc(tab_in, 16)
            act.dma_start(rt_decay, decay).then_inc(tab_in, 16)
            norm_tiles(1)
            mlp(0)
            norm(2)
            for u in range(8):
                refill(G_RET + u)
            for c in range(8):
                refill(G_RET + 8 + 2 * c)
                for t in range(TT):
                    evac(8 + 2 * c + t, G_RET + 9 + 2 * c, (rt_v if c < 4 else rt_g)[:, t, (c % 4) * 512:(c % 4 + 1) * 512],
                         rt_u.freed, func=ACT.Copy if c < 4 else ACT.Silu, after=8 if c + t == 0 else None)
                refill(G_RET + 9 + 2 * c)
            act.wait_ge(rt_rs, 1)
            for i in range(8):
                v = rt_g[:, i % 2, (i // 2) * 512:(i // 2 + 1) * 512]
                act.wait_ge(rt_of, i + 1)
                A(v, v, ACT.Copy, scale=rs8[:, i:i + 1]).then_inc(rt_yr, 1)
            for g in range(10):
                if g < 8:
                    act.wait_ge(rt_tr, g + 1)
                    if g >= 6:
                        act.wait_ge(done, G_RET + 24 + g - 6 + 1)
                    i = 2 * g % 12
                    A(y_hi[:, i:i + 2, :], ps[:, 4 + g % 4, :].rearrange("p (a t) -> p a t", t=T), ACT.Copy)\
                        .then_inc(rt_ya, 1)
                if g >= 2:
                    refill(G_RET + 24 + g - 2)
            sumsq(3)
            act.dma_start(tab[:, :], tables[2]).then_inc(tab_in, 16)
            norm_tiles(3)
            mlp(1)
            sumsq(4)
            sumsq(5)
            act.dma_start(rowg[:, :], rows[1:2, :].partition_broadcast(P)).then_inc(row_in, 16)
            norm_tiles(5)
            for u in range(1, 5):
                dst = (gl_q if u < 3 else gl_k)[:, 2 * ((u - 1) % 2):2 * ((u - 1) % 2) + 2, :]
                evac(u, G_GLA + u - 1, dst, gl_u.freed, scale=P ** -0.5 if u < 3 else 1.0, after=1 if u == 1 else None)
                refill(G_GLA + u - 1)
            act.wait_ge(gl_x_r, 1)
            A(gl_l[:, :, :], gl_l[:, :, :], ACT.Exp).then_inc(gl_e, 1)
            act.wait_ge(gl_e, 1)
            A(gl_l[:, :, :], gl_l[:, :, :], ACT.Ln, bias=1.0).then_inc(gl_lg, 1)
            for j in range(8):
                w = gl_w[j][:, :, :]
                act.wait_ge(gl_df, j + 1)
                link(A(w, w, ACT.Abs))
                A(w, w, ACT.Exp, scale=-1.0 / 16.0).then_inc(gl_ex, 1)
                refill(G_GLA + 4 + j)
                if j % 2 == 1:
                    c = (j // 2) % 2 * 512
                    for t in range(TT):
                        evac(7 + j - 1 + t, G_GLA + 4 + j, (gl_v if j < 4 else gl_r)[:, t, c:c + 512], gl_u.freed,
                             after=7 if j == 1 and t == 0 else None)
            for t in range(TT):
                act.wait_ge(gl_u.freed, 15)
                A(gl_r[:, t, :], gl_r[:, t, :], ACT.Silu).then_inc(gl_sl, 1)
            for t in range(TT):
                act.wait_ge(gl_o, t + 1)
                junk = (gl_c, gl_w[0])[t]
                for hd in range(GLA_HEADS):
                    r = A(junk[:, hd, :], ps[:, 4 + 2 * t + hd // 2, (hd % 2) * T:(hd % 2 + 1) * T], ACT.Square,
                          accum_out=ss8[:, 4 * t + hd:4 * t + hd + 1])
                r.then_inc(gl_s, 1)
            for g in range(4):
                act.wait_ge(gl_tr, g + 1)
                A(y_hi[:, 2 * g:2 * g + 2, :], ps[:, g, :].rearrange("p (a t) -> p a t", t=T), ACT.Copy).then_inc(gl_ya, 1)
            for i in range(4):
                refill(G_GLA + 12 + i)
            sumsq(6)
            act.dma_start(tab[:, :], tables[3]).then_inc(tab_in, 16)
            act.dma_start(rowg[:, :], rows[2:3, :].partition_broadcast(P)).then_inc(row_in, 16)
            norm_tiles(6)
            ffn(0)
            norm(7)
            for u in range(2):
                act.wait_ge(done, G_NSA + u + 1)
                for o in range(2):
                    src = ps[64 * o:64 * o + 64, bank(u), :].rearrange("p (a t) -> p a t", t=T)
                    A(ns_raw[0:64, u, o:o + 3:2, :], src, ACT.Copy)
                    r = A(ns_raw[64:128, u, o:o + 3:2, 0:T - 1], src[:, :, 1:T], ACT.Copy)
                r.then_inc(ns_u.freed, 1)
                refill(G_NSA + u)
            for u in range(2, 4):
                evac(u, G_NSA + u, ns_k[:, u - 2, :, :], ns_u.freed)
                refill(G_NSA + u)
            refill(G_NSA + 4)
            for t in range(TT):
                evac(4 + t, G_NSA + 5, ns_v[:, t, :], ns_u.freed)
            for i in range(2):
                act.wait_ge(ns_xf, i + 1)
                A(ns_xh[:, i, :, :], ns_x[:, i, :, :], ACT.Copy).then_inc(ns_xhr, 1)
            refill(G_NSA + 5)
            norm_tiles("7b")
            for i in range(2):
                refill(G_NSA + 6 + 2 * i)
                act.wait_ge(done, G_NSA + 8 + 2 * i)
                x = ps[:, i, 0:128].rearrange("p (c n) -> p c n", n=64)[:, :, 0:60]
                A(ns_h[:, i, :, 0:60], x, ACT.Square).then_inc(ns_sq, 1)
                act.wait_ge(ns_u1, i + 1)
                A(ns_h[:, i, :, 0:60], ns_h[:, i, :, 0:60], ACT.Tanh, scale=0.7978845608028654).then_inc(ns_th, 1)
                refill(G_NSA + 7 + 2 * i)
            for u in range(6, 10):
                evac(u, G_NSA + 4 + u, ns_q[:, 2 * (u - 6):2 * (u - 6) + 2, :], ns_u.freed, scale=0.125)
                refill(G_NSA + 4 + u)
            act.wait_ge(ns_u.freed, 16)
            act.wait_ge(ns_pj, 7)
            A(ns_gate[:, :, :], ps[:, bank(16), 0:128].rearrange("p (t n) -> p t n", n=64)[:, :, 0:48],
              ACT.Sigmoid).then_inc(ns_u.freed, 1)
            act.wait_ge(ns_kv, 1)
            A(ns_kc[:, :, :], ps[:, 2, 0:64], ACT.Copy, scale=0.5).then_inc(ns_kcr, 1)
            act.wait_ge(ns_ci, 1)
            A(ns_cs[:, :, :, :], ns_cs[:, :, :, :], ACT.Exp).then_inc(ns_ce, 1)
            act.wait_ge(ns_ct, 1)
            A(ns_cp[:, :, :], ps[:, 7, :], ACT.Copy).then_inc(ns_cc, 1)

            def ns_exp(it):
                act.wait_ge(ns_mx, it + 1)
                for i in range(2):
                    for t in range(2):
                        v = ns_s[:, it % 2, i, P * t:P * t + P * (t + 1)]
                        r = A(v, v, ACT.Exp, bias=ns_m[:, it % 2, i, t:t + 1], accum_out=ns_l[:, it % 2, i, t:t + 1])
                r.then_inc(ns_ex, 1)

            ns_exp(0)
            for it in range(16):
                if it + 1 < 16:
                    ns_exp(it + 1)
                act.wait_ge(ns_tp, it + 1)
                A(ns_p[:, it % 2, :, :], ps[:, 6:8, 0:384], ACT.Copy).then_inc(ns_tc, 1)
            for g in range(4):
                act.wait_ge(ns_ot, g + 1)
                A(y_hi[:, 2 * g:2 * g + 2, :], ps[:, 4 + g, :].rearrange("p (a t) -> p a t", t=T), ACT.Copy)\
                    .then_inc(ns_oa, 1)
            for i in range(4):
                refill(G_NSA + 14 + i)
            norm(8)
            ffn(1)
            sumsq(9)

        @block.vector
        def _(dve):
            V = nc.vector
            steps = [0]

            def link(ins):
                steps[0] += 1
                ins.then_inc(dve_step, 1)
                dve.wait_ge(dve_step, steps[0])

            dve.wait_ge(loaded, 48)

            def mean_square(n):
                dve.wait_ge(ss_ready, 2 * n + 2)
                V.tensor_scalar(msq, ssq, 1.0 / D, EPS, ALU.mult, ALU.add).then_inc(ms_ready, 1)
                dve.wait_ge(rstd_ready, n + 1)

            def lo(g, turn=None, each=0):
                s = g % RING
                dve.wait_ge(hi_ready, plus(g + 1, turn, each))
                V.tensor_tensor(w_lo[:, s, :], ring[:, s, :], w_hi[:, s, :].bitcast(F32), ALU.subtract).then_inc(lo_ready, 1)

            def refill(g, turn=None, each=0):
                if g + RING < G_END:
                    lo(g + RING, turn, each)

            def norm_tiles(n):
                i = XT_OF[n]
                for b in range(4):
                    dve.wait_ge(xT_hi, 4 * i + b + 1)
                    for k in (2 * b, 2 * b + 1):
                        c = S_GAIN + GAIN_OF[n] * KT + k
                        r = V.scalar_tensor_tensor(x_lo[:, k, :], ps[:, 4 + b, (k % 2) * T:(k % 2 + 1) * T],
                                                   sm[:, c:c + 1], x_hi[:, k, :].bitcast(F32), ALU.mult, ALU.subtract)
                    r.then_inc(xT_lo, 1)

            def norm(n):
                mean_square(n)
                for t in range(TT):
                    V.tensor_scalar(xs[:, t, :], h[:, t, :], rstd[:, t:t + 1], None, ALU.mult).then_inc(xs_ready, 1)
                norm_tiles(n)

            def y_pair(i, b, ready):
                V.tensor_tensor(y_lo[:, i:i + 2, :], ps[:, b, :].rearrange("p (a t) -> p a t", t=T),
                                y_hi[:, i:i + 2, :].bitcast(F32), ALU.subtract).then_inc(ready, 1)

            def natural_norm(n, row, dst, ready):
                dve.wait_ge(row_in, 16 * (row + 1))
                mean_square(n)
                for t in range(TT):
                    V.scalar_tensor_tensor(dst[:, t, :], h[:, t, :], rstd[:, t:t + 1], rowg[:, :],
                                           ALU.mult, ALU.mult).then_inc(ready, 1)

            def residual(g):
                dve.wait_ge(done, g + 1)
                for j in range(4):
                    v = h[:, j // 2, (j % 2) * 512:(j % 2 + 1) * 512]
                    V.tensor_tensor(v, ps[:, j, :], v, ALU.add).then_inc(h_ready, 1)

            def mlp(n):
                freed, ready, hh, sq = mlp_s[n]
                st = mlp_h[n]

                def up(c, turn):
                    for u in (2 * c, 2 * c + 1):
                        dve.wait_ge(freed, plus(u + 1, turn, 6))
                        v = relu[:, u % 2, :]
                        V.tensor_tensor(square[:, u % 2, :], v, v, ALU.mult).then_inc(sq, 1)
                        dve.wait_ge(sq, plus(u + 1, turn, 6))
                        dve.wait_ge(hh, plus(u + 1, turn, 6))
                        i = 4 * (c % 3) + 2 * (u % 2)
                        V.tensor_tensor(y_lo[:, i:i + 2, :], square[:, u % 2, :].rearrange("p (a t) -> p a t", t=T),
                                        y_hi[:, i:i + 2, :].bitcast(F32), ALU.subtract).then_inc(ready, 1)
                        refill(st.up(c) + u % 2, turn, st.each)

                def down(c, turn):
                    for i in range(st.dn):
                        refill(st.down(c) + i, turn, st.each)

                st.run(dve, up, down)

            def ffn(n):
                freed, ready, base, tap, sl, pr, hh = ffn_s[n]
                st = ffn_h[n]
                col = S_CONV + n * FFN_TILES * 8

                def par(u, j, turn):
                    c = col + 8 * u + j
                    return sm[:, c:c + 1] if turn is None else sm[:, bass.ds(turn * 48 + c, 1)]

                def up(c, turn):
                    for u in (2 * c, 2 * c + 1):
                        dve.wait_ge(base, plus(u + 1, turn, 6))
                        for e in range(2):
                            v = conv[:, u % 2, e, 1:T]
                            V.scalar_tensor_tensor(v, ps[:, bank(u), e * T:(e + 1) * T - 1], par(u, 2 + e, turn), v,
                                                   ALU.mult, ALU.add).then_inc(tap, 1)
                        dve.wait_ge(tap, plus(2 * u + 2, turn, 12))
                        for e in range(2):
                            v = conv[:, u % 2, e, 2:T]
                            r = V.scalar_tensor_tensor(v, ps[:, bank(u), e * T:(e + 1) * T - 2], par(u, e, turn), v,
                                                       ALU.mult, ALU.add)
                        r.then_inc(freed, 1)
                        refill(st.up(c) + u % 2, turn, st.each)

                def down(c, turn):
                    for i in range(st.dn):
                        refill(st.down(c) + i, turn, st.each)

                st.run(dve, up, down)

            for g in range(RING):
                lo(g)
            dve.wait_ge(n_ready, 1)
            V.tensor_tensor(n_lo[:, :], narrow_raw, n_hi[:, :].bitcast(F32), ALU.subtract).then_inc(n_ready, 1)
            norm(0)

            def banks(p):
                b = 4 + 2 * (p % 2)
                return ps[:, b:b + 2, 0:384]

            def clip(p):
                dve.wait_ge(sbz, p + 1)
                V.tensor_scalar(sb_e[:, p % 2, :, :], banks(p), SOFT_CAP, None, ALU.min).then_inc(sbc, 1)

            def softplus(p):
                dve.wait_ge(sbl, p + 1)
                V.tensor_tensor(sb_s[:, p % 2, :, :], banks(p), sb_e[:, p % 2, :, :], ALU.max).then_inc(sbm, 1)

            def out_copy(p):
                dve.wait_ge(y_h, p + 1)
                V.tensor_tensor(y_lo[:, p, :], ps[:, p % 2, 0:T], y_hi[:, p, :].bitcast(F32), ALU.subtract).then_inc(sbv, 1)

            for g in range(12):
                refill(G_SB + g)
            clip(0)
            clip(1)
            softplus(0)
            for p in range(8):
                if p + 1 < 8:
                    softplus(p + 1)
                if p:
                    out_copy(p - 1)
                if p + 2 < 8:
                    clip(p + 2)
            out_copy(7)
            for i in range(4):
                refill(G_SB + 12 + i)
            residual(G_SB + 15)
            norm(1)
            mlp(0)
            residual(G_MLP[0] + 31)
            norm(2)
            dve.wait_ge(tab_in, 48)
            cos = tab[:, C_COS:C_COS + T].unsqueeze(1).broadcast_to([P, 2, T])
            sin = tab[:, C_SIN:C_SIN + T].unsqueeze(1).broadcast_to([P, 2, T])
            for u in range(8):
                dve.wait_ge(done, G_RET + u + 1)
                if u >= 2:
                    dve.wait_ge(rt_qk, u - 1)
                src = ps[:, bank(u), :].rearrange("p (a t) -> p a t", t=T)
                V.tensor_tensor(rt_c[:, u % 2, :].rearrange("p (a t) -> p a t", t=T), src, cos, ALU.mult)
                V.tensor_tensor(rt_n[:, u % 2, :].rearrange("p (a t) -> p a t", t=T), src, sin, ALU.mult)\
                 .then_inc(rt_u.freed, 1)
                refill(G_RET + u)
            for g in range(8, 24):
                refill(G_RET + g)
            for hd in range(RET_HEADS):
                dve.wait_ge(rt_sc, hd + 1)
                c = 384 * hd
                V.tensor_tensor(rt_s[:, hd, :], ps[:, 4 + hd, 0:384], rt_decay[:, c:c + 384], ALU.mult).then_inc(rt_dec, 1)
            for i in range(8):
                dve.wait_ge(rt_o, i + 1)
                link(V.bn_stats(bn[:, i, :], ps[:, i % 4, :]))
                link(V.bn_aggr(mv[:, i, :], bn[:, i, :]))
                v = rt_g[:, i % 2, (i // 2) * 512:(i // 2 + 1) * 512]
                V.scalar_tensor_tensor(v, ps[:, i % 4, :], mv[:, i, 0:1], v, ALU.subtract, ALU.mult).then_inc(rt_of, 1)
            V.tensor_scalar(ms8, mv[:, :, 1], EPS, None, ALU.add).then_inc(rt_ms, 1)
            for g in range(10):
                if g < 8:
                    dve.wait_ge(rt_ya, g + 1)
                    y_pair(2 * g % 12, 4 + g % 4, rt_yd)
                if g >= 2:
                    refill(G_RET + 24 + g - 2)
            residual(G_RET + 31)
            norm(3)
            mlp(1)
            residual(G_MLP[1] + 31)
            natural_norm(4, 0, h, h_ready)
            norm(5)
            dve.wait_ge(gl_pj, 1)
            V.tensor_copy(gl_nat[:, :, :], ps[:, 4, 0:32].rearrange("p (t n) -> p t n", n=16)).then_inc(gl_u.freed, 1)
            dve.wait_ge(gl_u.freed, 1)
            dve.sem_inc(gl_nt, 1)
            dve.wait_ge(gl_pj, 2)
            V.tensor_copy(gl_low, ps[0:16, 7, 0:T]).then_inc(gl_nt, 1)
            for g in range(4):
                refill(G_GLA + g)
            for i in range(2):
                dve.wait_ge(gl_pj, 3 + i)
                if i == 0:
                    dve.wait_ge(gl_u.freed, 5)
                for j in range(2):
                    c = 2 * i + j
                    r = V.tensor_scalar(gl_x[:, c, :], ps[:, bank(5 + i), j * T:(j + 1) * T],
                                        sm[:, S_BALPHA + c:S_BALPHA + c + 1], -1.0, ALU.add, ALU.mult)
                r.then_inc(gl_u.freed, 1)
            dve.wait_ge(gl_u.freed, 7)
            V.tensor_scalar(gl_l[:, :, :], gl_x[:, :, :], SOFT_CAP, None, ALU.min).then_inc(gl_x_r, 1)
            dve.wait_ge(gl_lg, 1)
            link(V.tensor_tensor(gl_x[:, :, :], gl_x[:, :, :], gl_l[:, :, :], ALU.max))
            link(V.memset(gl_l[:, :, :], 0.0))
            for hd in range(GLA_HEADS):
                r = V.tensor_tensor_scan(gl_c[:, hd, :], gl_x[:, hd, :], gl_l[:, hd, :], 0.0, ALU.add, ALU.add)
            link(r)
            for t in range(TT):
                r = V.memset(gl_a[t][:, :, :], 0.0)
            link(r)
            flat = gl_c[:, :, :].rearrange("p a t -> p (a t)")

            def level(v, j):
                n = 2 << j
                return v.rearrange("p a t -> p (a t)").rearrange("p (b n) -> p b n", n=n)

            for j in range(8):
                n = 2 << j
                c = flat.rearrange("p (b n) -> p b n", n=n)
                V.tensor_tensor(level(gl_w[j], j), c, c[:, :, n // 2 - 1:n // 2].broadcast_to([P, 4 * T // n, n]),
                                ALU.subtract).then_inc(gl_df, 1)
                if j == 3:
                    refill(G_GLA + 4)
            for j in range(8):
                n = 2 << j
                dve.wait_ge(gl_ex, j + 1)
                w = level(gl_w[j], j)
                V.tensor_tensor(w[:, :, 0:n // 2], w[:, :, 0:n // 2], level(gl_k, j)[:, :, 0:n // 2], ALU.mult)
                V.tensor_tensor(w[:, :, n // 2:n], w[:, :, n // 2:n], level(gl_q, j)[:, :, n // 2:n],
                                ALU.mult).then_inc(gl_wr, 1)
                if j < 7:
                    refill(G_GLA + 5 + j)
            dve.wait_ge(tab_in, 64)
            for i in range(16):
                l, t = i // 2, i % 2
                dve.wait_ge(gl_lv, i + 1)
                if i >= 2:
                    dve.wait_ge(gl_cp, i - 1)
                m = tab[:, C_LEVEL + l * P:C_LEVEL + (l + 1) * P].bitcast(I32).unsqueeze(1).broadcast_to([P, 4, P])
                V.copy_predicated(gl_a[t][:, :, :], m, ps[:, i % 4, :].rearrange("p (a t) -> p a t", t=P))\
                 .then_inc(gl_cp, 1)
            dve.wait_ge(gl_lv, 17)
            V.tensor_copy(gl_across, ps[:, 0, :].rearrange("p (a t) -> p a t", t=P)).then_inc(gl_cp, 1)
            dve.wait_ge(gl_s, 2)
            V.tensor_scalar(ms8, ss8, 1.0 / 256, EPS, ALU.mult, ALU.add).then_inc(gl_m, 1)
            dve.wait_ge(gl_p, 1)
            for t in range(TT):
                dve.wait_ge(gl_rg, t + 1)
                for hd in range(GLA_HEADS):
                    v = gl_r[:, t, hd * 256:(hd + 1) * 256]
                    r = V.scalar_tensor_tensor(v, ps[:, 4 + 2 * t + hd // 2, (hd % 2) * T:(hd % 2 + 1) * T],
                                               rs8[:, 4 * t + hd:4 * t + hd + 1], v, ALU.mult, ALU.mult)
                r.then_inc(gl_yr, 1)
            for g in range(4):
                dve.wait_ge(gl_ya, g + 1)
                y_pair(2 * g, g, gl_yd)
            for i in range(4):
                refill(G_GLA + 12 + i)
            residual(G_GLA + 15)
            norm(6)
            ffn(0)
            residual(G_FFN[0] + 32)
            norm(7)
            link(V.memset(ns_h[:, 2:4, :, :], 0.0))
            dve.wait_ge(tab_in, 80)
            for g in range(4):
                refill(G_NSA + g)
            for i in range(2):
                dve.wait_ge(ns_u.freed, i + 1)
                for l in range(16):
                    o = ns_x[:, i, l, :].rearrange("p (a n) -> p a n", n=15)
                    pe_ = sm[:, S_PE + 16 * i + l:S_PE + 16 * i + l + 1]
                    r = V.tensor_scalar(o, ns_raw[:, i, :, 2 * l:2 * l + 16 * 14 + 1:16], pe_, None, ALU.add)
                r.then_inc(ns_xf, 1)
            refill(G_NSA + 4)
            for i in range(2):
                dve.wait_ge(ns_xhr, i + 1)
                V.tensor_tensor(ns_xl[:, i, :, :], ns_x[:, i, :, :], ns_xh[:, i, :, :].bitcast(F32), ALU.subtract)\
                 .then_inc(ns_xr, 1)
            refill(G_NSA + 5)
            norm_tiles("7b")
            for i in range(2):
                x = ps[:, i, 0:128].rearrange("p (c n) -> p c n", n=64)[:, :, 0:60]
                a = ns_h[:, i, :, 0:60]
                refill(G_NSA + 6 + 2 * i)
                dve.wait_ge(ns_sq, i + 1)
                link(V.tensor_scalar(a, a, 0.044715, 1.0, ALU.mult, ALU.add))
                V.tensor_tensor(a, x, a, ALU.mult).then_inc(ns_u1, 1)
                dve.wait_ge(ns_th, i + 1)
                o = ns_h[:, 2 + i, :, :].rearrange("p c (a n) -> p c a n", n=CMP)
                for c in range(2):
                    r = V.scalar_tensor_tensor(o[:, c, :, 0:15], ns_h[:, i, c, 0:60].rearrange("p (a n) -> p a n", n=15),
                                               1.0, ps[:, i, c * 64:c * 64 + 60].rearrange("p (a n) -> p a n", n=15),
                                               ALU.add, ALU.mult)
                r.then_inc(ns_hr, 1)
                refill(G_NSA + 7 + 2 * i)
            dve.wait_ge(ns_hr, 2)
            for g in range(2):
                for c in range(2):
                    src = ns_h[:, 3, c, :].rearrange("p (a n) -> p a n", n=CMP)[:, 2 * g:2 * g + 2, :]
                    dst = ns_hv[:, g, c, :].rearrange("p (a b n) -> p a b n", b=4, n=CMP)
                    r = V.tensor_copy(dst, src.unsqueeze(2).broadcast_to([P, 2, 4, CMP]))
            r.then_inc(ns_hr, 1)
            rcos = tab[:, C_RCOS:C_RCOS + T].unsqueeze(1).broadcast_to([P, 2, T])
            rsin = tab[:, C_RSIN:C_RSIN + T].unsqueeze(1).broadcast_to([P, 2, T])
            for g in range(10, 14):
                refill(G_NSA + g)
            dve.wait_ge(ns_u.freed, 10)
            for i in range(6):
                raw = ns_k[:, i, :, :] if i < 2 else ns_q[:, 2 * (i - 2):2 * (i - 2) + 2, :]
                link(V.tensor_tensor(ns_t1[:, :, :], raw, rcos, ALU.mult))
                dve.wait_ge(ns_pj, i + 1)
                V.tensor_tensor(ns_t2[:, :, :], ps[:, bank(10 + i), :].rearrange("p (a t) -> p a t", t=T), rsin,
                                ALU.mult).then_inc(ns_u.freed, 1)
                dve.wait_ge(ns_u.freed, 11 + i)
                if i < 2:
                    for o in range(2):
                        for d in range(2):
                            r = V.tensor_tensor(ns_kd[64 * d:64 * d + 64, i, o:o + 3:2, :],
                                                ns_t1[64 * o:64 * o + 64, :, :], ns_t2[64 * o:64 * o + 64, :, :], ALU.add)
                    r.then_inc(ns_kdr, 1)
                    dve.wait_ge(ns_kdr, i + 1)
                else:
                    V.tensor_tensor(ns_qr[:, 2 * (i - 2):2 * (i - 2) + 2, :], ns_t1[:, :, :], ns_t2[:, :, :],
                                    ALU.add).then_inc(ns_qrr, 1)
                    dve.wait_ge(ns_qrr, i - 1)
            dve.wait_ge(ns_kv, 2)
            for g in range(2):
                V.tensor_tensor(ns_vbd[:, g, :, :], ps[:, 3, g * 64:(g + 1) * 64].unsqueeze(1).broadcast_to([P, 8, 64]),
                                tab[:, C_BD:C_BD + 8].unsqueeze(2).broadcast_to([P, 8, 64]), ALU.mult).then_inc(ns_vr, 1)
            dve.wait_ge(ns_cq, 1)
            c3 = ns_cs[:, :, :, :].rearrange("p t h n -> p (t h) n")

            def cmask(c, t):
                return tab[:, c + t * CMP:c + (t + 1) * CMP].unsqueeze(1)

            for t in range(TT):
                for o in range(2):
                    r = V.tensor_tensor(ns_cs[:, t, o:16:2, :],
                                        ps[:, 6 - o, t * P:(t + 1) * P].rearrange("p (h n) -> p h n", n=CMP),
                                        cmask(C_CADD, t).broadcast_to([P, 8, CMP]), ALU.add)
            link(r)
            cm = ns_cm[:, :, :].rearrange("p t h -> p (t h)")
            cl = ns_cl[:, :, :].rearrange("p t h -> p (t h)")
            link(V.tensor_reduce(cm, c3, AX.X, ALU.max))
            V.tensor_tensor(c3, c3, cm.unsqueeze(2).broadcast_to([P, 32, CMP]), ALU.subtract).then_inc(ns_ci, 1)
            dve.wait_ge(ns_ce, 1)
            link(V.tensor_reduce(cl, c3, AX.X, ALU.add))
            link(V.reciprocal(cl, cl))
            link(V.tensor_tensor(ns_cl[:, :, :], ns_cl[:, :, :], ns_gate[:, :, 0:16], ALU.mult))
            for t in range(TT):
                r = V.tensor_tensor(ns_cs[:, t, :, :], ns_cs[:, t, :, :], cmask(C_CMUL, t).broadcast_to([P, 16, CMP]),
                                    ALU.mult)
            link(r)
            V.tensor_tensor(c3, c3, cl.unsqueeze(2).broadcast_to([P, 32, CMP]), ALU.mult).then_inc(ns_cpr, 1)

            def ns_scores(it):
                dve.wait_ge(ns_qk, it + 1)
                if it >= 2:
                    dve.wait_ge(ns_tp, it - 1)
                s = ns_s[:, it % 2, :, :]
                V.tensor_tensor(s, ps[:, 4:6, 0:384],
                                tab[:, C_CAUSAL:C_CAUSAL + 384].unsqueeze(1).broadcast_to([P, 2, 384]), ALU.add)\
                 .then_inc(ns_add, 1)
                dve.wait_ge(ns_add, it + 1)
                for t in range(2):
                    r = V.tensor_reduce(ns_m[:, it % 2, :, t], s[:, :, P * t:P * t + P * (t + 1)], AX.X, ALU.max,
                                        negate=True)
                r.then_inc(ns_mx, 1)

            ns_scores(0)
            for it in range(16):
                if it + 1 < 16:
                    ns_scores(it + 1)
                dve.wait_ge(ns_ex, it + 1)
                l, f = ns_l[:, it % 2, :, :], ns_f[:, it % 2, :, :]
                link(V.reciprocal(f, l))
                br, pr = it // 8, it % 8
                g = ns_gate[:, :, 16 * (br + 1) + 2 * pr:16 * (br + 1) + 2 * pr + 2].rearrange("p t h -> p h t")
                V.tensor_tensor(f, f, g, ALU.mult).then_inc(ns_co, 1)
            dve.wait_ge(ns_o, 1)
            for j in range(4):
                V.tensor_copy(ns_on[:, j // 2, (j % 2) * 512:(j % 2 + 1) * 512], ps[:, j, :]).then_inc(ns_oc, 1)
            for g in range(4):
                dve.wait_ge(ns_oa, g + 1)
                y_pair(2 * g, 4 + g, ns_od)
            for i in range(4):
                refill(G_NSA + 14 + i)
            residual(G_NSA + 17)
            norm(8)
            ffn(1)
            residual(G_FFN[1] + 32)
            natural_norm(9, 2, xs, xs_ready)


def constants():
    f = np.float32
    c = np.zeros((4, P, TAB), f)
    decay = np.zeros((P, DECAY), f)
    i = np.arange(P)
    c[0, :, C_NTRI:C_NTRI + P] = np.where(i[:, None] >= i[None, :], -1.0, 0.0)
    c[0, :, C_NONE:C_NONE + P] = -1.0
    pos = np.arange(T, dtype=f)
    inv = (f(1.0) / (f(10000.0) ** np.linspace(0.0, 1.0, P, dtype=f))).astype(f)
    ang = (inv[:, None] * pos[None, :]).astype(f)
    c[1, :, C_COS:C_COS + T], c[1, :, C_SIN:C_SIN + T] = np.cos(ang), np.sin(ang)
    lg = np.log1p(-np.exp2(-5.0 - np.arange(RET_HEADS)))
    for hd in range(RET_HEADS):
        for n, (s0, t0, w) in enumerate(((0, 0, T), (P, P, P))):
            rel = (t0 + np.arange(w))[None, :] - (s0 + i)[:, None]
            dec = np.where(rel >= 0, np.exp(lg[hd] * np.maximum(rel, 0)), 0.0) * 256 ** -0.5
            decay[:, 384 * hd + n * T:384 * hd + n * T + w] = dec
    c[2, :, C_LEVEL:C_LEVEL + P] = np.eye(P)
    for l in range(1, 8):
        m = 1 << l
        same = i[:, None] // m == i[None, :] // m
        c[2, :, C_LEVEL + l * P:C_LEVEL + (l + 1) * P] = same & (i[:, None] % m < m // 2) & (i[None, :] % m >= m // 2)
    inv = (f(10000.0) ** (-np.arange(32, dtype=f) / f(32))).astype(f)
    ang = (inv[i % 32][:, None] * pos[None, :]).astype(f)
    c[3, :, C_RCOS:C_RCOS + T] = np.cos(ang)
    c[3, :, C_RSIN:C_RSIN + T] = np.sin(ang) * np.where(i % 64 < 32, -1.0, 1.0)[:, None]
    partner = np.where(i % 64 < 32, i + 32, i - 32)
    c[3, partner, C_SWAP + i] = 1.0
    causal = np.where(i[None, :] <= i[:, None], 0.0, NEG)
    c[3, :, C_CAUSAL:C_CAUSAL + P] = causal
    c[3, :, C_CAUSAL + T:C_CAUSAL + 384] = causal
    n = np.arange(CMP)
    for t in range(TT):
        ok = (n[None, :] * 16 + 31 <= (t * P + i)[:, None]) & (n[None, :] < CMP - 1)
        c[3, :, C_CADD + t * CMP:C_CADD + (t + 1) * CMP] = np.where(ok, 0.0, NEG)
        c[3, :, C_CMUL + t * CMP:C_CMUL + (t + 1) * CMP] = ok
    c[3, :, C_BD:C_BD + 8] = 0.5 * (i[:, None] // CMP == np.arange(8)[None, :])
    return c, decay


def kernel(**inputs):
    import concourse.bacc as bacc
    from concourse.bass_utils import run_bass_kernel_spmd

    a = {k: np.asarray(v) for k, v in inputs.items()}

    ws = []

    def cols(w, c):
        ws.append(w[:, c].reshape(KT, P, 256).transpose(1, 0, 2).reshape(P, PIECE))

    def both(w, c0):
        for r in (0, 512):
            ws.append(w[r:r + 512, c0:c0 + 512].reshape(4, P, 512).transpose(1, 0, 2).reshape(P, PIECE))

    def rows_(w, r):
        ws.append(w[r:r + 256].reshape(2, P, D).transpose(1, 0, 2).reshape(P, PIECE))

    def hidden(up, down, chunks, dn):
        def down_(c):
            for i in range(dn):
                rows_(down, 256 * (dn * c + i))
        for c in range(chunks):
            for ix in up(c):
                cols(*ix)
            if c:
                down_(c - 1)
        down_(chunks - 1)

    def mlp(n):
        w = a["w_mlp_up"][n]
        hidden(lambda c: [(w, slice(512 * c + 256 * i, 512 * c + 256 * (i + 1))) for i in range(2)],
               a["w_mlp_down"][n], MLP_C, 2)

    def ffn(n):
        w, f = a["ffn_w_up_2"][n], FFN_TILES * P
        hidden(lambda c: [(w, np.concatenate([s * f + u * P + np.arange(P) for s in range(2)]))
                          for u in (2 * c, 2 * c + 1)], a["ffn_w_down_2"][n], FFN_C, 1)

    def mixer(w, n_cols, n_both, out):
        for j in range(n_cols):
            cols(w, slice(256 * j, 256 * (j + 1)))
        for j in range(n_both):
            both(w, 256 * n_cols + 512 * j)
        for r in range(0, out.shape[0], 256):
            rows_(out, r)

    mixer(a["w_sb_in"][0], 8, 2, a["w_sb_out"][0])
    mlp(0)
    mixer(a["w_ret_in"][0], 8, 8, a["w_ret_out"][0])
    mlp(1)
    mixer(a["gla_w_in_2"][0], 4, 4, a["gla_w_o_2"][0])
    ffn(0)
    kv, win = a["nsa_w_kv_2"], a["nsa_w_in_2"][0]
    for j in (0, 1, 2, 4):
        cols(kv, slice(256 * j, 256 * (j + 1)))
    both(np.concatenate([kv[:, 256 * 3:256 * 4], kv[:, 256 * 5:256 * 6]], 1), 0)
    for w in (a["cmp_k_w1_2"], a["cmp_v_w1_2"]):
        for r in (0, 1024):
            ws.append(w[r:r + 1024].reshape(8, P, 256).transpose(1, 0, 2).reshape(P, PIECE))
    for j in range(4):
        cols(win, slice(256 * j, 256 * (j + 1)))
    for r in range(0, D, 256):
        rows_(a["nsa_w_o_2"][0], r)
    ffn(1)
    ws = np.stack(ws)
    assert len(ws) == G_END

    small = np.zeros((P, S_TOTAL), np.float32)
    for g, v in enumerate((a["g_mix"][0], a["g_mlp"][0], a["g_mix"][1], a["g_mlp"][1], a["norm_mix_2"][0],
                           a["norm_ffn_2"][0], a["kv_norm_2"], a["norm_mix_2"][1], a["norm_ffn_2"][1])):
        small[:, S_GAIN + g * KT:S_GAIN + (g + 1) * KT] = v.reshape(KT, P).T
    for n in range(2):
        taps = np.concatenate([a["ffn_conv_w_2"][n], a["ffn_conv_b_2"][n][None]], 0)
        v = taps.reshape(4, 2, FFN_TILES, P).transpose(3, 2, 0, 1).reshape(P, FFN_TILES * 8)
        small[:, S_CONV + n * FFN_TILES * 8:S_CONV + (n + 1) * FFN_TILES * 8] = v
    small[:, S_BALPHA:S_BALPHA + 4] = a["gla_b_alpha_2"][0].reshape(4, P).T
    w2 = a["cmp_k_w2_2"].reshape(2, P, 64).transpose(1, 0, 2)
    small[:, S_W2K:S_W2V] = np.concatenate([w2, w2], 2).reshape(P, -1)
    small[:, S_W2V:S_PE] = a["cmp_v_w2_2"].reshape(2, P, 64).transpose(1, 0, 2).reshape(P, -1)
    small[:, S_PE:S_PE + 16] = a["cmp_pe_k_2"].reshape(16, P).T
    small[:, S_PE + 16:S_PE + 32] = a["cmp_pe_v_2"].reshape(16, P).T
    small[0:16, S_ALPHA:S_ALPHA + 512] = a["gla_w_alpha_up_2"][0]
    small[:, S_ID:S_ID + P] = np.eye(P)
    narrow = np.concatenate([a["gla_w_in_2"][0][:, 3072:3088].reshape(KT, P, 16).transpose(1, 0, 2).reshape(P, -1),
                             win[:, D:D + 48].reshape(KT, P, 48).transpose(1, 0, 2).reshape(P, -1)], 1)
    rows = np.stack([a["g_final"], a["gla_norm_2"][0].reshape(D), a["norm_final_2"]])

    tables, decay = constants()
    arrays = {"ws": ws, "small": small, "narrow": narrow, "tables": tables, "decay": decay, "rows": rows,
              "x": np.ascontiguousarray(a["x"][0])}
    nc = bacc.Bacc("TRN2", target_bir_lowering=False, num_devices=1)
    aps = {k: nc.dram_tensor(k, v.shape, mybir.dt.from_np(v.dtype), kind="ExternalInput").ap()
           for k, v in arrays.items()}
    out = nc.dram_tensor("out", (T, D), F32, kind="ExternalOutput").ap()
    build(nc, aps["ws"], aps["small"], aps["narrow"], aps["tables"], aps["decay"], aps["rows"], aps["x"], out)
    r = run_bass_kernel_spmd(nc, [arrays], core_ids=[0])
    return r.results[0]["out"].reshape(1, T, D)
```

```python
import numpy as np
import concourse.bass as bass
from concourse import mybir

F32 = mybir.dt.float32
F32R = mybir.dt.float32r
I32 = mybir.dt.int32
ALU = mybir.AluOpType
ACT = mybir.ActivationFunctionType
AX = mybir.AxisListType

T = 256
D = 1024
P = 128
TT = T // P
KT = D // P
PIECE = 2048
RING = 3
EPS = 1e-6
NEG = -1e30
SB_HEADS, RET_HEADS, GLA_HEADS, NSA_HEADS, NSA_KV = 16, 4, 4, 16, 4
MLP_C = 4 * D // 512
FFN_TILES = 2816 // P
FFN_C = FFN_TILES // 2
CMP = 16
SOFT_CAP = 30.0

GAINS = 9
S_GAIN = 0
S_CONV = S_GAIN + GAINS * KT
S_BALPHA = S_CONV + 2 * FFN_TILES * 8
S_W2K = S_BALPHA + 4
S_W2V = S_W2K + 2 * P
S_PE = S_W2V + 2 * 64
S_ALPHA = S_PE + 2 * 16
S_ID = S_ALPHA + 512
S_TOTAL = S_ID + P
N_LOW = KT * 16
N_GATE = KT * 48
N_TOTAL = N_LOW + N_GATE + 80

TAB = 1100
C_NTRI, C_NONE = 0, P
C_COS, C_SIN = 0, T
C_LEVEL = 0
C_RCOS, C_RSIN, C_SWAP, C_CAUSAL = 0, T, 2 * T, 2 * T + P
C_CADD = C_CAUSAL + 384
C_CMUL = C_CADD + TT * CMP
C_BD = C_CMUL + TT * CMP
DECAY = RET_HEADS * 384

G_SB = 0
G_MLP = (16, 80)
G_RET = 48
G_GLA = 112
G_FFN = (128, 179)
G_NSA = 161
G_END = 212
ARENA = 17408


def build(nc, ws, small, narrow, tables, decay, rows, x_in, out):
    from contextlib import ExitStack
    ctx = ExitStack()
    with ctx:
        def sb(name, shape, dt=F32):
            return ctx.enter_context(nc.sbuf_tensor(name, shape, dt))

        def sem(name):
            return ctx.enter_context(nc.semaphore(name))

        ring = sb("ring", [P, RING, PIECE])
        w_hi, w_lo = sb("w_hi", [P, RING, PIECE], F32R), sb("w_lo", [P, RING, PIECE], F32R)
        h = sb("h", [P, TT, D])
        x_hi, x_lo = sb("x_hi", [P, KT, T], F32R), sb("x_lo", [P, KT, T], F32R)
        y_hi, y_lo = sb("y_hi", [P, 12, T], F32R), sb("y_lo", [P, 12, T], F32R)
        n_hi, n_lo = sb("n_hi", [P, N_TOTAL], F32R), sb("n_lo", [P, N_TOTAL], F32R)
        sm = sb("sm", [P, S_TOTAL])
        tab = sb("tab", [P, TAB])
        rowg = sb("rowg", [P, D])
        stat = sb("stat", [P, 96])
        power = sb("power", [P, 16])
        arena = sb("arena", [P, ARENA])
        ps = ctx.enter_context(nc.psum_tensor("ps", [P, 8, 512], F32))

        ident = sm[:, S_ID:S_ID + P]
        ssq, msq, rstd = stat[:, 0:2], stat[:, 2:4], stat[:, 4:6]
        ss8, ms8, rs8 = stat[:, 8:16], stat[:, 16:24], stat[:, 24:32]
        mv = stat[:, 32:48].rearrange("p (i c) -> p i c", c=2)
        bn = stat[:, 48:96].rearrange("p (i c) -> p i c", c=6)

        def region(at, *dims):
            n = int(np.prod(dims))
            assert at + n <= ARENA, (at, n)
            v = arena[:, at:at + n]
            if len(dims) == 2:
                v = v.rearrange("p (a b) -> p a b", b=dims[1])
            if len(dims) == 3:
                v = v.rearrange("p (a b c) -> p a b c", b=dims[1], c=dims[2])
            return v

        xs = region(0, TT, D)
        narrow_raw = region(2048, N_TOTAL)
        relu, square = region(2048, 2, 512), region(5120, 2, 512)
        conv = region(3072, 2, 2, T)
        silu, prod = region(4096, 2, T), region(4608, 2, T)
        sb_q, sb_k, sb_v = region(0, KT, T), region(2048, KT, T), region(4096, TT, D)
        sb_e = region(8192, 3 * 2, 384).rearrange("p (s i) n -> p s i n", i=2)
        sb_s, sb_a = region(10496, 2, 2, 384), region(12032, 2, 2, 384)
        rt_q, rt_k = region(0, KT, T), region(2048, KT, T)
        rt_v, rt_g = region(4096, TT, 2 * D), region(8192, TT, 2 * D)
        rt_s = region(12288, RET_HEADS, 384)
        rt_c, rt_n = region(13824, 2, 512), region(14848, 2, 512)
        rt_decay = region(15872, DECAY)
        gl_q, gl_k = region(0, 4, T), region(1024, 4, T)
        gl_v, gl_r = region(2048, TT, D), region(4096, TT, D)
        gl_c, gl_x, gl_l = region(6144, 4, T), region(7168, 4, T), region(8192, 4, T)
        gl_w = [region(9216 + 1024 * j, 4, T) for j in range(8)]
        gl_a = [region(8192, 4, P), region(8192 + 512, 4, P)]

        def gl_level(v, j):
            return v.rearrange("p a t -> p (a t)").rearrange("p (b n) -> p b n", n=2 << j)

        gl_across = gl_x[:, 0:2, :].rearrange("p a (b c) -> p (a b) c", c=P)
        gl_low = gl_l[0:16, 0, :]
        ns_raw = region(2048, 2, NSA_KV, T)
        ns_x = region(4096, 2, 16, 60)
        ns_t2 = region(4096, 2, T)
        ns_s = region(4096, 3 * 2, 384).rearrange("p (s i) n -> p s i n", i=2)
        ns_h = region(3200, 4, 2, 64)
        ns_hv = region(2560, 2, 2, P)
        ns_kc = region(3072, NSA_KV, 2 * CMP)
        ns_gate = region(7104, TT, 48)
        ns_m = region(7200, 2, 2, 2)
        ns_l = region(7208, 2, 2, 2)
        ns_f = region(7216, 2, 2, 2)
        ns_cm, ns_cl = region(7232, TT, 16), region(7264, TT, 16)
        ns_vbd = region(7296, 2, 8, 64)
        ns_kd = region(8320, 2, NSA_KV, T), region(0, 2, NSA_KV, T)
        ns_v = region(10368, TT, 512)
        ns_q, ns_qr = region(11392, KT, T), region(13440, KT, T)
        ns_k, ns_t1 = region(15488, 2, 2, T), region(4608, 2, 2, T)
        ns_p = region(15488, 2, 2, 384)
        ns_cs, ns_cp = region(2048, TT, 16, CMP), region(2560, 4, P)
        ns_pre, ns_gt = region(7296, 2, T), region(7808, T)
        ns_xh = y_hi[:, 0:8, :].rearrange("p a t -> p (a t)")[:, 0:1920].rearrange("p (i l n) -> p i l n", i=2, n=60)
        ns_xl = y_lo[:, 0:8, :].rearrange("p a t -> p (a t)")[:, 0:1920].rearrange("p (i l n) -> p i l n", i=2, n=60)
        ns_xhf, ns_xlf = (y[:, 0:8, :].rearrange("p a t -> p (a t)") for y in (y_hi, y_lo))

        loaded, narrow_in = sem("small_loaded"), sem("narrow_loaded")
        x_loaded = [sem(f"x_loaded{t}") for t in range(TT)]
        half_done = sem("first_token_tile_done")
        tab_in, row_in = sem("tables_loaded"), sem("row_loaded")
        weights_in = [sem(f"weights_in{s}") for s in range(RING)]
        hi_ready, lo_ready = sem("piece_hi"), sem("piece_lo")
        done = sem("piece_done")
        n_ready = sem("narrow_split")
        ss_ready, ms_ready, rstd_ready = sem("sumsq_ready"), sem("meansq_ready"), sem("rstd_ready")
        xs_ready, xt_done = sem("xs_ready"), sem("norm_transposed")
        xT_hi, xT_lo = sem("xT_hi"), sem("xT_lo")
        h_ready = sem("h_ready")
        pow_ready = sem("power_ready")
        act_step, dve_step = sem("act_step"), sem("dve_step")
        stored = sem("stored")

        def bank(u):
            return 4 + u % 3

        def plus(n, turn, each):
            return n if turn is None else turn * each + n

        class Hidden:
            def __init__(self, g0, chunks, dn, rounds):
                self.g0, self.chunks, self.dn, self.rounds = g0, chunks, dn, rounds

            def up(self, c):
                return self.g0 + (2 * c if c < 2 else 4 + self.dn + (c - 2) * (2 + self.dn))

            def down(self, c):
                return self.g0 + 4 if c == 0 else self.g0 + 4 + self.dn + (c - 1) * (2 + self.dn) + \
                    (2 if c < self.chunks - 1 else 0)

            def run(self, eng, up, down):
                up(0, None)
                up(1, None)
                down(0, None)
                with eng.Fori(0, self.rounds) as turn:
                    for c in range(2, 5):
                        up(c, turn)
                        down(c - 1, turn)
                for c in range(2 + 3 * self.rounds, self.chunks):
                    up(c, None)
                    down(c - 1, None)
                down(self.chunks - 1, None)

            @property
            def each(self):
                return 3 * (2 + self.dn)

        mlp_h = [Hidden(g, MLP_C, 2, 2) for g in G_MLP]
        ffn_h = [Hidden(g, FFN_C, 1, 3 - n) for n, g in enumerate(G_FFN)]

        H_AT = [0, 4, 8, 12, 16, 18, 22, 26, 30, 34]
        XS_OF = {0: 0, 1: 1, 2: 2, 3: 3, 5: 4, 6: 5, 7: 6, 8: 7}
        XT_OF = {0: 0, 1: 1, 2: 2, 3: 3, 5: 4, 6: 5, 7: 6, "7b": 7, 8: 8}
        WARM = {1: 2, 2: 2, 3: 2, 5: 7, 6: 2, 7: 2, 8: 2}
        GAIN_OF = {0: 0, 1: 1, 2: 2, 3: 3, 5: 4, 6: 5, 7: 6, "7b": 7, 8: 8}

        sb_freed, ret_freed, gla_freed, nsa_freed = sem("sb_freed"), sem("ret_freed"), sem("gla_freed"), sem("nsa_freed")
        sb_z = sem("sb_z")
        sb_clipped = sem("sb_clipped")
        sb_exp = sem("sb_exp")
        sb_log = sem("sb_log")
        sb_softplus = sem("sb_softplus")
        sb_masked = sem("sb_masked")
        sb_summed = sem("sb_summed")
        sb_weights = sem("sb_weights")
        sb_wmasked = sem("sb_wmasked")
        sb_out = sem("sb_out")
        sb_out_copied = sem("sb_out_copied")
        sb_out_hi = sem("sb_out_hi")
        ret_qk = sem("ret_qk")
        ret_scores = sem("ret_scores")
        ret_decayed = sem("ret_decayed")
        ret_o = sem("ret_o")
        ret_o_free = sem("ret_o_free")
        ret_var = sem("ret_var")
        ret_rstd = sem("ret_rstd")
        ret_y = sem("ret_y")
        ret_transposed = sem("ret_transposed")
        ret_yT_hi = sem("ret_yT_hi")
        ret_yT_lo = sem("ret_yT_lo")
        gla_small_proj = sem("gla_small_proj")
        gla_logit = sem("gla_logit")
        gla_exp = sem("gla_exp")
        gla_log = sem("gla_log")
        gla_diff = sem("gla_diff")
        gla_decay = sem("gla_decay")
        gla_w = sem("gla_w")
        gla_level = sem("gla_level")
        gla_level_copied = sem("gla_level_copied")
        gla_o = sem("gla_o")
        gla_sumsq = sem("gla_sumsq")
        gla_meansq = sem("gla_meansq")
        gla_rstd = sem("gla_rstd")
        gla_y = sem("gla_y")
        gla_transposed = sem("gla_transposed")
        gla_yT_hi = sem("gla_yT_hi")
        gla_yT_lo = sem("gla_yT_lo")
        gla_gate = sem("gla_gate")
        gla_softplus = sem("gla_softplus")
        gla_tree_zero = sem("gla_tree_zero")
        gla_w_keys = sem("gla_w_keys")
        gla_silu = sem("gla_silu")
        nsa_blocks_f32 = sem("nsa_blocks_f32")
        nsa_blocks_hi = sem("nsa_blocks_hi")
        nsa_kd_zero = sem("nsa_kd_zero")
        nsa_cos_product = sem("nsa_cos_product")
        nsa_cmp_scores_copied = sem("nsa_cmp_scores_copied")
        nsa_inner_hidden = sem("nsa_inner_hidden")
        nsa_gates_transposed = sem("nsa_gates_transposed")
        nsa_small_proj = sem("nsa_small_proj")
        nsa_blocks = sem("nsa_blocks")
        nsa_hidden = sem("nsa_hidden")
        nsa_square = sem("nsa_square")
        nsa_inner = sem("nsa_inner")
        nsa_tanh = sem("nsa_tanh")
        nsa_gelu = sem("nsa_gelu")
        nsa_cmp_kv = sem("nsa_cmp_kv")
        nsa_kc = sem("nsa_kc")
        nsa_vbd = sem("nsa_vbd")
        nsa_roped = sem("nsa_roped")
        nsa_kd = sem("nsa_kd")
        nsa_cmp_scores = sem("nsa_cmp_scores")
        nsa_cmp_shifted = sem("nsa_cmp_shifted")
        nsa_cmp_exp = sem("nsa_cmp_exp")
        nsa_cmp_p = sem("nsa_cmp_p")
        nsa_cmp_pT = sem("nsa_cmp_pT")
        nsa_cmp_pT_copied = sem("nsa_cmp_pT_copied")
        nsa_scores = sem("nsa_scores")
        nsa_masked = sem("nsa_masked")
        nsa_max = sem("nsa_max")
        nsa_exp = sem("nsa_exp")
        nsa_coef = sem("nsa_coef")
        nsa_p = sem("nsa_p")
        nsa_pT = sem("nsa_pT")
        nsa_pT_copied = sem("nsa_pT_copied")
        nsa_o = sem("nsa_o")
        nsa_oT_hi = sem("nsa_oT_hi")
        nsa_oT_lo = sem("nsa_oT_lo")
        mlp_s = [(sem(f"mlp{i}_freed"), sem(f"mlp{i}_hidden"), sem(f"mlp{i}_hi"), sem(f"mlp{i}_square")) for i in range(2)]
        ffn_s = [(sem(f"ffn{i}_freed"), sem(f"ffn{i}_hidden"), sem(f"ffn{i}_base"), sem(f"ffn{i}_tap"),
                  sem(f"ffn{i}_silu"), sem(f"ffn{i}_product"), sem(f"ffn{i}_hi")) for i in range(2)]

        block = ctx.enter_context(nc.Block())

        @block.sync
        def _(sp):
            for t in range(TT):
                sp.dma_start(h[:, t, :], x_in[t * P:(t + 1) * P, :]).then_inc(x_loaded[t], 16)

            def stream(g, turn=None):
                if turn is not None or g >= RING:
                    sp.wait_ge(lo_ready, plus(g - RING + 1, turn, RING))
                src = ws[g] if turn is None else ws[bass.ds(turn * RING + g, 1), :, :].rearrange("a p n -> p (a n)")
                sp.dma_start(ring[:, g % RING, :], src).then_inc(weights_in[g % RING], 16)

            for g in range(RING):
                stream(g)
            turns = (G_END - RING) // RING
            with sp.Fori(0, turns) as turn:
                for g in range(RING, 2 * RING):
                    stream(g, turn)
            for g in range(RING + turns * RING, G_END):
                stream(g)
            for t in range(TT):
                sp.wait_ge(xs_ready, 2 * len(XS_OF) + t + 1)
                sp.dma_start(out[t * P:(t + 1) * P, :], xs[:, t, :]).then_inc(stored, 16)
            sp.wait_ge(stored, 16 * TT)

        @block.gpsimd
        def _(pool):
            gp = nc.gpsimd
            gp.memset(power[:, :], -0.5).then_inc(pow_ready, 1)
            pool.wait_ge(pow_ready, 1)

            def norm_power(n):
                for t in range(TT):
                    pool.wait_ge(ms_ready, 2 * n + t + 1)
                    gp.tensor_tensor(rstd[:, t:t + 1], msq[:, t:t + 1], power[:, 0:1], ALU.pow).then_inc(rstd_ready, 1)

            norm_power(0)

            def below(v):
                for d in (v[:, :, 0:P], v[:, :, T:384]):
                    r = gp.affine_select(out=d, in_=d, compare_op=ALU.is_gt, fill=0.0, base=0,
                                         pattern=[[0, 2], [1, P]], channel_multiplier=-1)
                return r

            def sp_mask(p):
                pool.wait_ge(sb_softplus, p + 1)
                below(sb_s[:, p % 2]).then_inc(sb_masked, 1)

            sp_mask(0)
            sp_mask(1)
            for p in range(8):
                pool.wait_ge(sb_weights, p + 1)
                below(sb_a[:, p % 2]).then_inc(sb_wmasked, 1)
                if p + 2 < 8:
                    sp_mask(p + 2)
            norm_power(1)
            norm_power(2)
            for u in range(8):
                dst = rt_q if u < 4 else rt_k
                v = dst[:, 2 * (u % 4):2 * (u % 4) + 2, :]
                a, b = rt_c[:, u % 2, :], rt_n[:, u % 2, :]
                pool.wait_ge(ret_freed, u + 1)
                gp.tensor_tensor(v[:, 0, :], a[:, 0:T], b[:, T:2 * T], ALU.subtract)
                gp.tensor_tensor(v[:, 1, :], b[:, 0:T], a[:, T:2 * T], ALU.add).then_inc(ret_qk, 1)
            for hd in range(RET_HEADS):
                pool.wait_ge(ret_var, hd + 1)
                gp.tensor_tensor(rs8[:, 2 * hd:2 * hd + 2], ms8[:, 2 * hd:2 * hd + 2], power[:, 0:2], ALU.pow)\
                  .then_inc(ret_rstd, 1)
            norm_power(3)
            norm_power(4)
            norm_power(5)
            pool.wait_ge(gla_softplus, 1)
            for t in range(TT):
                r = gp.memset(gl_a[t][:, :, :], 0.0)
            r.then_inc(gla_tree_zero, 1)
            for j in range(8):
                n = 2 << j
                pool.wait_ge(gla_decay, j + 1)
                w, k = gl_level(gl_w[j], j)[:, :, 0:n // 2], gl_level(gl_k, j)[:, :, 0:n // 2]
                gp.tensor_tensor(w, w, k, ALU.mult).then_inc(gla_w_keys, 1)
            pool.wait_ge(row_in, 32)
            for t in range(TT):
                pool.wait_ge(gla_silu, t + 1)
                gp.tensor_tensor(gl_r[:, t, :], gl_r[:, t, :], rowg[:, :], ALU.mult).then_inc(gla_gate, 1)
            for t in range(TT):
                pool.wait_ge(gla_meansq, t + 1)
                gp.tensor_tensor(rs8[:, 4 * t:4 * t + 4], ms8[:, 4 * t:4 * t + 4], power[:, 0:4], ALU.pow)\
                  .then_inc(gla_rstd, 1)
            norm_power(6)

            def ffn(n):
                freed, ready, base, tap, sl, pr, hh = ffn_s[n]
                st = ffn_h[n]

                def up(c, turn):
                    for u in (2 * c, 2 * c + 1):
                        pool.wait_ge(sl, plus(u + 1, turn, 6))
                        gp.tensor_tensor(prod[:, u % 2, :], silu[:, u % 2, :], conv[:, u % 2, 1, :], ALU.mult)\
                          .then_inc(pr, 1)
                        pool.wait_ge(hh, plus(u + 1, turn, 6))
                        i = 4 * (c % 3) + u % 2
                        gp.tensor_tensor(y_lo[:, i, :], prod[:, u % 2, :], y_hi[:, i, :].bitcast(F32), ALU.subtract)\
                          .then_inc(ready, 1)

                st.run(pool, up, lambda c, turn: None)

            ffn(0)
            norm_power(7)
            pool.wait_ge(tab_in, 80)
            pool.wait_ge(xT_lo, 4 * XT_OF["7b"] + 4)
            for d in range(2):
                gp.memset(ns_kd[d][64 - 64 * d:128 - 64 * d, :, :, :], 0.0).then_inc(nsa_kd_zero, 1)
            pool.wait_ge(nsa_kd_zero, 2)
            pool.wait_ge(nsa_blocks, 2)
            rcos = tab[:, C_RCOS:C_RCOS + T].unsqueeze(1).broadcast_to([P, 2, T])
            for i in range(6):
                pool.wait_ge(nsa_freed, 4 if i < 2 else 6 + i)
                dst, raw = (ns_t1[:, i, :, :], ns_k[:, i, :, :]) if i < 2 else \
                    (ns_qr[:, 2 * (i - 2):2 * (i - 2) + 2, :], ns_q[:, 2 * (i - 2):2 * (i - 2) + 2, :])
                gp.tensor_tensor(dst, raw, rcos, ALU.mult).then_inc(nsa_cos_product, 1)
            for it in range(16):
                pool.wait_ge(nsa_coef, it + 1)
                for t in range(2):
                    v = ns_s[:, it % 3, :, P * t:P * t + P * (t + 1)]
                    f = ns_f[:, it % 2, :, t:t + 1].broadcast_to([P, 2, P * (t + 1)])
                    r = gp.tensor_tensor(v, v, f, ALU.mult)
                r.then_inc(nsa_p, 1)
            norm_power(8)
            ffn(1)
            norm_power(9)

        @block.tensor
        def _(pe):
            mm = nc.tensor.matmul

            def keep_clock(count, b=7):
                for _ in range(count):
                    mm(ps[:, b, :], ident, sm[:, 0:512], start=True, stop=True, skip_group_check=True)

            def norm(n):
                if n in WARM:
                    keep_clock(WARM[n])
                for t in range(TT):
                    if n in XS_OF:
                        pe.wait_ge(xs_ready, 2 * XS_OF[n] + t + 1)
                    for k in range(KT):
                        r = nc.tensor.transpose(ps[:, 4 + k // 2, (k % 2) * T + t * P:(k % 2) * T + (t + 1) * P],
                                                xs[:, t, k * P:(k + 1) * P], ident)
                        if t == 1 and k % 2 == 1:
                            r.then_inc(xt_done, 1)

            def x_tiles(n, k):
                if k % 2 == 0:
                    pe.wait_ge(xT_lo, 4 * XT_OF[n] + k // 2 + 1)

            def split(g, turn=None, each=0):
                pe.wait_ge(lo_ready, plus(g + 1, turn, each))

            def mm3(o, lh, ll, rh, rl, start, stop):
                mm(o, lh, rh, start=start, stop=False, skip_group_check=True)
                mm(o, lh, rl, start=False, stop=False, skip_group_check=True)
                return mm(o, ll, rh, start=False, stop=stop, skip_group_check=True)

            def transposed(g, u, freed, first=None, turn=None, each=0, units=0):
                split(g, turn, each)
                if u >= 3:
                    pe.wait_ge(freed, plus(u - 2, turn, units))
                s = g % RING
                for j in range(2):
                    for k in range(KT):
                        if first is not None and j == 0:
                            x_tiles(first, k)
                        c = k * 256 + j * P
                        r = mm3(ps[:, bank(u), j * T:(j + 1) * T], w_hi[:, s, c:c + P], w_lo[:, s, c:c + P],
                                x_hi[:, k, :], x_lo[:, k, :], k == 0, k == KT - 1)
                r.then_inc(done, 1)

            def natural(g, u, freed):
                for e in range(2):
                    split(g + e)
                    s = (g + e) % RING
                    for t in range(TT):
                        if e == 0 and u + t >= 3:
                            pe.wait_ge(freed, u + t - 2)
                        for k in range(4):
                            x = 4 * e + k
                            r = mm3(ps[:, bank(u + t), :], x_hi[:, x, t * P:(t + 1) * P], x_lo[:, x, t * P:(t + 1) * P],
                                    w_hi[:, s, k * 512:(k + 1) * 512], w_lo[:, s, k * 512:(k + 1) * 512],
                                    x == 0, x == KT - 1)
                    r.then_inc(done, 1)

            def accumulate(g, tiles, first, last, turn=None, each=0):
                split(g, turn, each)
                s = g % RING
                order = [(k, j) for k in range(2) for j in range(4)]
                for k, j in sorted(order, key=lambda kj: kj[1]) if last else order:
                    t, c = j // 2, k * D + (j % 2) * 512
                    r = mm3(ps[:, j, :], y_hi[:, tiles[k], t * P:(t + 1) * P], y_lo[:, tiles[k], t * P:(t + 1) * P],
                            w_hi[:, s, c:c + 512], w_lo[:, s, c:c + 512], first and k == 0, last and k == 1)
                    if last and (k, j) == (1, 1):
                        r.then_inc(half_done, 1)
                r.then_inc(done, 1)

            def hidden(n, st, freed, ready):
                def up(c, turn):
                    for i in range(2):
                        transposed(st.up(c) + i, 2 * c + i, freed, first=n if c + i == 0 else None,
                                   turn=turn, each=st.each, units=6)

                def down(c, turn):
                    pe.wait_ge(ready, plus(2 * c + 2, turn, 6))
                    for i in range(st.dn):
                        accumulate(st.down(c) + i, (4 * (c % 3) + 2 * i, 4 * (c % 3) + 2 * i + 1), c == 0 and i == 0,
                                   c == st.chunks - 1 and i == st.dn - 1, turn, st.each)

                st.run(pe, up, down)

            def transpose_pair(b, src, g):
                for k in range(2):
                    for t in range(TT):
                        r = nc.tensor.transpose(ps[:, b, k * T + t * P:k * T + (t + 1) * P],
                                                src[:, t, (2 * g + k) * P:(2 * g + k + 1) * P], ident)
                return r

            pe.wait_ge(loaded, 16)
            norm(0)
            for u in range(8):
                transposed(G_SB + u, u, sb_freed, first=0 if u == 0 else None)
            for c in range(2):
                natural(G_SB + 8 + 2 * c, 8 + 2 * c, sb_freed)
            ntri, none = tab[:, C_NTRI:C_NTRI + P], tab[:, C_NONE:C_NONE + P]

            def sb_z_(p):
                if p == 0:
                    pe.wait_ge(tab_in, 16)
                    pe.wait_ge(sb_freed, 12)
                if p >= 3:
                    pe.wait_ge(sb_weights, p - 2)
                for i in range(2):
                    b, o = 2 + 2 * (p % 3) + i, 64 * i
                    mm(ps[:, b, 0:T], sb_k[o:o + 64, p, 0:P], sb_q[o:o + 64, p, :], start=True, stop=True,
                       skip_group_check=True)
                    r = mm(ps[:, b, T:384], sb_k[o:o + 64, p, P:T], sb_q[o:o + 64, p, P:T], start=False, stop=True,
                           skip_group_check=True)
                r.then_inc(sb_z, 1)

            def sb_sum(p):
                pe.wait_ge(sb_masked, p + 1)
                for i in range(2):
                    b, s = 2 + 2 * (p % 3) + i, sb_s[:, p % 2, i, :]
                    mm(ps[:, b, 0:T], ntri, s[:, 0:T], start=False, stop=True, skip_group_check=True)
                    mm(ps[:, b, P:T], none, s[:, T:384], start=False, stop=True, skip_group_check=True)
                    r = mm(ps[:, b, T:384], ntri, s[:, T:384], start=False, stop=True, skip_group_check=True)
                r.then_inc(sb_summed, 1)

            def sb_av(p):
                pe.wait_ge(sb_wmasked, p + 1)
                if p >= 2:
                    pe.wait_ge(sb_out_copied, p - 1)
                for i in range(2):
                    c, a = (2 * p + i) * 64, sb_a[:, p % 2, i, :]
                    o = ps[64 * i:64 * i + 64, p % 2, :]
                    mm(o[:, 0:T], sb_v[:, 0, c:c + 64], a[:, 0:T], start=True, stop=False, skip_group_check=True)
                    r = mm(o[:, P:T], sb_v[:, 1, c:c + 64], a[:, T:384], start=False, stop=True, skip_group_check=True)
                r.then_inc(sb_out, 1)

            for p in range(3):
                sb_z_(p)
            keep_clock(5, 0)
            for p in range(8):
                sb_sum(p)
                if p:
                    sb_av(p - 1)
                if p + 3 < 8:
                    sb_z_(p + 3)
            sb_av(7)
            for i in range(4):
                pe.wait_ge(sb_out_copied, 2 * i + 2 if i else 8)
                accumulate(G_SB + 12 + i, (2 * i, 2 * i + 1), i == 0, i == 3)
            norm(1)
            hidden(1, mlp_h[0], mlp_s[0][0], mlp_s[0][1])

            norm(2)
            for u in range(8):
                transposed(G_RET + u, u, ret_freed, first=2 if u == 0 else None)

            def ret_score():
                for hd in range(RET_HEADS):
                    for k in range(2):
                        mm(ps[:, hd, 0:T], rt_k[:, 2 * hd + k, 0:P], rt_q[:, 2 * hd + k, :], start=k == 0, stop=k == 1)
                    for k in range(2):
                        r = mm(ps[:, hd, T:384], rt_k[:, 2 * hd + k, P:T], rt_q[:, 2 * hd + k, P:T],
                               start=k == 0, stop=k == 1)
                    r.then_inc(ret_scores, 1)

            def ret_out(hd):
                for t in range(TT):
                    i = 2 * hd + t
                    if i >= 4:
                        pe.wait_ge(ret_o_free, i - 3)
                    r = mm(ps[:, i % 4, :], rt_s[:, hd, t * P:(t + 1) * P], rt_v[:, 0, hd * 512:(hd + 1) * 512],
                           start=True, stop=t == 0)
                    if t == 1:
                        r = mm(ps[:, i % 4, :], rt_s[:, hd, T:384], rt_v[:, 1, hd * 512:(hd + 1) * 512],
                               start=False, stop=True)
                    r.then_inc(ret_o, 1)

            for c in range(8):
                natural(G_RET + 8 + 2 * c, 8 + 2 * c, ret_freed)
                if c == 3:
                    pe.wait_ge(ret_qk, 8)
                    ret_score()
                if c == 5:
                    pe.wait_ge(ret_decayed, 4)
                    pe.wait_ge(ret_freed, 16)
                if c >= 5:
                    ret_out(c - 5)
            ret_out(3)
            pe.wait_ge(ret_freed, 24)
            keep_clock(3)
            for g in range(10):
                if g < 8:
                    pe.wait_ge(ret_y, 2 * (g // 2) + 2)
                    if g >= 4:
                        pe.wait_ge(ret_yT_lo, g - 3)
                    transpose_pair(4 + g % 4, rt_g, g).then_inc(ret_transposed, 1)
                if g >= 2:
                    i = g - 2
                    if i == 0:
                        pe.wait_ge(ret_o_free, 8)
                    pe.wait_ge(ret_yT_lo, i + 1)
                    accumulate(G_RET + 24 + i, (2 * i % 12, 2 * i % 12 + 1), i == 0, i == 7)
            norm(3)
            hidden(3, mlp_h[1], mlp_s[1][0], mlp_s[1][1])

            norm(5)
            pe.wait_ge(n_ready, 2)
            for k in range(KT):
                x_tiles(5, k)
                r = mm3(ps[:, 4, 0:T], n_hi[:, 16 * k:16 * k + P], n_lo[:, 16 * k:16 * k + P],
                        x_hi[:, k, :], x_lo[:, k, :], k == 0, k == KT - 1)
            r.then_inc(gla_small_proj, 1)
            for u in range(1, 5):
                transposed(G_GLA + u - 1, u, gla_freed)
            for i in range(2):
                pe.wait_ge(gla_freed, 5 + i - 2)
                for j in range(2):
                    c = S_ALPHA + (2 * i + j) * P
                    r = mm(ps[:, bank(5 + i), j * T:(j + 1) * T], sm[0:16, c:c + P], gl_low, start=True, stop=True)
                r.then_inc(gla_small_proj, 1)
            for c in range(4):
                natural(G_GLA + 4 + 2 * c, 7 + 2 * c, gla_freed)
            for i in range(16):
                l, t = i // 2, i % 2
                if l >= 1:
                    pe.wait_ge(gla_w, l)
                    pe.wait_ge(gla_w_keys, l)
                if i >= 4:
                    pe.wait_ge(gla_level_copied, i - 3)
                for hd in range(GLA_HEADS):
                    kk = gl_k if l == 0 else gl_w[l - 1]
                    qq = gl_q if l == 0 else gl_w[l - 1]
                    r = mm(ps[:, i % 4, hd * P:(hd + 1) * P], kk[:, hd, t * P:(t + 1) * P], qq[:, hd, t * P:(t + 1) * P],
                           start=True, stop=True)
                r.then_inc(gla_level, 1)
            pe.wait_ge(gla_w, 8)
            pe.wait_ge(gla_w_keys, 8)
            pe.wait_ge(gla_level_copied, 13)
            for hd in range(GLA_HEADS):
                r = mm(ps[:, 0, hd * P:(hd + 1) * P], gl_w[7][:, hd, 0:P], gl_w[7][:, hd, P:T], start=True, stop=True)
            r.then_inc(gla_level, 1)
            pe.wait_ge(gla_freed, 15)
            pe.wait_ge(gla_level_copied, 17)
            for t in range(TT):
                for hd in range(GLA_HEADS):
                    o = ps[:, 4 + 2 * t + hd // 2, (hd % 2) * T:(hd % 2 + 1) * T]
                    v = gl_v[:, :, hd * 256:(hd + 1) * 256]
                    if t == 1:
                        mm(o, gl_across[:, hd, :], v[:, 0, :], start=True, stop=False)
                    r = mm(o, gl_a[t][:, hd, :], v[:, t, :], start=t == 0, stop=True)
                r.then_inc(gla_o, 1)
            keep_clock(3, 3)
            for t in range(TT):
                pe.wait_ge(gla_y, t + 1)
                for k in range(KT):
                    r = nc.tensor.transpose(ps[:, k // 2, (k % 2) * T + t * P:(k % 2) * T + (t + 1) * P],
                                            gl_r[:, t, k * P:(k + 1) * P], ident)
                    if t == 1 and k % 2 == 1:
                        r.then_inc(gla_transposed, 1)
            pe.wait_ge(gla_yT_lo, 4)
            for i in range(4):
                accumulate(G_GLA + 12 + i, (2 * i, 2 * i + 1), i == 0, i == 3)
            norm(6)
            hidden(6, ffn_h[0], ffn_s[0][0], ffn_s[0][1])

            norm(7)
            for u in range(4):
                transposed(G_NSA + u, u, nsa_freed, first=7 if u == 0 else None)
            natural(G_NSA + 4, 4, nsa_freed)
            pe.wait_ge(nsa_freed, 6)
            norm("7b")
            for k in range(KT):
                x_tiles("7b", k)
                c = N_LOW + 48 * k
                r = mm3(ps[:, bank(6), 0:T], n_hi[:, c:c + P], n_lo[:, c:c + P], x_hi[:, k, :], x_lo[:, k, :],
                        k == 0, k == KT - 1)
            r.then_inc(nsa_small_proj, 1)
            for u in range(7, 11):
                transposed(G_NSA - 1 + u, u, nsa_freed)
                if u == 7:
                    pe.wait_ge(nsa_gates_transposed, 1)
                    for t in range(TT):
                        r = nc.tensor.transpose(ps[:, bank(6), T + t * 64:T + t * 64 + 48],
                                                ns_gt[0:48, t * P:(t + 1) * P], ident[0:48, 0:48])
                    r.then_inc(nsa_small_proj, 1)
            pe.wait_ge(tab_in, 80)
            swap = tab[:, C_SWAP:C_SWAP + P]

            def ns_swap(i):
                pe.wait_ge(nsa_freed, 9 + i)
                src = ns_k[:, i, :, :] if i < 2 else ns_q[:, 2 * (i - 2):2 * (i - 2) + 2, :]
                mm(ps[:, bank(11 + i), :], swap, src, start=True, stop=True).then_inc(nsa_small_proj, 1)

            for i in range(3):
                if i == 2:
                    pe.wait_ge(nsa_freed, 11)
                ns_swap(i)
            pe.wait_ge(nsa_blocks, 2)
            for i in range(2):
                for e in range(2):
                    g = G_NSA + 10 + 2 * i + e
                    split(g)
                    s = g % RING
                    for l in range(8):
                        w, x = l * 256, (16 * i + 8 * e + l) * 60
                        r = mm3(ps[:, 2 + i, 0:256], ns_xhf[:, x:x + P], ns_xlf[:, x:x + P],
                                w_hi[:, s, w:w + 256], w_lo[:, s, w:w + 256], e + l == 0, e * l == 7)
                    r.then_inc(done, 1)
                    if 2 * i + e < 3:
                        ns_swap(3 + 2 * i + e)

            def ns_hidden_t():
                for i in range(2):
                    pe.wait_ge(nsa_inner_hidden, i + 1)
                    for c in range(2):
                        r = nc.tensor.transpose(ps[:, 2 + i, 256 + c * 64:256 + c * 64 + 60],
                                                ns_pre[0:60, i, c * P:(c + 1) * P], ident[0:60, 0:60])
                    r.then_inc(nsa_hidden, 1)

            def ns_cmp_kv():
                pe.wait_ge(nsa_gelu, 3)
                for c in range(2):
                    r = mm(ps[:, 2, 384:448], sm[:, S_W2K + c * P:S_W2K + (c + 1) * P], ns_h[:, 2, c, :],
                           start=c == 0, stop=c == 1)
                r.then_inc(nsa_cmp_kv, 1)
                for g in range(2):
                    for c in range(2):
                        r = mm(ps[:, 3, 384 + g * 64:384 + (g + 1) * 64], ns_hv[:, g, c, :],
                               sm[:, S_W2V + c * 64:S_W2V + (c + 1) * 64], start=c == 0, stop=c == 1)
                r.then_inc(nsa_cmp_kv, 1)

            def ns_cmp_qk():
                pe.wait_ge(nsa_kc, 1)
                pe.wait_ge(nsa_vbd, 2)
                pe.wait_ge(nsa_pT_copied, 3)
                for t in range(TT):
                    for pr in range(NSA_HEADS // 2):
                        c = t * T + pr * 2 * CMP
                        r = mm(ps[:, 7, c:c + 2 * CMP], ns_q[:, pr, t * P:(t + 1) * P], ns_kc[:, pr // 2, :],
                               start=True, stop=True)
                r.then_inc(nsa_cmp_scores, 1)
                pe.wait_ge(nsa_cmp_scores_copied, 1)

            def ns_cmp_t():
                pe.wait_ge(nsa_cmp_p, 1)
                pe.wait_ge(nsa_pT_copied, 9)
                for i in range(4):
                    r = nc.tensor.transpose(ps[:, 7, i * P:(i + 1) * P],
                                            ns_cs[:, i % 2, 8 * (i // 2):8 * (i // 2) + 8, :], ident)
                r.then_inc(nsa_cmp_pT, 1)
                pe.wait_ge(nsa_cmp_pT_copied, 1)

            def ns_cmp_v():
                for pr in range(NSA_HEADS // 2):
                    mm(ps[:, pr // 2, (pr % 2) * T:(pr % 2 + 1) * T], ns_vbd[:, pr // 4, 2 * (pr % 4):2 * (pr % 4) + 2, :],
                       ns_cp[:, 2 * (pr // 4):2 * (pr // 4) + 2, :], start=False, stop=False, skip_group_check=True)

            def ns_qk_(it):
                br, pr = it // 8, it % 8
                if it == 0:
                    pe.wait_ge(nsa_kd, 2)
                    pe.wait_ge(nsa_kd_zero, 2)
                    pe.wait_ge(nsa_roped, 4)
                else:
                    pe.wait_ge(nsa_masked, it)
                for i in range(2):
                    kd, q = ns_kd[i][:, br, pr // 2, :], ns_qr[:, pr, :]
                    mm(ps[:, 4 + i, 0:P], q[:, 0:P], kd[:, 0:P], start=True, stop=True)
                    r = mm(ps[:, 4 + i, P:384], q[:, P:T], kd, start=True, stop=True)
                r.then_inc(nsa_scores, 1)

            def ns_t_(it):
                pe.wait_ge(nsa_p, it + 1)
                for i in range(2):
                    for j in range(3):
                        r = nc.tensor.transpose(ps[:, 6 + i, j * P:(j + 1) * P],
                                                ns_s[:, it % 3, i, j * P:(j + 1) * P], ident)
                r.then_inc(nsa_pT, 1)

            def ns_pv_(it):
                br, pr = it // 8, it % 8
                pe.wait_ge(nsa_pT_copied, it + 1)
                for i in range(2):
                    v = ns_v[:, :, br * 256 + (pr // 2) * 64:br * 256 + (pr // 2) * 64 + 64]
                    p_ = ns_p[:, it % 2, i, :]
                    o = ps[64 * i:64 * i + 64, pr // 2, (pr % 2) * T:(pr % 2 + 1) * T]
                    first = br == 0 and pr % 2 == 0
                    mm(o, v[:, 0, :], p_[:, 0:T], start=first, stop=False, skip_group_check=True)
                    r = mm(o[:, P:T], v[:, 1, :], p_[:, T:384], start=False, stop=br == 1, skip_group_check=True)
                return r

            ns_qk_(0)
            ns_qk_(1)
            ns_hidden_t()
            keep_clock(4)
            for it in range(16):
                if it + 2 < 16:
                    ns_qk_(it + 2)
                if it == 3:
                    ns_cmp_qk()
                if it:
                    ns_pv_(it - 1)
                if it == 9:
                    ns_cmp_t()
                ns_t_(it)
                if it == 1:
                    ns_cmp_kv()
                if it == 9:
                    ns_cmp_v()
            ns_pv_(15).then_inc(nsa_o, 1)
            keep_clock(3)
            pe.wait_ge(nsa_oT_lo, 4)
            for i in range(4):
                accumulate(G_NSA + 14 + i, (2 * i, 2 * i + 1), i == 0, i == 3)
            norm(8)
            hidden(8, ffn_h[1], ffn_s[1][0], ffn_s[1][1])

        @block.scalar
        def _(act):
            A = nc.scalar.activation
            steps = [0]
            act.dma_start(sm[:, :], small).then_inc(loaded, 16)
            def link(ins):
                steps[0] += 1
                ins.then_inc(act_step, 1)
                act.wait_ge(act_step, steps[0])

            def sumsq(n):
                for t in range(TT):
                    if n == 0:
                        act.wait_ge(x_loaded[t], 16)
                    else:
                        act.wait_ge(h_ready, H_AT[n] - (2 if n != 5 else 1) * (1 - t))
                    A(xs[:, t, :], h[:, t, :], ACT.Square, accum_out=ssq[:, t:t + 1]).then_inc(ss_ready, 1)

            def hi(g, turn=None, each=0):
                s = g % RING
                act.wait_ge(weights_in[s], 16 * (g // RING + 1) + (0 if turn is None else turn * (16 * each // RING)))
                A(w_hi[:, s, :], ring[:, s, :], ACT.Copy).then_inc(hi_ready, 1)

            def refill(g, turn=None, each=0):
                if g + RING < G_END:
                    act.wait_ge(done, plus(g + 1, turn, each))
                    hi(g + RING, turn, each)

            def norm_tiles(n):
                i = XT_OF[n]
                for b in range(4):
                    act.wait_ge(xt_done, 4 * i + b + 1)
                    for k in (2 * b, 2 * b + 1):
                        c = S_GAIN + GAIN_OF[n] * KT + k
                        r = A(x_hi[:, k, :], ps[:, 4 + b, (k % 2) * T:(k % 2 + 1) * T], ACT.Copy, scale=sm[:, c:c + 1])
                    r.then_inc(xT_hi, 1)

            def norm(n, g):
                sumsq(n)
                refill(g)
                norm_tiles(n)

            def evac(u, g, dst, freed, func=ACT.Copy, scale=1.0, after=None):
                if after is not None:
                    act.wait_ge(freed, after)
                act.wait_ge(done, g + 1)
                A(dst, ps[:, bank(u), :], func, scale=scale).then_inc(freed, 1)

            def mlp(n):
                freed, ready, hh, sq = mlp_s[n]
                st = mlp_h[n]

                def up(c, turn):
                    for u in (2 * c, 2 * c + 1):
                        g = st.up(c) + u % 2
                        act.wait_ge(done, plus(g + 1, turn, st.each))
                        if u >= 2:
                            act.wait_ge(ready, plus(u - 1, turn, 6))
                        A(relu[:, u % 2, :], ps[:, bank(u), :], ACT.Relu).then_inc(freed, 1)
                        act.wait_ge(freed, plus(u + 1, turn, 6))
                        i = 4 * (c % 3) + 2 * (u % 2)
                        A(y_hi[:, i:i + 2, :], relu[:, u % 2, :].rearrange("p (a t) -> p a t", t=T), ACT.Square)\
                            .then_inc(hh, 1)
                        refill(g, turn, st.each)

                def down(c, turn):
                    for i in range(st.dn - (c == st.chunks - 1)):
                        refill(st.down(c) + i, turn, st.each)

                st.run(act, up, down)

            def ffn(n):
                freed, ready, base, tap, sl, pr, hh = ffn_s[n]
                st = ffn_h[n]
                col = S_CONV + n * FFN_TILES * 8

                def par(u, j, turn):
                    c = col + 8 * u + j
                    return sm[:, c:c + 1] if turn is None else sm[:, bass.ds(turn * 48 + c, 1)]

                def up(c, turn):
                    for u in (2 * c, 2 * c + 1):
                        g = st.up(c) + u % 2
                        act.wait_ge(done, plus(g + 1, turn, st.each))
                        if u >= 2:
                            act.wait_ge(ready, plus(u - 1, turn, 6))
                        for e in range(2):
                            r = A(conv[:, u % 2, e, :], ps[:, bank(u), e * T:(e + 1) * T], ACT.Identity,
                                  scale=par(u, 4 + e, turn), bias=par(u, 6 + e, turn))
                        r.then_inc(base, 1)
                        refill(g, turn, st.each)
                        act.wait_ge(freed, plus(u + 1, turn, 6))
                        A(silu[:, u % 2, :], conv[:, u % 2, 0, :], ACT.Silu).then_inc(sl, 1)
                        act.wait_ge(pr, plus(u + 1, turn, 6))
                        A(y_hi[:, 4 * (c % 3) + u % 2, :], prod[:, u % 2, :], ACT.Copy).then_inc(hh, 1)

                def down(c, turn):
                    for i in range(st.dn - (c == st.chunks - 1)):
                        refill(st.down(c) + i, turn, st.each)

                st.run(act, up, down)

            sumsq(0)
            hi(0)
            act.dma_start(narrow_raw, narrow).then_inc(narrow_in, 16)
            act.dma_start(tab[:, :], tables[0]).then_inc(tab_in, 16)
            act.dma_start(rowg[:, :], rows[0:1, :].partition_broadcast(P)).then_inc(row_in, 16)
            act.wait_ge(loaded, 16)
            norm_tiles(0)
            for g in range(1, RING):
                hi(g)
            act.wait_ge(narrow_in, 16)
            A(n_hi[:, :], narrow_raw, ACT.Copy).then_inc(n_ready, 1)
            for u in range(8):
                if u == 4:
                    act.wait_ge(n_ready, 2)
                evac(u, G_SB + u, (sb_q if u < 4 else sb_k)[:, 2 * (u % 4):2 * (u % 4) + 2, :], sb_freed,
                     scale=0.125 if u < 4 else 1.0)
                refill(G_SB + u)
            for c in range(2):
                refill(G_SB + 8 + 2 * c)
                for t in range(TT):
                    evac(8 + 2 * c + t, G_SB + 9 + 2 * c, sb_v[:, t, c * 512:(c + 1) * 512], sb_freed)
                refill(G_SB + 9 + 2 * c)

            def sb_soft(p):
                e = sb_e[:, p % 3, :, :]
                act.wait_ge(sb_clipped, p + 1)
                A(e, e, ACT.Exp).then_inc(sb_exp, 1)
                act.wait_ge(sb_exp, p + 1)
                A(e, e, ACT.Ln, bias=1.0).then_inc(sb_log, 1)

            def sb_hi(p):
                act.wait_ge(sb_out, p + 1)
                A(y_hi[:, p, :], ps[:, p % 2, 0:T], ACT.Copy).then_inc(sb_out_hi, 1)

            sb_soft(0)
            sb_soft(1)
            for p in range(8):
                act.wait_ge(sb_summed, p + 1)
                b = 2 + 2 * (p % 3)
                A(sb_a[:, p % 2, :, :], ps[:, b:b + 2, 0:384], ACT.Exp).then_inc(sb_weights, 1)
                if p:
                    sb_hi(p - 1)
                if p + 2 < 8:
                    sb_soft(p + 2)
            sb_hi(7)
            for i in range(3):
                refill(G_SB + 12 + i)
            sumsq(1)
            refill(G_SB + 15)
            act.dma_start(tab[:, :], tables[1]).then_inc(tab_in, 16)
            act.dma_start(rt_decay, decay).then_inc(tab_in, 16)
            norm_tiles(1)
            mlp(0)
            norm(2, G_MLP[0] + 31)
            for u in range(8):
                refill(G_RET + u)

            def ret_scale(hd):
                act.wait_ge(ret_rstd, hd + 1)
                for t in range(TT):
                    v = rt_g[:, t, hd * 512:(hd + 1) * 512]
                    A(v, v, ACT.Copy, scale=rs8[:, 2 * hd + t:2 * hd + t + 1]).then_inc(ret_y, 1)

            for c in range(8):
                refill(G_RET + 8 + 2 * c)
                for t in range(TT):
                    evac(8 + 2 * c + t, G_RET + 9 + 2 * c, (rt_v if c < 4 else rt_g)[:, t, (c % 4) * 512:(c % 4 + 1) * 512],
                         ret_freed, func=ACT.Copy if c < 4 else ACT.Silu, after=8 if c + t == 0 else None)
                refill(G_RET + 9 + 2 * c)
                if c >= 6:
                    ret_scale(c - 6)
            ret_scale(2)
            ret_scale(3)
            for g in range(10):
                if g < 8:
                    act.wait_ge(ret_transposed, g + 1)
                    if g >= 6:
                        act.wait_ge(done, G_RET + 24 + g - 6 + 1)
                    i = 2 * g % 12
                    A(y_hi[:, i:i + 2, :], ps[:, 4 + g % 4, :].rearrange("p (a t) -> p a t", t=T), ACT.Copy)\
                        .then_inc(ret_yT_hi, 1)
                if 2 <= g < 9:
                    refill(G_RET + 24 + g - 2)
            sumsq(3)
            refill(G_RET + 31)
            act.dma_start(tab[:, :], tables[2]).then_inc(tab_in, 16)
            norm_tiles(3)
            mlp(1)
            sumsq(4)
            refill(G_MLP[1] + 31)
            sumsq(5)
            act.dma_start(rowg[:, :], rows[1:2, :].partition_broadcast(P)).then_inc(row_in, 16)
            norm_tiles(5)
            for u in range(1, 5):
                dst = (gl_q if u < 3 else gl_k)[:, 2 * ((u - 1) % 2):2 * ((u - 1) % 2) + 2, :]
                evac(u, G_GLA + u - 1, dst, gla_freed, scale=P ** -0.5 if u < 3 else 1.0, after=1 if u == 1 else None)
                refill(G_GLA + u - 1)
            act.wait_ge(gla_logit, 1)
            A(gl_l[:, :, :], gl_l[:, :, :], ACT.Exp).then_inc(gla_exp, 1)
            act.wait_ge(gla_exp, 1)
            A(gl_l[:, :, :], gl_l[:, :, :], ACT.Ln, bias=1.0).then_inc(gla_log, 1)
            refill(G_GLA + 4)
            for j in range(8):
                if j % 2 == 0:
                    c = (j // 2) % 2 * 512
                    for t in range(TT):
                        evac(7 + j + t, G_GLA + 5 + j, (gl_v if j < 4 else gl_r)[:, t, c:c + 512], gla_freed,
                             after=7 if j + t == 0 else None)
                w = gl_w[j][:, :, :]
                act.wait_ge(gla_diff, j + 1)
                link(A(w, w, ACT.Abs))
                A(w, w, ACT.Exp, scale=-1.0 / 16.0).then_inc(gla_decay, 1)
                if j < 4:
                    refill(G_GLA + 5 + j)
            for t in range(TT):
                act.wait_ge(gla_freed, 15)
                A(gl_r[:, t, :], gl_r[:, t, :], ACT.Silu).then_inc(gla_silu, 1)
            refill(G_GLA + 9)
            refill(G_GLA + 10)
            for t in range(TT):
                act.wait_ge(gla_o, t + 1)
                junk = (gl_c, gl_w[0])[t]
                for hd in range(GLA_HEADS):
                    r = A(junk[:, hd, :], ps[:, 4 + 2 * t + hd // 2, (hd % 2) * T:(hd % 2 + 1) * T], ACT.Square,
                          accum_out=ss8[:, 4 * t + hd:4 * t + hd + 1])
                r.then_inc(gla_sumsq, 1)
            for g in range(4):
                act.wait_ge(gla_transposed, g + 1)
                A(y_hi[:, 2 * g:2 * g + 2, :], ps[:, g, :].rearrange("p (a t) -> p a t", t=T), ACT.Copy).then_inc(gla_yT_hi, 1)
            for i in range(4):
                refill(G_GLA + 11 + i)
            sumsq(6)
            refill(G_GLA + 15)
            act.dma_start(tab[:, :], tables[3]).then_inc(tab_in, 16)
            act.dma_start(rowg[:, :], rows[2:3, :].partition_broadcast(P)).then_inc(row_in, 16)
            norm_tiles(6)
            ffn(0)
            norm(7, G_FFN[0] + 32)
            for u in range(2):
                act.wait_ge(done, G_NSA + u + 1)
                for o in range(2):
                    src = ps[64 * o:64 * o + 64, bank(u), :].rearrange("p (a t) -> p a t", t=T)
                    A(ns_raw[0:64, u, o:o + 3:2, :], src, ACT.Copy)
                    r = A(ns_raw[64:128, u, o:o + 3:2, 0:T - 1], src[:, :, 1:T], ACT.Copy)
                r.then_inc(nsa_freed, 1)
                refill(G_NSA + u)
            for u in range(2, 4):
                evac(u, G_NSA + u, ns_k[:, u - 2, :, :], nsa_freed)
                refill(G_NSA + u)
            refill(G_NSA + 4)
            for t in range(TT):
                evac(4 + t, G_NSA + 5, ns_v[:, t, :], nsa_freed)
            norm_tiles("7b")
            refill(G_NSA + 5)
            act.wait_ge(nsa_small_proj, 1)
            A(ns_gt[0:48, :], ps[0:48, bank(6), 0:T], ACT.Sigmoid).then_inc(nsa_gates_transposed, 1)
            act.wait_ge(nsa_small_proj, 2)
            A(ns_gate[:, :, :], ps[:, bank(6), T:T + 128].rearrange("p (t n) -> p t n", n=64)[:, :, 0:48],
              ACT.Copy).then_inc(nsa_freed, 1)
            for u in range(7, 11):
                evac(u, G_NSA - 1 + u, ns_q[:, 2 * (u - 7):2 * (u - 7) + 2, :], nsa_freed, scale=0.125)
                refill(G_NSA - 1 + u)
                if u == 7:
                    for i in range(2):
                        act.wait_ge(nsa_blocks_f32, i + 1)
                        A(ns_xh[:, i, :, :], ns_x[:, i, :, :], ACT.Copy).then_inc(nsa_blocks_hi, 1)
            for i in range(2):
                refill(G_NSA + 10 + 2 * i)
                act.wait_ge(done, G_NSA + 12 + 2 * i)
                A(ns_pre[0:60, i, :], ps[0:60, 2 + i, 0:256], ACT.Copy).then_inc(nsa_inner_hidden, 1)
                if i == 0:
                    refill(G_NSA + 11)

            def ns_gelu_square():
                for i in range(2):
                    act.wait_ge(nsa_hidden, i + 1)
                    x = ps[:, 2 + i, 256:384].rearrange("p (c n) -> p c n", n=64)[:, :, 0:60]
                    A(ns_h[:, i, :, 0:60], x, ACT.Square).then_inc(nsa_square, 1)

            def ns_gelu_tanh():
                for i in range(2):
                    act.wait_ge(nsa_inner, i + 1)
                    A(ns_h[:, i, :, 0:60], ns_h[:, i, :, 0:60], ACT.Tanh, scale=0.7978845608028654).then_inc(nsa_tanh, 1)

            def ns_cmp_keys():
                act.wait_ge(nsa_cmp_kv, 2)
                for o in range(2):
                    r = A(ns_kc[64 * o:64 * o + 64, :, CMP * o:CMP * o + CMP],
                          ps[64 * o:64 * o + 64, 2, 384:448].rearrange("p (a n) -> p a n", n=CMP), ACT.Copy, scale=0.5)
                r.then_inc(nsa_kc, 1)

            def ns_exp(it):
                act.wait_ge(nsa_max, it + 1)
                for i in range(2):
                    for t in range(2):
                        v = ns_s[:, it % 3, i, P * t:P * t + P * (t + 1)]
                        r = A(v, v, ACT.Exp, bias=ns_m[:, it % 2, i, t:t + 1], accum_out=ns_l[:, it % 2, i, t:t + 1])
                r.then_inc(nsa_exp, 1)

            def ns_copy(it):
                act.wait_ge(nsa_pT, it + 1)
                A(ns_p[:, it % 2, :, :], ps[:, 6:8, 0:384], ACT.Copy).then_inc(nsa_pT_copied, 1)

            ns_exp(0)
            ns_gelu_square()
            for it in range(16):
                if it:
                    ns_copy(it - 1)
                if it == 2:
                    ns_cmp_keys()
                if it == 9:
                    act.wait_ge(nsa_cmp_pT, 1)
                    A(ns_cp[:, :, :], ps[:, 7, :], ACT.Copy).then_inc(nsa_cmp_pT_copied, 1)
                if it + 1 < 16:
                    ns_exp(it + 1)
                if it == 0:
                    ns_gelu_tanh()
                if it == 5:
                    act.wait_ge(nsa_cmp_shifted, 1)
                    A(ns_cs[:, :, :, :], ns_cs[:, :, :, :], ACT.Exp).then_inc(nsa_cmp_exp, 1)
                if it == 6:
                    refill(G_NSA + 13)
            ns_copy(15)
            act.wait_ge(nsa_o, 1)
            for g in range(4):
                A(y_hi[:, 2 * g:2 * g + 2, :], ps[:, g, :].rearrange("p (a t) -> p a t", t=T), ACT.Copy)\
                    .then_inc(nsa_oT_hi, 1)
            for i in range(3):
                refill(G_NSA + 14 + i)
            norm(8, G_NSA + 17)
            ffn(1)
            sumsq(9)

        @block.vector
        def _(dve):
            V = nc.vector
            steps, residuals = [0], [0]

            def link(ins):
                steps[0] += 1
                ins.then_inc(dve_step, 1)
                dve.wait_ge(dve_step, steps[0])

            def mean_square(n, t):
                dve.wait_ge(ss_ready, 2 * n + t + 1)
                V.tensor_scalar(msq[:, t:t + 1], ssq[:, t:t + 1], 1.0 / D, EPS, ALU.mult, ALU.add).then_inc(ms_ready, 1)

            def lo(g, turn=None, each=0):
                s = g % RING
                dve.wait_ge(hi_ready, plus(g + 1, turn, each))
                V.tensor_tensor(w_lo[:, s, :], ring[:, s, :], w_hi[:, s, :].bitcast(F32), ALU.subtract).then_inc(lo_ready, 1)

            def refill(g, turn=None, each=0):
                if g + RING < G_END:
                    lo(g + RING, turn, each)

            def norm_tiles(n):
                i = XT_OF[n]
                for b in range(4):
                    dve.wait_ge(xT_hi, 4 * i + b + 1)
                    for k in (2 * b, 2 * b + 1):
                        c = S_GAIN + GAIN_OF[n] * KT + k
                        r = V.scalar_tensor_tensor(x_lo[:, k, :], ps[:, 4 + b, (k % 2) * T:(k % 2 + 1) * T],
                                                   sm[:, c:c + 1], x_hi[:, k, :].bitcast(F32), ALU.mult, ALU.subtract)
                    r.then_inc(xT_lo, 1)

            def scaled(n):
                for t in range(TT):
                    if t:
                        mean_square(n, t)
                    dve.wait_ge(rstd_ready, 2 * n + t + 1)
                    V.tensor_scalar(xs[:, t, :], h[:, t, :], rstd[:, t:t + 1], None, ALU.mult).then_inc(xs_ready, 1)

            def norm(n, *late):
                scaled(n)
                norm_tiles(n)
                for g in late:
                    refill(g)

            def y_pair(i, b, ready):
                V.tensor_tensor(y_lo[:, i:i + 2, :], ps[:, b, :].rearrange("p (a t) -> p a t", t=T),
                                y_hi[:, i:i + 2, :].bitcast(F32), ALU.subtract).then_inc(ready, 1)

            def natural_norm(n, row, dst, ready):
                dve.wait_ge(row_in, 16 * (row + 1))
                for t in range(TT):
                    if t:
                        mean_square(n, t)
                    dve.wait_ge(rstd_ready, 2 * n + t + 1)
                    V.scalar_tensor_tensor(dst[:, t, :], h[:, t, :], rstd[:, t:t + 1], rowg[:, :],
                                           ALU.mult, ALU.mult).then_inc(ready, 1)

            def residual(n, g):
                for j in range(4):
                    if j == 0:
                        residuals[0] += 1
                        dve.wait_ge(half_done, residuals[0])
                    if j == 2:
                        mean_square(n, 0)
                        dve.wait_ge(done, g + 1)
                    v = h[:, j // 2, (j % 2) * 512:(j % 2 + 1) * 512]
                    V.tensor_tensor(v, ps[:, j, :], v, ALU.add).then_inc(h_ready, 1)

            def mlp(n):
                freed, ready, hh, sq = mlp_s[n]
                st = mlp_h[n]

                def up(c, turn):
                    for u in (2 * c, 2 * c + 1):
                        dve.wait_ge(freed, plus(u + 1, turn, 6))
                        v = relu[:, u % 2, :]
                        V.tensor_tensor(square[:, u % 2, :], v, v, ALU.mult).then_inc(sq, 1)
                        dve.wait_ge(sq, plus(u + 1, turn, 6))
                        dve.wait_ge(hh, plus(u + 1, turn, 6))
                        i = 4 * (c % 3) + 2 * (u % 2)
                        V.tensor_tensor(y_lo[:, i:i + 2, :], square[:, u % 2, :].rearrange("p (a t) -> p a t", t=T),
                                        y_hi[:, i:i + 2, :].bitcast(F32), ALU.subtract).then_inc(ready, 1)
                        refill(st.up(c) + u % 2, turn, st.each)

                def down(c, turn):
                    if c < st.chunks - 1:
                        for i in range(st.dn):
                            refill(st.down(c) + i, turn, st.each)

                st.run(dve, up, down)

            def ffn(n):
                freed, ready, base, tap, sl, pr, hh = ffn_s[n]
                st = ffn_h[n]
                col = S_CONV + n * FFN_TILES * 8

                def par(u, j, turn):
                    c = col + 8 * u + j
                    return sm[:, c:c + 1] if turn is None else sm[:, bass.ds(turn * 48 + c, 1)]

                def up(c, turn):
                    for u in (2 * c, 2 * c + 1):
                        dve.wait_ge(base, plus(u + 1, turn, 6))
                        for e in range(2):
                            v = conv[:, u % 2, e, 1:T]
                            V.scalar_tensor_tensor(v, ps[:, bank(u), e * T:(e + 1) * T - 1], par(u, 2 + e, turn), v,
                                                   ALU.mult, ALU.add).then_inc(tap, 1)
                        dve.wait_ge(tap, plus(2 * u + 2, turn, 12))
                        for e in range(2):
                            v = conv[:, u % 2, e, 2:T]
                            r = V.scalar_tensor_tensor(v, ps[:, bank(u), e * T:(e + 1) * T - 2], par(u, e, turn), v,
                                                       ALU.mult, ALU.add)
                        r.then_inc(freed, 1)
                        refill(st.up(c) + u % 2, turn, st.each)

                def down(c, turn):
                    if c < st.chunks - 1:
                        for i in range(st.dn):
                            refill(st.down(c) + i, turn, st.each)

                st.run(dve, up, down)

            mean_square(0, 0)
            scaled(0)
            lo(0)
            dve.wait_ge(loaded, 16)
            norm_tiles(0)
            for g in range(1, RING):
                lo(g)
            dve.wait_ge(n_ready, 1)
            V.tensor_tensor(n_lo[:, :], narrow_raw, n_hi[:, :].bitcast(F32), ALU.subtract).then_inc(n_ready, 1)

            def banks(p):
                b = 2 + 2 * (p % 3)
                return ps[:, b:b + 2, 0:384]

            def clip(p):
                dve.wait_ge(sb_z, p + 1)
                V.tensor_scalar(sb_e[:, p % 3, :, :], banks(p), SOFT_CAP, None, ALU.min).then_inc(sb_clipped, 1)

            def softplus(p):
                dve.wait_ge(sb_log, p + 1)
                V.tensor_tensor(sb_s[:, p % 2, :, :], banks(p), sb_e[:, p % 3, :, :], ALU.max).then_inc(sb_softplus, 1)

            def out_copy(p):
                dve.wait_ge(sb_out_hi, p + 1)
                V.tensor_tensor(y_lo[:, p, :], ps[:, p % 2, 0:T], y_hi[:, p, :].bitcast(F32), ALU.subtract).then_inc(sb_out_copied, 1)

            for g in range(12):
                refill(G_SB + g)
            clip(0)
            clip(1)
            softplus(0)
            clip(2)
            for p in range(8):
                if p + 1 < 8:
                    softplus(p + 1)
                if p:
                    out_copy(p - 1)
                if p + 3 < 8:
                    clip(p + 3)
            out_copy(7)
            for i in range(2):
                refill(G_SB + 12 + i)
            residual(1, G_SB + 15)
            norm(1, G_SB + 14, G_SB + 15)
            mlp(0)
            residual(2, G_MLP[0] + 31)
            norm(2, G_MLP[0] + 30, G_MLP[0] + 31)
            dve.wait_ge(tab_in, 48)
            cos = tab[:, C_COS:C_COS + T].unsqueeze(1).broadcast_to([P, 2, T])
            sin = tab[:, C_SIN:C_SIN + T].unsqueeze(1).broadcast_to([P, 2, T])
            for u in range(8):
                dve.wait_ge(done, G_RET + u + 1)
                if u >= 2:
                    dve.wait_ge(ret_qk, u - 1)
                src = ps[:, bank(u), :].rearrange("p (a t) -> p a t", t=T)
                V.tensor_tensor(rt_c[:, u % 2, :].rearrange("p (a t) -> p a t", t=T), src, cos, ALU.mult)
                V.tensor_tensor(rt_n[:, u % 2, :].rearrange("p (a t) -> p a t", t=T), src, sin, ALU.mult)\
                 .then_inc(ret_freed, 1)
                refill(G_RET + u)

            def ret_norm(hd):
                dve.wait_ge(ret_freed, 18 + 2 * hd)
                for i in (2 * hd, 2 * hd + 1):
                    dve.wait_ge(ret_o, i + 1)
                    link(V.bn_stats(bn[:, i, :], ps[:, i % 4, :]))
                    link(V.bn_aggr(mv[:, i, :], bn[:, i, :]))
                    v = rt_g[:, i % 2, hd * 512:(hd + 1) * 512]
                    V.scalar_tensor_tensor(v, ps[:, i % 4, :], mv[:, i, 0:1], v, ALU.subtract, ALU.mult)\
                     .then_inc(ret_o_free, 1)
                V.tensor_scalar(ms8[:, 2 * hd:2 * hd + 2], mv[:, 2 * hd:2 * hd + 2, 1], EPS, None, ALU.add)\
                 .then_inc(ret_var, 1)

            for c in range(8):
                refill(G_RET + 8 + 2 * c)
                refill(G_RET + 9 + 2 * c)
                if c == 3:
                    for hd in range(RET_HEADS):
                        dve.wait_ge(ret_scores, hd + 1)
                        V.tensor_tensor(rt_s[:, hd, :], ps[:, hd, 0:384], rt_decay[:, 384 * hd:384 * (hd + 1)],
                                        ALU.mult).then_inc(ret_decayed, 1)
                if c >= 5:
                    ret_norm(c - 5)
            ret_norm(3)
            for g in range(10):
                if g < 8:
                    dve.wait_ge(ret_yT_hi, g + 1)
                    y_pair(2 * g % 12, 4 + g % 4, ret_yT_lo)
                if 2 <= g < 8:
                    refill(G_RET + 24 + g - 2)
            residual(3, G_RET + 31)
            norm(3, G_RET + 30, G_RET + 31)
            mlp(1)
            residual(4, G_MLP[1] + 31)
            natural_norm(4, 0, h, h_ready)
            mean_square(5, 0)
            norm(5, G_MLP[1] + 30, G_MLP[1] + 31)
            dve.wait_ge(gla_small_proj, 1)
            V.tensor_copy(gl_low, ps[0:16, 4, 0:T]).then_inc(gla_freed, 1)
            for g in range(4):
                refill(G_GLA + g)
            for i in range(2):
                dve.wait_ge(gla_small_proj, 2 + i)
                if i == 0:
                    dve.wait_ge(gla_freed, 5)
                for j in range(2):
                    c = 2 * i + j
                    r = V.tensor_scalar(gl_x[:, c, :], ps[:, bank(5 + i), j * T:(j + 1) * T],
                                        sm[:, S_BALPHA + c:S_BALPHA + c + 1], -1.0, ALU.add, ALU.mult)
                r.then_inc(gla_freed, 1)
            dve.wait_ge(gla_freed, 7)
            V.tensor_scalar(gl_l[:, :, :], gl_x[:, :, :], SOFT_CAP, None, ALU.min).then_inc(gla_logit, 1)
            dve.wait_ge(gla_log, 1)
            V.tensor_tensor(gl_x[:, :, :], gl_x[:, :, :], gl_l[:, :, :], ALU.max).then_inc(gla_softplus, 1)
            dve.wait_ge(gla_softplus, 1)
            for hd in range(GLA_HEADS):
                r = V.tensor_tensor_scan(gl_c[:, hd, :], gl_x[:, hd, :], gl_x[:, hd, :], 0.0, ALU.add, ALU.max)
            link(r)
            refill(G_GLA + 4)
            flat = gl_c[:, :, :].rearrange("p a t -> p (a t)")

            for j in range(8):
                n = 2 << j
                c = flat.rearrange("p (b n) -> p b n", n=n)
                V.tensor_tensor(gl_level(gl_w[j], j), c, c[:, :, n // 2 - 1:n // 2].broadcast_to([P, 4 * T // n, n]),
                                ALU.subtract).then_inc(gla_diff, 1)
                if j in (2, 5):
                    refill(G_GLA + 4 + (j + 1) // 3)
            for j in range(8):
                n = 2 << j
                dve.wait_ge(gla_decay, j + 1)
                w, q = gl_level(gl_w[j], j)[:, :, n // 2:n], gl_level(gl_q, j)[:, :, n // 2:n]
                V.tensor_tensor(w, w, q, ALU.mult).then_inc(gla_w, 1)
                if j < 2:
                    refill(G_GLA + 7 + j)
            dve.wait_ge(tab_in, 64)
            dve.wait_ge(gla_tree_zero, 1)
            for i in range(16):
                l, t = i // 2, i % 2
                dve.wait_ge(gla_level, i + 1)
                if i >= 2:
                    dve.wait_ge(gla_level_copied, i - 1)
                m = tab[:, C_LEVEL + l * P:C_LEVEL + (l + 1) * P].bitcast(I32).unsqueeze(1).broadcast_to([P, 4, P])
                V.copy_predicated(gl_a[t][:, :, :], m, ps[:, i % 4, :].rearrange("p (a t) -> p a t", t=P))\
                 .then_inc(gla_level_copied, 1)
            dve.wait_ge(gla_level, 17)
            V.tensor_copy(gl_across, ps[:, 0, :].rearrange("p (a t) -> p a t", t=P)).then_inc(gla_level_copied, 1)
            refill(G_GLA + 9)
            refill(G_GLA + 10)
            for t in range(TT):
                dve.wait_ge(gla_sumsq, t + 1)
                V.tensor_scalar(ms8[:, 4 * t:4 * t + 4], ss8[:, 4 * t:4 * t + 4], 1.0 / 256, EPS, ALU.mult, ALU.add)\
                 .then_inc(gla_meansq, 1)
                dve.wait_ge(gla_rstd, t + 1)
                dve.wait_ge(gla_gate, t + 1)
                for hd in range(GLA_HEADS):
                    v = gl_r[:, t, hd * 256:(hd + 1) * 256]
                    r = V.scalar_tensor_tensor(v, ps[:, 4 + 2 * t + hd // 2, (hd % 2) * T:(hd % 2 + 1) * T],
                                               rs8[:, 4 * t + hd:4 * t + hd + 1], v, ALU.mult, ALU.mult)
                r.then_inc(gla_y, 1)
            for g in range(4):
                dve.wait_ge(gla_yT_hi, g + 1)
                y_pair(2 * g, g, gla_yT_lo)
            for i in range(3):
                refill(G_GLA + 11 + i)
            residual(6, G_GLA + 15)
            norm(6, G_GLA + 14, G_GLA + 15)
            ffn(0)
            residual(7, G_FFN[0] + 32)
            norm(7, G_FFN[0] + 32)
            dve.wait_ge(tab_in, 80)
            for g in range(5):
                refill(G_NSA + g)
            norm_tiles("7b")
            refill(G_NSA + 5)
            for i in range(2):
                dve.wait_ge(nsa_freed, i + 1)
                for l in range(16):
                    o = ns_x[:, i, l, :].rearrange("p (a n) -> p a n", n=15)
                    pe_ = sm[:, S_PE + 16 * i + l:S_PE + 16 * i + l + 1]
                    r = V.tensor_scalar(o, ns_raw[:, i, :, 2 * l:2 * l + 16 * 14 + 1:16], pe_, None, ALU.add)
                r.then_inc(nsa_blocks_f32, 1)
            refill(G_NSA + 6)
            for i in range(2):
                dve.wait_ge(nsa_blocks_hi, i + 1)
                V.tensor_tensor(ns_xl[:, i, :, :], ns_x[:, i, :, :], ns_xh[:, i, :, :].bitcast(F32), ALU.subtract)\
                 .then_inc(nsa_blocks, 1)
            for g in range(7, 10):
                refill(G_NSA + g)
            dve.wait_ge(nsa_blocks, 2)
            V.memset(ns_kc[:, :, :], 0.0)
            link(V.memset(ns_h[:, 2:4, :, :], 0.0))
            rsin = tab[:, C_RSIN:C_RSIN + T].unsqueeze(1).broadcast_to([P, 2, T])

            def ns_sin(i):
                dve.wait_ge(nsa_small_proj, 3 + i)
                dve.wait_ge(nsa_freed, 11 + i)
                V.tensor_tensor(ns_t2[:, :, :], ps[:, bank(11 + i), :].rearrange("p (a t) -> p a t", t=T), rsin,
                                ALU.mult).then_inc(nsa_freed, 1)
                dve.wait_ge(nsa_freed, 12 + i)
                dve.wait_ge(nsa_cos_product, i + 1)

            for i in range(2):
                ns_sin(i)
                for o in range(2):
                    for d in range(2):
                        r = V.tensor_tensor(ns_kd[d][64 * d:64 * d + 64, i, o:o + 3:2, :],
                                            ns_t1[64 * o:64 * o + 64, i, :, :], ns_t2[64 * o:64 * o + 64, :, :], ALU.add)
                r.then_inc(nsa_kd, 1)
                dve.wait_ge(nsa_kd, i + 1)
            for i in range(4):
                ns_sin(2 + i)
                v = ns_qr[:, 2 * i:2 * i + 2, :]
                V.tensor_tensor(v, v, ns_t2[:, :, :], ALU.add).then_inc(nsa_roped, 1)
                dve.wait_ge(nsa_roped, i + 1)
                if i == 0:
                    refill(G_NSA + 10)

            def ns_gelu_inner():
                for i in range(2):
                    x = ps[:, 2 + i, 256:384].rearrange("p (c n) -> p c n", n=64)[:, :, 0:60]
                    a = ns_h[:, i, :, 0:60]
                    dve.wait_ge(nsa_square, i + 1)
                    link(V.tensor_scalar(a, a, 0.044715, 1.0, ALU.mult, ALU.add))
                    V.tensor_tensor(a, x, a, ALU.mult).then_inc(nsa_inner, 1)

            def ns_gelu():
                for i in range(2):
                    dve.wait_ge(nsa_tanh, i + 1)
                    o = ns_h[:, 2 + i, :, :].rearrange("p c (a n) -> p c a n", n=CMP)
                    for c in range(2):
                        x = ps[:, 2 + i, 256 + c * 64:256 + c * 64 + 60].rearrange("p (a n) -> p a n", n=15)
                        r = V.scalar_tensor_tensor(o[:, c, :, 0:15],
                                                   ns_h[:, i, c, 0:60].rearrange("p (a n) -> p a n", n=15),
                                                   1.0, x, ALU.add, ALU.mult)
                    r.then_inc(nsa_gelu, 1)
                dve.wait_ge(nsa_gelu, 2)
                for g in range(2):
                    for c in range(2):
                        src = ns_h[:, 3, c, :].rearrange("p (a n) -> p a n", n=CMP)[:, 2 * g:2 * g + 2, :]
                        dst = ns_hv[:, g, c, :].rearrange("p (a b n) -> p a b n", b=4, n=CMP)
                        r = V.tensor_copy(dst, src.unsqueeze(2).broadcast_to([P, 2, 4, CMP]))
                r.then_inc(nsa_gelu, 1)

            def ns_cmp_values():
                dve.wait_ge(nsa_cmp_kv, 2)
                for g in range(2):
                    V.tensor_tensor(ns_vbd[:, g, :, :],
                                    ps[:, 3, 384 + g * 64:384 + (g + 1) * 64].unsqueeze(1).broadcast_to([P, 8, 64]),
                                    tab[:, C_BD:C_BD + 8].unsqueeze(2).broadcast_to([P, 8, 64]), ALU.mult).then_inc(nsa_vbd, 1)

            c3 = ns_cs[:, :, :, :].rearrange("p t h n -> p (t h) n")
            cm = ns_cm[:, :, :].rearrange("p t h -> p (t h)")
            cl = ns_cl[:, :, :].rearrange("p t h -> p (t h)")

            def cmask(c, t):
                return tab[:, c + t * CMP:c + (t + 1) * CMP].unsqueeze(1).broadcast_to([P, 16, CMP])

            def ns_cmp_scores():
                dve.wait_ge(nsa_cmp_scores, 1)
                for t in range(TT):
                    r = V.tensor_tensor(ns_cs[:, t, :, :],
                                        ps[:, 7, t * T:(t + 1) * T].rearrange("p (h n) -> p h n", n=CMP),
                                        cmask(C_CADD, t), ALU.add)
                r.then_inc(nsa_cmp_scores_copied, 1)

            def ns_cmp_shift():
                dve.wait_ge(nsa_cmp_scores_copied, 1)
                link(V.tensor_reduce(cm, c3, AX.X, ALU.max))
                V.tensor_tensor(c3, c3, cm.unsqueeze(2).broadcast_to([P, 32, CMP]), ALU.subtract).then_inc(nsa_cmp_shifted, 1)

            def ns_cmp_p():
                dve.wait_ge(nsa_cmp_exp, 1)
                link(V.tensor_reduce(cl, c3, AX.X, ALU.add))
                link(V.reciprocal(cl, cl))
                link(V.tensor_tensor(ns_cl[:, :, :], ns_cl[:, :, :], ns_gate[:, :, 0:16], ALU.mult))
                for t in range(TT):
                    r = V.tensor_tensor(ns_cs[:, t, :, :], ns_cs[:, t, :, :], cmask(C_CMUL, t), ALU.mult)
                link(r)
                V.tensor_tensor(c3, c3, cl.unsqueeze(2).broadcast_to([P, 32, CMP]), ALU.mult).then_inc(nsa_cmp_p, 1)

            def ns_scores(it):
                dve.wait_ge(nsa_scores, it + 1)
                if it >= 3:
                    dve.wait_ge(nsa_pT, it - 2)
                s = ns_s[:, it % 3, :, :]
                V.tensor_tensor(s, ps[:, 4:6, 0:384],
                                tab[:, C_CAUSAL:C_CAUSAL + 384].unsqueeze(1).broadcast_to([P, 2, 384]), ALU.add)\
                 .then_inc(nsa_masked, 1)
                dve.wait_ge(nsa_masked, it + 1)
                for t in range(2):
                    r = V.tensor_reduce(ns_m[:, it % 2, :, t], s[:, :, P * t:P * t + P * (t + 1)], AX.X, ALU.max,
                                        negate=True)
                r.then_inc(nsa_max, 1)

            def ns_coef(it):
                dve.wait_ge(nsa_exp, it + 1)
                l, f = ns_l[:, it % 2, :, :], ns_f[:, it % 2, :, :]
                link(V.reciprocal(f, l))
                br, pr = it // 8, it % 8
                g = ns_gate[:, :, 16 * (br + 1) + 2 * pr:16 * (br + 1) + 2 * pr + 2].rearrange("p t h -> p h t")
                V.tensor_tensor(f, f, g, ALU.mult).then_inc(nsa_coef, 1)

            ns_scores(0)
            ns_coef(0)
            ns_scores(1)
            ns_gelu_inner()
            for it in range(16):
                if it + 2 < 16:
                    ns_scores(it + 2)
                if it == 3:
                    ns_cmp_scores()
                if it + 1 < 16:
                    ns_coef(it + 1)
                if it == 0:
                    ns_gelu()
                if it == 2:
                    ns_cmp_values()
                if it == 4:
                    ns_cmp_shift()
                if it == 6:
                    ns_cmp_p()
                if it in (7, 9, 11):
                    refill(G_NSA + {7: 11, 9: 12, 11: 13}[it])
            for g in range(4):
                dve.wait_ge(nsa_oT_hi, g + 1)
                y_pair(2 * g, g, nsa_oT_lo)
            for i in range(2):
                refill(G_NSA + 14 + i)
            residual(8, G_NSA + 17)
            norm(8, G_NSA + 16, G_NSA + 17)
            ffn(1)
            residual(9, G_FFN[1] + 32)
            natural_norm(9, 2, xs, xs_ready)


def constants():
    f = np.float32
    c = np.zeros((4, P, TAB), f)
    decay = np.zeros((P, DECAY), f)
    i = np.arange(P)
    c[0, :, C_NTRI:C_NTRI + P] = np.where(i[:, None] >= i[None, :], -1.0, 0.0)
    c[0, :, C_NONE:C_NONE + P] = -1.0
    pos = np.arange(T, dtype=f)
    inv = (f(1.0) / (f(10000.0) ** np.linspace(0.0, 1.0, P, dtype=f))).astype(f)
    ang = (inv[:, None] * pos[None, :]).astype(f)
    c[1, :, C_COS:C_COS + T], c[1, :, C_SIN:C_SIN + T] = np.cos(ang), np.sin(ang)
    lg = np.log1p(-np.exp2(-5.0 - np.arange(RET_HEADS)))
    for hd in range(RET_HEADS):
        for n, (s0, t0, w) in enumerate(((0, 0, T), (P, P, P))):
            rel = (t0 + np.arange(w))[None, :] - (s0 + i)[:, None]
            dec = np.where(rel >= 0, np.exp(lg[hd] * np.maximum(rel, 0)), 0.0) * 256 ** -0.5
            decay[:, 384 * hd + n * T:384 * hd + n * T + w] = dec
    c[2, :, C_LEVEL:C_LEVEL + P] = np.eye(P)
    for l in range(1, 8):
        m = 1 << l
        same = i[:, None] // m == i[None, :] // m
        c[2, :, C_LEVEL + l * P:C_LEVEL + (l + 1) * P] = same & (i[:, None] % m < m // 2) & (i[None, :] % m >= m // 2)
    inv = (f(10000.0) ** (-np.arange(32, dtype=f) / f(32))).astype(f)
    ang = (inv[i % 32][:, None] * pos[None, :]).astype(f)
    c[3, :, C_RCOS:C_RCOS + T] = np.cos(ang)
    c[3, :, C_RSIN:C_RSIN + T] = np.sin(ang) * np.where(i % 64 < 32, -1.0, 1.0)[:, None]
    partner = np.where(i % 64 < 32, i + 32, i - 32)
    c[3, partner, C_SWAP + i] = 1.0
    causal = np.where(i[None, :] <= i[:, None], 0.0, NEG)
    c[3, :, C_CAUSAL:C_CAUSAL + P] = causal
    c[3, :, C_CAUSAL + T:C_CAUSAL + 384] = causal
    n = np.arange(CMP)
    for t in range(TT):
        ok = (n[None, :] * 16 + 31 <= (t * P + i)[:, None]) & (n[None, :] < CMP - 1)
        c[3, :, C_CADD + t * CMP:C_CADD + (t + 1) * CMP] = np.where(ok, 0.0, NEG)
        c[3, :, C_CMUL + t * CMP:C_CMUL + (t + 1) * CMP] = ok
    c[3, :, C_BD:C_BD + 8] = 0.5 * (i[:, None] // CMP == np.arange(8)[None, :])
    return c, decay


def kernel(**inputs):
    import concourse.bacc as bacc
    from concourse.bass_utils import run_bass_kernel_spmd

    a = {k: np.asarray(v) for k, v in inputs.items()}

    ws = []

    def cols(w, c):
        ws.append(w[:, c].reshape(KT, P, 256).transpose(1, 0, 2).reshape(P, PIECE))

    def both(w, c0):
        for r in (0, 512):
            ws.append(w[r:r + 512, c0:c0 + 512].reshape(4, P, 512).transpose(1, 0, 2).reshape(P, PIECE))

    def rows_(w, r):
        ws.append(w[r:r + 256].reshape(2, P, D).transpose(1, 0, 2).reshape(P, PIECE))

    def hidden(up, down, chunks, dn):
        def down_(c):
            for i in range(dn):
                rows_(down, 256 * (dn * c + i))
        for c in range(chunks):
            for ix in up(c):
                cols(*ix)
            if c:
                down_(c - 1)
        down_(chunks - 1)

    def mlp(n):
        w = a["w_mlp_up"][n]
        hidden(lambda c: [(w, slice(512 * c + 256 * i, 512 * c + 256 * (i + 1))) for i in range(2)],
               a["w_mlp_down"][n], MLP_C, 2)

    def ffn(n):
        w, f = a["ffn_w_up_2"][n], FFN_TILES * P
        hidden(lambda c: [(w, np.concatenate([s * f + u * P + np.arange(P) for s in range(2)]))
                          for u in (2 * c, 2 * c + 1)], a["ffn_w_down_2"][n], FFN_C, 1)

    def mixer(w, n_cols, n_both, out):
        for j in range(n_cols):
            cols(w, slice(256 * j, 256 * (j + 1)))
        for j in range(n_both):
            both(w, 256 * n_cols + 512 * j)
        for r in range(0, out.shape[0], 256):
            rows_(out, r)

    mixer(a["w_sb_in"][0], 8, 2, a["w_sb_out"][0])
    mlp(0)
    mixer(a["w_ret_in"][0], 8, 8, a["w_ret_out"][0])
    mlp(1)
    mixer(a["gla_w_in_2"][0], 4, 4, a["gla_w_o_2"][0])
    ffn(0)
    kv, win = a["nsa_w_kv_2"], a["nsa_w_in_2"][0]
    for j in (0, 1, 2, 4):
        cols(kv, slice(256 * j, 256 * (j + 1)))
    both(np.concatenate([kv[:, 256 * 3:256 * 4], kv[:, 256 * 5:256 * 6]], 1), 0)
    for j in range(4):
        cols(win, slice(256 * j, 256 * (j + 1)))
    for w in (a["cmp_k_w1_2"], a["cmp_v_w1_2"]):
        for r in (0, 1024):
            ws.append(w[r:r + 1024].reshape(8, P, 256).transpose(1, 0, 2).reshape(P, PIECE))
    for r in range(0, D, 256):
        rows_(a["nsa_w_o_2"][0], r)
    ffn(1)
    ws = np.stack(ws)
    assert len(ws) == G_END

    small = np.zeros((P, S_TOTAL), np.float32)
    for g, v in enumerate((a["g_mix"][0], a["g_mlp"][0], a["g_mix"][1], a["g_mlp"][1], a["norm_mix_2"][0],
                           a["norm_ffn_2"][0], a["kv_norm_2"], a["norm_mix_2"][1], a["norm_ffn_2"][1])):
        small[:, S_GAIN + g * KT:S_GAIN + (g + 1) * KT] = v.reshape(KT, P).T
    for n in range(2):
        taps = np.concatenate([a["ffn_conv_w_2"][n], a["ffn_conv_b_2"][n][None]], 0)
        v = taps.reshape(4, 2, FFN_TILES, P).transpose(3, 2, 0, 1).reshape(P, FFN_TILES * 8)
        small[:, S_CONV + n * FFN_TILES * 8:S_CONV + (n + 1) * FFN_TILES * 8] = v
    small[:, S_BALPHA:S_BALPHA + 4] = a["gla_b_alpha_2"][0].reshape(4, P).T
    w2 = a["cmp_k_w2_2"].reshape(2, P, 64).transpose(1, 0, 2)
    small[:, S_W2K:S_W2V] = np.concatenate([w2, w2], 2).reshape(P, -1)
    small[:, S_W2V:S_PE] = a["cmp_v_w2_2"].reshape(2, P, 64).transpose(1, 0, 2).reshape(P, -1)
    small[:, S_PE:S_PE + 16] = a["cmp_pe_k_2"].reshape(16, P).T
    small[:, S_PE + 16:S_PE + 32] = a["cmp_pe_v_2"].reshape(16, P).T
    small[0:16, S_ALPHA:S_ALPHA + 512] = a["gla_w_alpha_up_2"][0]
    small[:, S_ID:S_ID + P] = np.eye(P)
    narrow = np.concatenate([a["gla_w_in_2"][0][:, 3072:3088].reshape(KT, P, 16).transpose(1, 0, 2).reshape(P, -1),
                             win[:, D:D + 48].reshape(KT, P, 48).transpose(1, 0, 2).reshape(P, -1),
                             np.zeros((P, N_TOTAL - N_LOW - N_GATE), np.float32)], 1)
    rows = np.stack([a["g_final"], a["gla_norm_2"][0].reshape(D), a["norm_final_2"]])

    tables, decay = constants()
    arrays = {"ws": ws, "small": small, "narrow": narrow, "tables": tables, "decay": decay, "rows": rows,
              "x": np.ascontiguousarray(a["x"][0])}
    nc = bacc.Bacc("TRN2", target_bir_lowering=False, num_devices=1)
    aps = {k: nc.dram_tensor(k, v.shape, mybir.dt.from_np(v.dtype), kind="ExternalInput").ap()
           for k, v in arrays.items()}
    out = nc.dram_tensor("out", (T, D), F32, kind="ExternalOutput").ap()
    build(nc, aps["ws"], aps["small"], aps["narrow"], aps["tables"], aps["decay"], aps["rows"], aps["x"], out)
    r = run_bass_kernel_spmd(nc, [arrays], core_ids=[0])
    return r.results[0]["out"].reshape(1, T, D)
```
